# Optimizing a Trainium2 kernel written in Bass

```python
import math
import jax, jax.numpy as jnp
from jax import lax
import numpy as np
import jax
import jax.numpy as jnp

D_MODEL = 1024
BATCH = 1
SEQ = 512
DEPTH = 1

GRID_W = 64
CTX_LEN = 256
N_DA_HEADS = 4
DA_HEAD_DIM = 64
DA_V_DIM = 2 * DA_HEAD_DIM
QK_WIDTH = N_DA_HEADS * 2 * DA_HEAD_DIM
ATTN_WIDTH = N_DA_HEADS * DA_V_DIM
N_FOURIER_GROUPS = 4
FOURIER_GROUP_DIM = 128
FOURIER_WIDTH = N_FOURIER_GROUPS * FOURIER_GROUP_DIM
MIX_WIDTH = ATTN_WIDTH + FOURIER_WIDTH
IN_PROJ_WIDTH = 2 * QK_WIDTH + ATTN_WIDTH + FOURIER_WIDTH
ROPE_THETA = 10000.0
ROPE_AXIS_DIM = DA_HEAD_DIM // 2
Q_BLOCK = 128
N_GROUPS = 4
EXPERTS_PER_GROUP = 8
N_EXPERTS = N_GROUPS * EXPERTS_PER_GROUP
TOP_K = 2
D_EXPERT = 512
MOE_BLOCK = 128
N_MOD = 6
EPS = 1e-6


def rms_norm(x, g):
    xf = x.astype(jnp.float32)
    y = xf * lax.rsqrt(jnp.mean(xf * xf, axis=-1, keepdims=True) + EPS)
    return (y * g.astype(jnp.float32)).astype(x.dtype)

def modulate(h, shift, scale):
    return h * (1 + scale) + shift

def axial_rope_tables(rows, dtype):
    r, col = jnp.meshgrid(jnp.arange(rows), jnp.arange(GRID_W), indexing='ij')
    pos = jnp.stack([r.reshape(-1), col.reshape(-1)], axis=-1).astype(jnp.float32)
    inv_freq = ROPE_THETA ** (-jnp.arange(0, ROPE_AXIS_DIM, 2, dtype=jnp.float32) / ROPE_AXIS_DIM)
    ang = pos[:, :, None] * inv_freq
    ang = jnp.concatenate([ang, ang], axis=-1)
    return jnp.cos(ang).astype(dtype), jnp.sin(ang).astype(dtype)

def apply_axial_rope(x, cos, sin):
    xr = x.reshape(*x.shape[:-1], 2, ROPE_AXIS_DIM)
    x1, x2 = jnp.split(xr, 2, axis=-1)
    rot = jnp.concatenate([-x2, x1], axis=-1)
    c = cos[None, :, None, None]
    s = sin[None, :, None, None]
    return (xr * c + rot * s).reshape(x.shape)

def diff_lambda(lq1, lk1, lq2, lk2, lambda_init):
    f = lambda a: a.astype(jnp.float32)
    return jnp.exp(jnp.sum(f(lq1) * f(lk1))) - jnp.exp(jnp.sum(f(lq2) * f(lk2))) + lambda_init

def diff_attention(q, k, v, lam, g_subln, lambda_init):
    b, n = q.shape[:2]
    nb = n // Q_BLOCK
    qb = jnp.moveaxis(q.reshape(b, nb, Q_BLOCK, *q.shape[2:]), 1, 0)
    scale = DA_HEAD_DIM ** -0.5

    def block(qi):
        s = jnp.einsum('bqhmd,bkhmd->bhmqk', qi, k, preferred_element_type=jnp.float32) * scale
        p = jax.nn.softmax(s, axis=-1)
        a = p[:, :, 0] - lam * p[:, :, 1]
        return jnp.einsum('bhqk,bkhv->bqhv', a.astype(v.dtype), v)

    o = lax.map(block, qb)
    o = jnp.moveaxis(o, 0, 1).reshape(b, n, N_DA_HEADS, DA_V_DIM)
    o = rms_norm(o, g_subln) * (1.0 - lambda_init)
    return o.reshape(b, n, ATTN_WIDTH)

def fourier_mix(f, w_fourier):
    b, n, _ = f.shape
    fg = f.reshape(b, n, N_FOURIER_GROUPS, FOURIER_GROUP_DIM).astype(jnp.float32)
    fr = jnp.fft.fft2(fg, axes=(1, 3), norm='ortho').real.astype(f.dtype)
    return jnp.einsum('bngc,gcd->bngd', fr, w_fourier).reshape(b, n, FOURIER_WIDTH)

def hier_moe(h, w_rg, b_rg, w_re, b_re, w_gate, w_up, w_down):
    t, d = h.shape
    hf = h.astype(jnp.float32)
    g_logits = hf @ w_rg.astype(jnp.float32) + b_rg.astype(jnp.float32)
    grp = jnp.argmax(g_logits, axis=-1)
    p_grp = jnp.take_along_axis(jax.nn.softmax(g_logits, axis=-1), grp[:, None], axis=-1)
    e_logits = (hf @ w_re.astype(jnp.float32) + b_re.astype(jnp.float32)).reshape(t, N_GROUPS, EXPERTS_PER_GROUP)
    e_in = jnp.take_along_axis(e_logits, grp[:, None, None], axis=1)[:, 0]
    top_val, top_idx = lax.top_k(e_in, TOP_K)
    gate = p_grp * jax.nn.softmax(top_val, axis=-1)
    expert = grp[:, None] * EXPERTS_PER_GROUP + top_idx

    n_assign = t * TOP_K
    e_flat = expert.reshape(n_assign).astype(jnp.int32)
    tok_flat = jnp.repeat(jnp.arange(t, dtype=jnp.int32), TOP_K)
    w_flat = gate.reshape(n_assign)
    order = jnp.argsort(e_flat)
    e_sorted = e_flat[order]
    counts = jnp.bincount(e_flat, length=N_EXPERTS).astype(jnp.int32)
    starts = jnp.cumsum(counts) - counts
    padded = (counts + MOE_BLOCK - 1) // MOE_BLOCK * MOE_BLOCK
    pad_ends = jnp.cumsum(padded)
    pad_starts = pad_ends - padded
    dest = pad_starts[e_sorted] + jnp.arange(n_assign, dtype=jnp.int32) - starts[e_sorted]
    n_blocks = -(-n_assign // MOE_BLOCK) + N_EXPERTS
    buf_tok = jnp.full((n_blocks * MOE_BLOCK,), t, jnp.int32).at[dest].set(tok_flat[order])
    buf_w = jnp.zeros((n_blocks * MOE_BLOCK,), h.dtype).at[dest].set(w_flat[order].astype(h.dtype))
    block_expert = jnp.minimum(
        jnp.searchsorted(pad_ends, jnp.arange(n_blocks, dtype=jnp.int32) * MOE_BLOCK, side='right'),
        N_EXPERTS - 1)
    h_pad = jnp.concatenate([h, jnp.zeros((1, d), h.dtype)], axis=0)

    def expert_block(args):
        tok, wt, e = args
        xb = h_pad[tok]
        y = (jax.nn.silu(xb @ w_gate[e]) * (xb @ w_up[e])) @ w_down[e]
        return y * wt[:, None]

    ys = lax.map(expert_block, (buf_tok.reshape(n_blocks, MOE_BLOCK),
                                buf_w.reshape(n_blocks, MOE_BLOCK), block_expert))
    out = jnp.zeros((t + 1, d), ys.dtype).at[buf_tok].add(ys.reshape(-1, d))
    return out[:t]

def first_inputs(seed: int = 0) -> dict:
    key = jax.random.key(seed)
    ks = jax.random.split(key, 24)
    f32 = jnp.float32
    nrm = lambda k, shape, std: jax.random.normal(k, shape, f32) * std
    L = DEPTH
    return {
        'x': nrm(ks[0], (BATCH, SEQ, D_MODEL), 1.0),
        'c': nrm(ks[1], (BATCH, D_MODEL), 1.0),
        'ctx': nrm(ks[2], (BATCH, CTX_LEN, D_MODEL), 1.0),
        'c_ctx': nrm(ks[3], (D_MODEL,), 1.0),
        'w_ada': nrm(ks[4], (L, D_MODEL, N_MOD * D_MODEL), 0.5 * D_MODEL ** -0.5),
        'b_ada': nrm(ks[5], (L, N_MOD * D_MODEL), 0.02),
        'g_mix_norm': 1.0 + nrm(ks[6], (L, D_MODEL), 0.02),
        'g_ffn_norm': 1.0 + nrm(ks[7], (L, D_MODEL), 0.02),
        'w_in': nrm(ks[8], (L, D_MODEL, IN_PROJ_WIDTH), D_MODEL ** -0.5),
        'lambda_q1': nrm(ks[9], (L, DA_HEAD_DIM), 0.1),
        'lambda_k1': nrm(ks[10], (L, DA_HEAD_DIM), 0.1),
        'lambda_q2': nrm(ks[11], (L, DA_HEAD_DIM), 0.1),
        'lambda_k2': nrm(ks[12], (L, DA_HEAD_DIM), 0.1),
        'g_subln': 1.0 + nrm(ks[13], (L, DA_V_DIM), 0.02),
        'w_fourier': nrm(ks[14], (L, N_FOURIER_GROUPS, FOURIER_GROUP_DIM, FOURIER_GROUP_DIM), FOURIER_GROUP_DIM ** -0.5),
        'w_out': nrm(ks[15], (L, MIX_WIDTH, D_MODEL), MIX_WIDTH ** -0.5),
        'w_router_group': nrm(ks[16], (L, D_MODEL, N_GROUPS), D_MODEL ** -0.5),
        'b_router_group': nrm(ks[17], (L, N_GROUPS), 0.01),
        'w_router_expert': nrm(ks[18], (L, D_MODEL, N_EXPERTS), D_MODEL ** -0.5),
        'b_router_expert': nrm(ks[19], (L, N_EXPERTS), 0.01),
        'w_gate': nrm(ks[20], (L, N_EXPERTS, D_MODEL, D_EXPERT), D_MODEL ** -0.5),
        'w_up': nrm(ks[21], (L, N_EXPERTS, D_MODEL, D_EXPERT), D_MODEL ** -0.5),
        'w_down': nrm(ks[22], (L, N_EXPERTS, D_EXPERT, D_MODEL), D_EXPERT ** -0.5),
        'g_final': 1.0 + nrm(ks[23], (D_MODEL,), 0.02),
    }

def first_block(x, c, ctx, c_ctx, w_ada, b_ada, g_mix_norm, g_ffn_norm, w_in,
              lambda_q1, lambda_k1, lambda_q2, lambda_k2, g_subln, w_fourier, w_out,
              w_router_group, b_router_group, w_router_expert, b_router_expert,
              w_gate, w_up, w_down, g_final):
    b, s, d = x.shape
    n_ctx = ctx.shape[1]
    ROWS = s // GRID_W
    cos, sin = axial_rope_tables(ROWS, x.dtype)
    o_k = QK_WIDTH
    o_v = 2 * QK_WIDTH
    o_f = 2 * QK_WIDTH + ATTN_WIDTH
    xl, xc = x, ctx
    for l in range(DEPTH):
        last = l == DEPTH - 1
        lambda_init = 0.8 - 0.6 * math.exp(-0.3 * l)
        lam = diff_lambda(lambda_q1[l], lambda_k1[l], lambda_q2[l], lambda_k2[l], lambda_init)
        mod_l = (jax.nn.silu(c) @ w_ada[l] + b_ada[l]).reshape(b, N_MOD, 1, d)
        mod_c = (jax.nn.silu(c_ctx) @ w_ada[l] + b_ada[l]).reshape(N_MOD, d)
        sh1, sc1, gt1, sh2, sc2, gt2 = (mod_l[:, i] for i in range(N_MOD))
        csh1, csc1, cgt1, csh2, csc2, cgt2 = (mod_c[i] for i in range(N_MOD))
        wl = w_in[l]
        moe_args = (w_router_group[l], b_router_group[l], w_router_expert[l], b_router_expert[l],
                    w_gate[l], w_up[l], w_down[l])

        hl = modulate(rms_norm(xl, g_mix_norm[l]), sh1, sc1)
        pl = hl @ wl
        ql = apply_axial_rope(pl[..., :o_k].reshape(b, s, N_DA_HEADS, 2, DA_HEAD_DIM), cos, sin)
        kl = apply_axial_rope(pl[..., o_k:o_v].reshape(b, s, N_DA_HEADS, 2, DA_HEAD_DIM), cos, sin)
        vl = pl[..., o_v:o_f].reshape(b, s, N_DA_HEADS, DA_V_DIM)
        fl = pl[..., o_f:]

        hc = modulate(rms_norm(xc, g_mix_norm[l]), csh1, csc1)
        pc_kv = hc @ wl[:, o_k:o_f]
        kc = pc_kv[..., :QK_WIDTH].reshape(b, n_ctx, N_DA_HEADS, 2, DA_HEAD_DIM)
        vc = pc_kv[..., QK_WIDTH:].reshape(b, n_ctx, N_DA_HEADS, DA_V_DIM)

        k_all = jnp.concatenate([kc, kl], axis=1)
        v_all = jnp.concatenate([vc, vl], axis=1)
        mix_l = jnp.concatenate([diff_attention(ql, k_all, v_all, lam, g_subln[l], lambda_init),
                                 fourier_mix(fl, w_fourier[l])], axis=-1)
        xl = xl + gt1 * (mix_l @ w_out[l])
        h2l = modulate(rms_norm(xl, g_ffn_norm[l]), sh2, sc2)

        if last:
            xl = xl + gt2 * hier_moe(h2l.reshape(b * s, d), *moe_args).reshape(b, s, d)
        else:
            qc = (hc @ wl[:, :o_k]).reshape(b, n_ctx, N_DA_HEADS, 2, DA_HEAD_DIM)
            fc = hc @ wl[:, o_f:]
            mix_c = jnp.concatenate([diff_attention(qc, kc, vc, lam, g_subln[l], lambda_init),
                                     fourier_mix(fc, w_fourier[l])], axis=-1)
            xc = xc + cgt1 * (mix_c @ w_out[l])
            h2c = modulate(rms_norm(xc, g_ffn_norm[l]), csh2, csc2)
            y = hier_moe(jnp.concatenate([h2l.reshape(b * s, d), h2c.reshape(b * n_ctx, d)], axis=0), *moe_args)
            xl = xl + gt2 * y[:b * s].reshape(b, s, d)
            xc = xc + cgt2 * y[b * s:].reshape(b, n_ctx, d)
    return rms_norm(xl, g_final)


DEPTH_2 = 2

N_MIXERS = 2
N_A_LAYERS = (DEPTH_2 + 1) // 2
N_B_LAYERS = DEPTH_2 // 2
NORM_EPS = 1e-5
D_FF = 4 * D_MODEL

S5_WIDTH = D_MODEL
S5_GROUP = 16
S5_GROUPS = S5_WIDTH // S5_GROUP
S5_STATE = 64
S5_CHUNK = 128
S5_DT_MIN = 0.001
S5_DT_MAX = 0.1

M2_D_INNER = 2 * D_MODEL
M2_HEADDIM = 64
M2_HEADS = M2_D_INNER // M2_HEADDIM
M2_GROUPS = 4
M2_HPG = M2_HEADS // M2_GROUPS
M2_STATE = 128
M2_CONV = 4
M2_CHUNK = 128
M2_CONV_DIM = M2_D_INNER + 2 * M2_GROUPS * M2_STATE
M2_IN_DIM = M2_D_INNER + M2_CONV_DIM + M2_HEADS
M2_DT_MIN = 0.001
M2_DT_MAX = 0.1


def _rmsnorm(x, g):
    xf = x.astype(jnp.float32)
    y = xf * lax.rsqrt(jnp.mean(xf * xf, axis=-1, keepdims=True) + NORM_EPS)
    return (y * g.astype(jnp.float32)).astype(x.dtype)

def _modulate(h, shift, scale):
    return h * (1 + scale) + shift

def _sq_relu_mlp(h, w1, w2):
    a = jax.nn.relu(h @ w1)
    return (a * a) @ w2

def _s5_combine(e1, e2):
    a1, b1 = e1
    a2, b2 = e2
    return a2 * a1, a2 * b1 + b2

def _s5_mixer(h, w_in, lam_re, lam_im, log_dt, b_re, b_im, c_re, c_im, d, w_glu, b_glu):
    f32 = jnp.float32
    bsz, L, _ = h.shape
    nc = L // S5_CHUNK
    u = (h @ w_in).astype(f32)
    lam = lax.complex(lam_re.astype(f32), lam_im.astype(f32))
    dt = jnp.exp(log_dt.astype(f32))[:, None]
    lam_dt = lam * dt
    lam_bar = jnp.exp(lam_dt)
    b_bar = ((lam_bar - 1) / lam)[..., None] * lax.complex(b_re.astype(f32), b_im.astype(f32))
    c_mat = lax.complex(c_re.astype(f32), c_im.astype(f32))
    steps = jnp.arange(1, S5_CHUNK + 1, dtype=f32)[:, None, None]
    a_pow = jnp.exp(lam_dt[None] * steps)
    a_elems = jnp.broadcast_to(lam_bar, (bsz, S5_CHUNK, S5_GROUPS, S5_STATE))
    u_blocks = u.reshape(bsz, nc, S5_CHUNK, S5_GROUPS, S5_GROUP).transpose(1, 0, 2, 3, 4)

    def block_step(carry, u_blk):
        bu = jnp.einsum('btgh,gph->btgp', u_blk.astype(jnp.complex64), b_bar)
        _, hs = lax.associative_scan(_s5_combine, (a_elems, bu), axis=1)
        hs = hs + a_pow[None] * carry[:, None]
        y = jnp.einsum('btgp,ghp->btgh', hs, c_mat).real
        return hs[:, -1], y

    carry0 = jnp.zeros((bsz, S5_GROUPS, S5_STATE), jnp.complex64)
    _, ys = lax.scan(block_step, carry0, u_blocks)
    y = ys.transpose(1, 0, 2, 3, 4).reshape(bsz, L, S5_WIDTH) + d.astype(f32) * u
    g = jax.nn.gelu(y)
    ab = g @ w_glu.astype(f32) + b_glu.astype(f32)
    val, gate = jnp.split(ab, 2, axis=-1)
    return (val * jax.nn.sigmoid(gate)).astype(h.dtype)

def _causal_dwconv(u, w):
    return lax.conv_general_dilated(u, w[:, None, :].astype(u.dtype), (1,), [(M2_CONV - 1, 0)],
                                    dimension_numbers=('NWC', 'WIO', 'NWC'),
                                    feature_group_count=u.shape[-1])

def _segsum(a):
    t = a.shape[-1]
    cs = jnp.cumsum(a, axis=-1)
    diff = cs[..., :, None] - cs[..., None, :]
    mask = jnp.tril(jnp.ones((t, t), dtype=bool))
    return jnp.where(mask, diff, -jnp.inf)

def _ssd_mixer(h, w_in, conv_w, conv_b, dt_bias, a_log, d, norm_g, w_out):
    f32 = jnp.float32
    bsz, L, _ = h.shape
    nc = L // M2_CHUNK
    G, R, P, N, Q = M2_GROUPS, M2_HPG, M2_HEADDIM, M2_STATE, M2_CHUNK
    zxbcdt = h @ w_in
    z, xbc, dt_raw = jnp.split(zxbcdt, [M2_D_INNER, M2_D_INNER + M2_CONV_DIM], axis=-1)
    xbc = jax.nn.silu(_causal_dwconv(xbc, conv_w) + conv_b)
    xs, b_in, c_in = jnp.split(xbc, [M2_D_INNER, M2_D_INNER + G * N], axis=-1)
    dt = jax.nn.softplus(dt_raw.astype(f32) + dt_bias.astype(f32))
    a = -jnp.exp(a_log.astype(f32)).reshape(G, R)
    xs = xs.astype(f32).reshape(bsz, nc, Q, G, R, P)
    b_in = b_in.astype(f32).reshape(bsz, nc, Q, G, N)
    c_in = c_in.astype(f32).reshape(bsz, nc, Q, G, N)
    dt = dt.reshape(bsz, nc, Q, G, R)
    xdt = xs * dt[..., None]
    a_dt = jnp.transpose(dt * a, (0, 3, 4, 1, 2))
    a_cs = jnp.cumsum(a_dt, axis=-1)
    l_mat = jnp.exp(_segsum(a_dt))
    cb = jnp.einsum('bclgn,bcsgn->bcgls', c_in, b_in)
    y_diag = jnp.einsum('bcgls,bgrcls,bcsgrp->bclgrp', cb, l_mat, xdt)
    decay_states = jnp.exp(a_cs[..., -1:] - a_cs)
    states = jnp.einsum('bclgn,bgrcl,bclgrp->bcgrpn', b_in, decay_states, xdt)
    chunk_decay = jnp.exp(a_cs[..., -1])

    def carry_step(carry, inp):
        st, dec = inp
        return dec[..., None, None] * carry + st, carry

    _, prev = lax.scan(carry_step, jnp.zeros((bsz, G, R, P, N), f32),
                       (jnp.moveaxis(states, 1, 0), jnp.moveaxis(chunk_decay, -1, 0)))
    prev = jnp.moveaxis(prev, 0, 1)
    y_off = jnp.einsum('bclgn,bcgrpn,bgrcl->bclgrp', c_in, prev, jnp.exp(a_cs))
    y = y_diag + y_off + xs * d.astype(f32).reshape(G, R, 1)
    y = y.reshape(bsz, L, M2_D_INNER) * jax.nn.silu(z.astype(f32))
    yg = y.reshape(bsz, L, G, M2_D_INNER // G)
    yg = yg * lax.rsqrt(jnp.mean(yg * yg, axis=-1, keepdims=True) + NORM_EPS)
    y = yg.reshape(bsz, L, M2_D_INNER) * norm_g.astype(f32)
    return y.astype(h.dtype) @ w_out

def second_inputs(seed: int = 0) -> dict:
    f32 = jnp.float32
    key = jax.random.key(seed)
    it = iter(jax.random.split(key, 28))

    def nrm(shape, scale):
        return scale * jax.random.normal(next(it), shape, f32)

    D, F = D_MODEL, D_FF
    NA, NB = N_A_LAYERS, N_B_LAYERS
    G, P, H = S5_GROUPS, S5_STATE, S5_GROUP
    x = nrm((BATCH, SEQ, D), 1.0)
    c = nrm((BATCH, D), 1.0)
    ada_w = nrm((DEPTH_2, D, N_MOD * D), 0.5 * D ** -0.5)
    ada_b = nrm((DEPTH_2, N_MOD * D), 0.02)
    norm_mix_g = 1.0 + nrm((DEPTH_2, D), 0.05)
    norm_mlp_g = 1.0 + nrm((DEPTH_2, D), 0.05)
    mlp_w1 = nrm((DEPTH_2, D, F), D ** -0.5)
    mlp_w2 = nrm((DEPTH_2, F, D), F ** -0.5)
    s5_w_in = nrm((NA, D, S5_WIDTH), D ** -0.5)
    s5_lambda_re = -0.5 + nrm((NA, G, P), 0.01)
    s5_lambda_im = math.pi * jnp.arange(P, dtype=f32) + nrm((NA, G, P), 0.01)
    s5_log_dt = jax.random.uniform(next(it), (NA, G), f32, minval=math.log(S5_DT_MIN), maxval=math.log(S5_DT_MAX))
    s5_b_re = nrm((NA, G, P, H), (2 * H) ** -0.5)
    s5_b_im = nrm((NA, G, P, H), (2 * H) ** -0.5)
    s5_c_re = nrm((NA, G, H, P), (2 * P) ** -0.5)
    s5_c_im = nrm((NA, G, H, P), (2 * P) ** -0.5)
    s5_d = nrm((NA, S5_WIDTH), 1.0)
    s5_w_glu = nrm((NA, S5_WIDTH, 2 * D), S5_WIDTH ** -0.5)
    s5_b_glu = nrm((NA, 2 * D), 0.02)
    m2_w_in = nrm((NB, D, M2_IN_DIM), D ** -0.5)
    m2_conv_w = nrm((NB, M2_CONV, M2_CONV_DIM), M2_CONV ** -0.5)
    m2_conv_b = nrm((NB, M2_CONV_DIM), 0.02)
    dt0 = jnp.exp(jax.random.uniform(next(it), (NB, M2_HEADS), f32, minval=math.log(M2_DT_MIN), maxval=math.log(M2_DT_MAX)))
    m2_dt_bias = dt0 + jnp.log(-jnp.expm1(-dt0))
    m2_a_log = jnp.log(jax.random.uniform(next(it), (NB, M2_HEADS), f32, minval=1.0, maxval=16.0))
    m2_d = 1.0 + nrm((NB, M2_HEADS), 0.1)
    m2_norm_g = 1.0 + nrm((NB, M2_D_INNER), 0.05)
    m2_w_out = nrm((NB, M2_D_INNER, D), M2_D_INNER ** -0.5)
    final_norm_g = 1.0 + nrm((D,), 0.05)
    return {'x': x, 'c': c, 'ada_w': ada_w, 'ada_b': ada_b,
            'norm_mix_g': norm_mix_g, 'norm_mlp_g': norm_mlp_g,
            'mlp_w1': mlp_w1, 'mlp_w2': mlp_w2,
            's5_w_in': s5_w_in, 's5_lambda_re': s5_lambda_re, 's5_lambda_im': s5_lambda_im,
            's5_log_dt': s5_log_dt, 's5_b_re': s5_b_re, 's5_b_im': s5_b_im,
            's5_c_re': s5_c_re, 's5_c_im': s5_c_im, 's5_d': s5_d,
            's5_w_glu': s5_w_glu, 's5_b_glu': s5_b_glu,
            'm2_w_in': m2_w_in, 'm2_conv_w': m2_conv_w, 'm2_conv_b': m2_conv_b,
            'm2_dt_bias': m2_dt_bias, 'm2_a_log': m2_a_log, 'm2_d': m2_d,
            'm2_norm_g': m2_norm_g, 'm2_w_out': m2_w_out,
            'final_norm_g': final_norm_g}

def second_block(x, c, ada_w, ada_b, norm_mix_g, norm_mlp_g, mlp_w1, mlp_w2,
              s5_w_in, s5_lambda_re, s5_lambda_im, s5_log_dt, s5_b_re, s5_b_im,
              s5_c_re, s5_c_im, s5_d, s5_w_glu, s5_b_glu,
              m2_w_in, m2_conv_w, m2_conv_b, m2_dt_bias, m2_a_log, m2_d,
              m2_norm_g, m2_w_out, final_norm_g):
    cond = jax.nn.silu(c)
    for i in range(DEPTH_2):
        mod = cond @ ada_w[i] + ada_b[i]
        sh1, sc1, g1, sh2, sc2, g2 = jnp.split(mod[:, None, :], N_MOD, axis=-1)
        h = _modulate(_rmsnorm(x, norm_mix_g[i]), sh1, sc1)
        j = i // N_MIXERS
        if i % N_MIXERS == 0:
            y = _s5_mixer(h, s5_w_in[j], s5_lambda_re[j], s5_lambda_im[j], s5_log_dt[j],
                          s5_b_re[j], s5_b_im[j], s5_c_re[j], s5_c_im[j], s5_d[j],
                          s5_w_glu[j], s5_b_glu[j])
        else:
            y = _ssd_mixer(h, m2_w_in[j], m2_conv_w[j], m2_conv_b[j], m2_dt_bias[j],
                           m2_a_log[j], m2_d[j], m2_norm_g[j], m2_w_out[j])
        x = x + g1 * y
        h = _modulate(_rmsnorm(x, norm_mlp_g[i]), sh2, sc2)
        x = x + g2 * _sq_relu_mlp(h, mlp_w1[i], mlp_w2[i])
    return _rmsnorm(x, final_norm_g)


def setup_inputs(seed=0):
    out = dict(first_inputs(seed))
    for name, value in second_inputs(seed + 1).items():
        if name != "x":
            out[name + "_2"] = value
    return out


def reference(
    x, c, ctx, c_ctx, w_ada, b_ada, g_mix_norm, g_ffn_norm, w_in, lambda_q1, lambda_k1,
    lambda_q2, lambda_k2, g_subln, w_fourier, w_out, w_router_group, b_router_group,
    w_router_expert, b_router_expert, w_gate, w_up, w_down, g_final, c_2, ada_w_2, ada_b_2,
    norm_mix_g_2, norm_mlp_g_2, mlp_w1_2, mlp_w2_2, s5_w_in_2, s5_lambda_re_2, s5_lambda_im_2,
    s5_log_dt_2, s5_b_re_2, s5_b_im_2, s5_c_re_2, s5_c_im_2, s5_d_2, s5_w_glu_2, s5_b_glu_2,
    m2_w_in_2, m2_conv_w_2, m2_conv_b_2, m2_dt_bias_2, m2_a_log_2, m2_d_2, m2_norm_g_2,
    m2_w_out_2, final_norm_g_2,
):
    x = first_block(
        x, c, ctx, c_ctx, w_ada, b_ada, g_mix_norm, g_ffn_norm, w_in, lambda_q1, lambda_k1,
        lambda_q2, lambda_k2, g_subln, w_fourier, w_out, w_router_group, b_router_group,
        w_router_expert, b_router_expert, w_gate, w_up, w_down, g_final,
    )
    return second_block(
        x, c_2, ada_w_2, ada_b_2, norm_mix_g_2, norm_mlp_g_2, mlp_w1_2, mlp_w2_2, s5_w_in_2,
        s5_lambda_re_2, s5_lambda_im_2, s5_log_dt_2, s5_b_re_2, s5_b_im_2, s5_c_re_2, s5_c_im_2,
        s5_d_2, s5_w_glu_2, s5_b_glu_2, m2_w_in_2, m2_conv_w_2, m2_conv_b_2, m2_dt_bias_2,
        m2_a_log_2, m2_d_2, m2_norm_g_2, m2_w_out_2, final_norm_g_2,
    )


_drawn_inputs = setup_inputs


def setup_inputs(seed=0):
    import zlib

    import numpy as np

    out = dict(_drawn_inputs(seed))
    spreads = {}
    factors = {'g_mix_norm': 8.0,
     'g_ffn_norm': 4.646,
     'lambda_q1': 8.0,
     'lambda_k1': 8.0,
     'lambda_q2': 2.842,
     'lambda_k2': 48.416,
     'g_subln': 8.0,
     'b_router_group': 8.0,
     'b_router_expert': 8.0,
     'g_final': 2.722,
     'norm_mix_g_2': 8.578,
     's5_lambda_re_2': 64.0,
     's5_lambda_im_2': 49.832,
     's5_log_dt_2': 58.072,
     's5_b_re_2': 64.0,
     's5_b_im_2': 64.0,
     's5_c_re_2': 64.0,
     's5_c_im_2': 64.0,
     's5_b_glu_2': 29.921,
     'm2_conv_b_2': 41.829,
     'm2_d_2': 200.0,
     'm2_norm_g_2': 28.311,
     'norm_mlp_g_2': 4.136}
    for name, (base, spread) in spreads.items():
        noise = np.random.default_rng([zlib.crc32(name.encode()), seed]).standard_normal(out[name].shape)
        drawn = base * np.exp(spread * noise) if base else spread * noise
        out[name] = jnp.asarray(drawn.astype(out[name].dtype))
    for name, factor in factors.items():
        out[name] = (out[name] * factor).astype(out[name].dtype)
    return out
```

```python
from contextlib import ExitStack

import numpy as np

import concourse.bass as bass
from concourse import mybir

F32 = mybir.dt.float32
I32 = mybir.dt.int32
U32 = mybir.dt.uint32
ALU = mybir.AluOpType
ACT = mybir.ActivationFunctionType
AX = mybir.AxisListType.X

P = 128
D = 1024
KC = D // P
T = 512
TC = T // P
CTX = 256
KEYS = CTX + T
KCH = KEYS // P
HEADS = 4
DH = 64
GROUPS = 4
EPG = 8
EXPERTS = GROUPS * EPG
DE = 512
BLOCKS = T * 2 // P + EXPERTS
NMOD = 6
TN = 512
ADA_TILES = NMOD * KC // 4
DFF = 4096
LAMBDA_INIT = 0.8 - 0.6 * 1.0
S5_TILES = 32
S5_Q = 128
S5_NC = T // S5_Q
ROUND = 1.5 * 2.0 ** 23
TWO_PI_HI = 6.28125
TWO_PI_LO = 2 * np.pi - TWO_PI_HI
PI_BELOW = 3.1415925
HP = 16
M2_IN = 2048
M2_XBC = 3072
M2_HEADS = 32
M2_XC = M2_IN // P
M2_CC = M2_XBC // P
M2_G = 4
M2_Q = 128
M2_NC = T // M2_Q

COLS = {}
for _name, _count in (
    ("b_ada", 48), ("ada_b0", 48), ("ada_b1", 48), ("g_mix", 8), ("g_ffn", 8), ("g_final", 8), ("g_subln", 1),
    ("nmix0", 8), ("nmix1", 8), ("nmlp0", 8), ("nmlp1", 8), ("s5_d", 8), ("b_glu", 16), ("conv_w", 96),
    ("conv_b", 24), ("m2_d", 16), ("m2_norm", 16), ("fin", 8), ("dt_bias", 1), ("a_log", 1),
    ("lam_re", 32), ("lam_im", 32), ("log_dt", 32),
):
    COLS[_name] = (sum(n for _, n in COLS.values()), _count)
NCOLS = sum(n for _, n in COLS.values())


def build(nc, A, out):
    with ExitStack() as ctx:
        def sb(name, shape, dt=F32):
            return ctx.enter_context(nc.sbuf_tensor(name, shape, dt))

        def sem(name):
            return ctx.enter_context(nc.semaphore(name))

        PS = ctx.enter_context(nc.psum_tensor("PS", [P, 8, 512], F32))
        ring = sb("ring", [P, 2, KC, TN])
        work = sb("work", [P, 32768])
        x = sb("x", [P, KC, T])
        h = sb("h", [P, KC, T])
        cols = sb("cols_sb", [P, NCOLS])
        cond2 = sb("cond2", [P, D])
        mats = sb("mats_sb", [P, 4, P])
        ones = sb("ones", [P, P])
        mod1 = sb("mod1", [P, NMOD * KC])
        modc = sb("modc", [P, 2 * KC])
        mod2 = sb("mod2", [P, 2, NMOD * KC])
        gain = sb("gain", [P, 7, KC])
        norm_buf = sb("norm_buf", [P, 2 * T])
        var, rstd = norm_buf[:, 0:T], norm_buf[:, T:2 * T]
        iota = sb("iota_sb", [P, 64])
        tokid = sb("tokid_sb", [P, TC], U32)
        route_i = sb("route_i", [P, 64], I32)
        slot_of = sb("slot_of", [P, 2, TC], I32)
        gates = sb("gates", [P, 2, TC])
        eye, tri, causal, rope_rot = (mats[:, n, :] for n in range(4))

        def wk(at, *shape):
            n = int(np.prod(shape))
            v = work[:, at:at + n]
            if len(shape) == 2:
                return v.rearrange("p (a b) -> p a b", b=shape[1])
            if len(shape) == 3:
                return v.rearrange("p (a b c) -> p a b c", b=shape[1], c=shape[2])
            return v

        def col(name, n=0, count=1):
            first = COLS[name][0] + n
            return cols[:, first:first + count]

        qT, kT, vtok, fT, cx = wk(0, 4, T), wk(2048, 4, KEYS), wk(5120, KCH, 512), wk(8192, 4, T), wk(10240, KC, CTX)
        rope_c, rope_s = wk(12288, T), wk(12800, T)
        dft_c, dft_s, dft_ch = wk(13312, TC, T), wk(15360, TC, T), wk(17408, 256)
        fab, fre = wk(17664, 2, 4, 256), wk(19712, T)
        attn_a, attn_t = wk(20224, 2, KEYS), wk(21760, KEYS)
        aT, oT, oSq = wk(22528, KCH, T), wk(25600, T), wk(26112, T)
        rope_t = wk(26624, 2, 2, T)
        probs = wk(28672, 2, 2, KEYS)
        ada_buf = [wk(20224, 4, D), wk(24320, 4, D)]
        cond1 = wk(28672, 2, D)
        lam_t = wk(30720, 2, 64)
        wfour = wk(31744, GROUPS, P)
        lam4 = wk(32256, 4, 64)
        csq = wk(0, KC, CTX)
        sm = sb("sm", [P, 64])
        rowmax, negmax, rowsum, rsum, rneg = (sm[:, 4 * n:4 * n + 4].rearrange("p (a b) -> p a b", b=2) for n in range(5))
        lam_d, neglam = sm[:, 24:28], sm[:, 28:29]
        gsub = sm[:, 29:30]

        expert_w = [(ring[:, 0, :, :], ring[:, 1, :, :], wk(0, 4, D)),
                    (wk(4096, KC, DE), wk(8192, KC, DE), wk(12288, 4, D))]
        xb, xbT, silu_b = wk(16384, 2, D), wk(18432, 2, KC, P), wk(20480, 2, DE)
        hid, hidT, yb = wk(21504, 2, DE), wk(22528, 2, 4, P), wk(23552, 2, D)
        hrow = wk(25600, 2, D)
        y_of = wk(0, 2, TC, D)
        ysum = wk(16384, 2, D)
        routing_at = [27648]

        def rt(*shape):
            n = int(np.prod(shape))
            routing_at[0] += n
            return wk(routing_at[0] - n, *shape)

        w_router, b_router = rt(KC, GROUPS + EXPERTS), rt(GROUPS + EXPERTS)
        logits, g_exp, g_eq, g_id, g_hot = rt(TC, GROUPS + EXPERTS), rt(TC, 4), rt(TC, 4), rt(TC, 4), rt(TC, 4)
        e_all, e_in, e_eq, e_id, e_hot = rt(TC, 4, EPG), rt(TC, EPG), rt(TC, EPG), rt(TC, EPG), rt(2, TC, EPG)
        e_left, hot, chosen = rt(TC, EPG), rt(2, TC, EXPERTS), rt(TC, EXPERTS)
        place, n_blk, blk_end, blk_start, ones_e = (rt(TC, EXPERTS), rt(EXPERTS), rt(EXPERTS), rt(EXPERTS), rt(EXPERTS))
        blk_cmp, blk_exp, pair_cmp, n_pairs = rt(BLOCKS, EXPERTS), rt(BLOCKS), rt(BLOCKS // 2), rt(1)
        g_max, g_sum, g_idx, top1, top2, e_idx = (rt(TC) for _ in range(6))
        e2, e_sum, dest = rt(TC), rt(TC), rt(2, TC)
        assert routing_at[0] <= 32768
        idx_all = sb("idx_all", [P, BLOCKS], U32)
        idx = [sb(f"idx{s}", [P, 1], U32) for s in range(2)]
        slot_at = sb("slot_at", [P, 2, TC], U32)
        slot_part = sb("slot_part", [P, 2, 2, TC], I32)
        zeros = sb("zeros", [P, 256])
        h_rows = nc.dram_tensor("h_rows", [T + 1, D], F32, kind="Internal").ap()
        slot_tok = nc.dram_tensor("slot_tok", [P * BLOCKS, 1], U32, kind="Internal").ap()
        y_rows = nc.dram_tensor("y_rows", [(BLOCKS + 2) * P, D], F32, kind="Internal").ap()

        turn = wk(0, 2, S5_TILES, S5_Q)
        uT, s5_b, s5_c, s5_cf = wk(8192, KC, T), wk(12288, KC, 2, P), wk(14336, S5_TILES, 2, HP), wk(15360, S5_TILES, 2, HP)
        scan_g, rot, scan_h = wk(16384, 4, 2, T), wk(20480, 2, 4, T), wk(24576, 4, 2, T)
        turn_t = [wk(16384 + 2048 * n, S5_TILES, 64) for n in range(4)]
        u_now, b_now, c_now = wk(28672, T), wk(29184, 2, P), wk(29440, 4, 288)
        s5_at = [30592]

        def s5p():
            s5_at[0] += S5_TILES
            return wk(s5_at[0] - S5_TILES, S5_TILES)

        (s5_dt, s5_a, s5_th, s5_k, s5_r, s5_ab, radius, half_sin, half_cos, s5_s2, cos1, sin1, num_re, num_im, f_re, f_im,
         s5_den, s5_t) = (s5p() for _ in range(18))
        carry, carry_t = wk(s5_at[0], 2, 4), wk(s5_at[0] + 8, 4, 4)
        glu_gate, glu_t = wk(0, 2, T), wk(1024, 2, T)
        mlp_h = wk(0, DFF // P, T)
        ada_buf1 = [wk(16384, 4, D), wk(20480, 4, D)]
        xs, xs_now = wk(0, M2_CC, T), wk(12288, M2_CC, P)
        xdt, xdt_dec, state, b_tok = wk(15360, M2_IN), wk(17408, M2_IN), wk(19456, M2_IN), wk(21504, M2_G, P)
        cb = wk(22016, M2_G, P)
        decay, exp_cs, m_now, c_dec = (wk(22528 + 1024 * n, 2, 4, P) for n in range(4))
        y_tok = wk(26624, 2, 2 * P)
        dt_t, a_dt, a_cs, dt_raw, dt_abs = (wk(27136 + 512 * n, T)[0:M2_HEADS, :] for n in range(5))
        cs_tok, dt_tok, dec_tok, dec_chunk = (wk(29696 + 128 * n, M2_NC, M2_HEADS) for n in range(4))
        last_diag = wk(30208, M2_NC, M2_HEADS)[0:M2_HEADS, :, :]
        w_dt = wk(30336, KC, M2_HEADS)
        z_silu = wk(30592, 2, T)
        a_pos, sums_now = wk(31616, 1)[0:M2_HEADS, :], wk(31620, M2_Q)[0:M2_HEADS, :]
        m2_sq = wk(12288, M2_XC, T)

        in_cond, in_small, in_x, in_mix, in_late = (sem(n) for n in ("in_cond", "in_small", "in_x", "in_mix", "in_late"))
        tile_loaded = [sem("tile_loaded0"), sem("tile_loaded1")]
        tile_used = sem("tile_used")
        ada_loaded, ada_used = [sem("ada_loaded0"), sem("ada_loaded1")], sem("ada_used")
        consts_set, cond_ready, mods_ready = sem("consts_set"), sem("cond_ready"), sem("mods_ready")
        sq_ready, ms_done, var_ready, std_ready = sem("sq_ready"), sem("ms_done"), sem("var_ready"), sem("std_ready")
        xn_ready, h_ready = sem("xn_ready"), sem("h_ready")
        exp_in, exp_out = sem("exp_in"), sem("exp_out")
        proj_mm = sem("proj_mm")
        qkv_mm, qkv_evac, rope_mm, rope_done = sem("qkv_mm"), sem("qkv_evac"), sem("rope_mm"), sem("rope_done")
        ab_mm, ab_evac, fr_mm, fr_evac = sem("ab_mm"), sem("ab_evac"), sem("fr_mm"), sem("fr_evac")
        fo_mm, fo_evac = sem("fo_mm"), sem("fo_evac")
        score_mm, negmax_ready, exp_done, a_ready = sem("score_mm"), sem("negmax_ready"), sem("exp_done"), sem("a_ready")
        at_mm, at_evac, pv_mm, o_ready = sem("at_mm"), sem("at_evac"), sem("pv_mm"), sem("o_ready")
        osq_ready, oms_done, ovar_ready, ostd_ready = sem("osq_ready"), sem("oms_done"), sem("ovar_ready"), sem("ostd_ready")
        head_done, x1_ready, out_stored = sem("head_done"), sem("x1_ready"), sem("out_stored")
        idx_filled, zero_row, lg_mm = sem("idx_filled"), sem("zero_row"), sem("lg_mm")
        hrow_mm, hrow_evac, hrow_stored = sem("hrow_mm"), sem("hrow_evac"), [sem("hrow_stored0"), sem("hrow_stored1")]
        chosen_ready, rank_mm, route_ready = sem("chosen_ready"), sem("rank_mm"), sem("route_ready")
        idx_set, idx_stored, idx_loaded = sem("idx_set"), sem("idx_stored"), sem("idx_loaded")
        gate_loaded, up_loaded, down_loaded, xb_loaded, y_stored = (
            [sem(f"{n}{s}") for s in range(2)] for n in ("gate_loaded", "up_loaded", "down_loaded", "xb_loaded", "y_stored"))
        xT_mm, xT_evac, gate_mm, up_mm, silu_done = sem("xT_mm"), sem("xT_evac"), sem("gate_mm"), sem("up_mm"), sem("silu_done")
        hid_ready, hT_mm, hT_evac, down_mm, y_ready = sem("hid_ready"), sem("hT_mm"), sem("hT_evac"), sem("down_mm"), sem("y_ready")
        moe_done, y_loaded, ysum_ready, yT_mm, yT_used = sem("moe_done"), sem("y_loaded"), sem("ysum_ready"), sem("yT_mm"), sem("yT_used")
        y_zeroed, x2_ready = sem("y_zeroed"), sem("x2_ready")
        u_evac, dt_exp, angle_ready, trig_ready = (sem(n) for n in ("u_evac", "dt_exp", "angle_ready", "trig_ready"))
        c_zero, c_ready, ub_staged, c_staged = (sem(n) for n in ("c_zero", "c_ready", "ub_staged", "c_staged"))
        bu_mm, bu_used, state_ready, s5_mm, s5_used, gelu_done = (
            sem(n) for n in ("bu_mm", "bu_used", "state_ready", "s5_mm", "s5_used", "gelu_done"))
        glu_mm, gate_sig, glu_used = sem("glu_mm"), sem("gate_sig"), sem("glu_used")
        mlp1_mm, relu_done, sqr_done, mlp2_mm, mlp_added = (
            sem(n) for n in ("mlp1_mm", "relu_done", "sqr_done", "mlp2_mm", "mlp_added"))
        xbc_mm, conv_done, xs_ready, dt_mm, tok_mm = (sem(n) for n in ("xbc_mm", "conv_done", "xs_ready", "dt_mm", "tok_mm"))
        step_dve = sem("step_dve")
        step_act = sem("step_act")
        ssd_staged, xs_tok_mm, xdt_ready, xdt_dec_ready, b_tok_mm, b_tok_evac, cb_mm = (
            sem(n) for n in ("ssd_staged", "xs_tok_mm", "xdt_ready", "xdt_dec_ready", "b_tok_mm", "b_tok_evac", "cb_mm"))
        cs_mm, diff_ready, decay_ready, exp_cs_ready, m_ready, c_dec_ready = (
            sem(n) for n in ("cs_mm", "diff_ready", "decay_ready", "exp_cs_ready", "m_ready", "c_dec_ready"))
        y7_mm, y_tok_evac, y_turned, y_added, st_mm, state_new = (
            sem(n) for n in ("y7_mm", "y_tok_evac", "y_turned", "y_added", "st_mm", "state_new"))
        z_mm, z_ready, z_used, yn_ready, x5_ready = (sem(n) for n in ("z_mm", "z_ready", "z_used", "yn_ready", "x5_ready"))

        PAIRS = {}
        for name, n in (("in", 2), ("out", 1), ("s5_in", 1), ("glu", 2), ("mlp1_0", 4), ("mlp2_0", 4),
                        ("xbc", 3), ("z", 2), ("m2_out", 2), ("mlp1_1", 4), ("mlp2_1", 4)):
            PAIRS[name] = (sum(m for _, m in PAIRS.values()), n)

        def rows(w):
            return w.rearrange("(c p) n -> p c n", p=P)

        block = ctx.enter_context(nc.Block())

        @block.sync
        def _(sp):
            sp.dma_start(cond1, A["c_rows"][0:2, :].partition_broadcast(P)).then_inc(in_cond, 16)
            sp.dma_start(cond2[:], A["c_rows"][2, :].partition_broadcast(P)).then_inc(in_cond, 16)
            for name, tile in (("cols", cols), ("mats", mats), ("iota", iota), ("tokid", tokid)):
                sp.dma_start(tile[:], A[name]).then_inc(in_small, 16)
            sp.dma_start(lam4, A["lam4"]).then_inc(in_small, 16)

            def load_pairs(name, source, n=None, at=0):
                first, count = PAIRS[name]
                with sp.Fori(0, count if n is None else n) as i:
                    for s in range(2):
                        sp.wait_ge(tile_used, i * 2 + (2 * (first + at) + s + 1))
                        sp.dma_start(ring[:, s, :, :], source(i, s)).then_inc(tile_loaded[s], 16)

            def columns(w, first=0):
                return lambda i, s: rows(w)[:, :, bass.ds(i * (2 * TN) + (first + s * TN), TN)]

            sp.dma_start(x[:], A["xT"]).then_inc(in_x, 16)
            sp.dma_start(cx, A["ctxT"]).then_inc(in_x, 16)
            for name, tile in (("rope_c", rope_c), ("rope_s", rope_s), ("dft_c", dft_c), ("dft_s", dft_s),
                               ("dft_ch", dft_ch), ("wfour", wfour)):
                sp.dma_start(tile, A[name]).then_inc(in_mix, 16)
            load_pairs("in", columns(A["w_in"]))
            load_pairs("out", columns(A["w_out"]))

            sp.wait_ge(consts_set, 2)
            sp.dma_start(h_rows[T:T + 1, :].rearrange("o (q n) -> o q n", n=256),
                         zeros[0:1, :].unsqueeze(1).broadcast_to([1, 4, 256])).then_inc(zero_row, 16)
            y_quarters = y_rows.rearrange("(b p) (q n) -> q p b n", p=P, n=256)
            for q in range(4):
                sp.dma_start(y_quarters[q], zeros[:].unsqueeze(1).broadcast_to([P, BLOCKS + 2, 256])) \
                    .then_inc(y_stored[0] if q == 3 else y_zeroed, 16)
            sp.wait_ge(x1_ready, KC)
            sp.dma_start(w_router, A["w_router"]).then_inc(in_late, 16)
            sp.dma_start(b_router, A["b_router"]).then_inc(in_late, 16)
            sp.wait_ge(route_ready, 1)
            pairs = sp.value_load(route_i[0:1, BLOCKS:BLOCKS + 1], min_val=1, max_val=BLOCKS // 2)
            with sp.Fori(0, pairs) as i:
                for s in range(2):
                    e = sp.value_load(route_i[0:1, bass.ds(i * 2 + s, 1)], min_val=0, max_val=EXPERTS - 1)
                    for w, tile, used, loaded in (("w_gate", expert_w[s][0], gate_mm, gate_loaded[s]),
                                                  ("w_up", expert_w[s][1], up_mm, up_loaded[s]),
                                                  ("w_down", expert_w[s][2], down_mm, down_loaded[s])):
                        sp.wait_ge(used, i * 2 + (s + 1))
                        sp.dma_start(tile, A[w][bass.ds(e, 1), :, :].rearrange("o (c p) n -> p (o c) n", p=P)) \
                            .then_inc(loaded, 16)

            sp.wait_ge(ysum_ready, TC)
            sp.dma_start(s5_b, A["s5_b"]).then_inc(in_late, 16)
            sp.dma_start(s5_c, A["s5_c"]).then_inc(in_late, 16)
            load_pairs("s5_in", columns(A["s5_w_in"]))
            load_pairs("glu", lambda i, s: rows(A["w_glu"])[:, :, bass.ds(i * TN + s * D, TN)])

            def load_mlp(layer):
                load_pairs(f"mlp1_{layer}", columns(A["mlp_w1"][layer, :, :]))
                for half in range(2):
                    load_pairs(f"mlp2_{layer}", lambda i, s: A["mlp_w2"][
                        layer, bass.ds(i * (2 * D) + s * D, D), half * TN:(half + 1) * TN].rearrange("(c p) n -> p c n", p=P),
                        n=2, at=2 * half)

            load_mlp(0)
            sp.wait_ge(mlp_added, KC)
            sp.dma_start(w_dt, A["m2_w_dt"]).then_inc(in_late, 16)
            load_pairs("xbc", columns(A["m2_w_in"], M2_IN))
            load_pairs("z", columns(A["m2_w_in"]))
            load_pairs("m2_out", lambda i, s: A["m2_w_out"][s * D:(s + 1) * D, bass.ds(i * TN, TN)]
                       .rearrange("(c p) n -> p c n", p=P))
            load_mlp(1)
            sp.wait_ge(h_ready, 9 * KC)
            sp.dma_start(out, x[:]).then_inc(out_stored, 16)
            sp.wait_ge(out_stored, 16)

        @block.gpsimd
        def _(pool):
            pool.memset(ones[:], 1.0).then_inc(consts_set, 1)
            pool.memset(zeros[:], 0.0).then_inc(consts_set, 1)
            pool.iota(idx_all[:], [[0, BLOCKS]], base=T, channel_multiplier=0).then_inc(idx_set, 1)
            pool.wait_ge(idx_set, 1)
            pool.dma_start(slot_tok.rearrange("(p b) o -> p (b o)", b=BLOCKS), idx_all[:]).then_inc(idx_filled, 16)
            pool.sem_inc(ada_used, 2)
            for first, w in ((0, A["w_adaT"]), (1, A["ada_w_2T"][0, :, :])):
                with pool.Fori(0, ADA_TILES // 2) as i:
                    for s in range(2):
                        pool.wait_ge(ada_used, i * 2 + (ADA_TILES * first + s + 1))
                        pool.dma_start(ada_buf[s], w[bass.ds(i * (8 * P) + s * 4 * P, 4 * P), :]
                                       .rearrange("(n p) k -> p n k", p=P)).then_inc(ada_loaded[s], 16)

            pool.wait_ge(idx_filled, 16)
            pool.wait_ge(route_ready, 1)
            for k in range(2):
                for t in range(TC):
                    pool.indirect_dma_start(slot_tok, bass.IndirectOffsetOnAxis(slot_at[:, k, t:t + 1], 0),
                                            tokid[:, t:t + 1], None).then_inc(idx_stored, 16)
            pool.wait_ge(idx_stored, 16 * 2 * TC)
            pool.dma_start(idx_all[:], slot_tok.rearrange("(p b) o -> p (b o)", b=BLOCKS)).then_inc(idx_loaded, 16)
            pairs = pool.value_load(route_i[0:1, BLOCKS:BLOCKS + 1], min_val=1, max_val=BLOCKS // 2)
            pool.wait_ge(idx_loaded, 16)
            pool.wait_ge(zero_row, 16)
            for s in range(2):
                pool.wait_ge(hrow_stored[s], 32)
            with pool.Fori(0, pairs) as i:
                for s in range(2):
                    pool.wait_ge(xT_mm, i * 2 + (s + 1))
                    pool.tensor_copy(idx[s][:], idx_all[:, bass.ds(i * 2 + s, 1)])
                    pool.drain()
                    pool.indirect_dma_start(xb[:, s, :], None, h_rows, bass.IndirectOffsetOnAxis(idx[s][:, 0:1], 0)) \
                        .then_inc(xb_loaded[s], 16)
            pool.wait_ge(moe_done, 1)
            for t in range(TC):
                for k in range(2):
                    pool.indirect_dma_start(y_of[:, k, t, :], None, y_rows,
                                            bass.IndirectOffsetOnAxis(slot_of[:, k, t:t + 1].bitcast(U32), 0)) \
                        .then_inc(y_loaded, 16)
            pool.wait_ge(ysum_ready, TC)
            pool.memset(wk(29440, 1152), 0.0).then_inc(c_zero, 1)
            pool.wait_ge(glu_used, KC)
            with pool.Fori(0, ADA_TILES // 2) as i:
                for s in range(2):
                    pool.wait_ge(ada_used, i * 2 + (ADA_TILES * 2 + s + 1))
                    pool.dma_start(ada_buf1[s], A["ada_w_2T"][1, bass.ds(i * (8 * P) + s * 4 * P, 4 * P), :]
                                   .rearrange("(n p) k -> p n k", p=P)).then_inc(ada_loaded[s], 16)

        @block.tensor
        def _(pe):
            pe.sem_inc(tile_used, 2)

            def tile_wait(name, i, s):
                pe.wait_ge(tile_loaded[s], i * 16 + 16 * (PAIRS[name][0] + 1))

            def tile_done():
                pe.drain().then_inc(tile_used, 1)

            def norm_sum(k, sq, n, last=KC):
                for c in range(KC):
                    pe.wait_ge(sq_ready, KC * k + c + 1)
                    mm = nc.tensor.matmul(PS[:, k % 2, 0:n], ones[:], sq[:, c, 0:n], start=(c == 0), stop=(c == KC - 1))
                mm.then_inc(ms_done, 1)

            pe.wait_ge(consts_set, 1)
            norm_sum(0, h, T)
            norm_sum(1, csq, CTX)

            pe.wait_ge(h_ready, 2 * KC)
            group = [0]

            def projection(s, cols_of, rhs_of, n):
                e = group[0]
                if e >= 8:
                    pe.wait_ge(qkv_evac, e - 7)
                for c in range(KC):
                    mm = nc.tensor.matmul(PS[:, e % 8, 0:n], cols_of(c), rhs_of(c), start=(c == 0), stop=(c == KC - 1))
                mm.then_inc(qkv_mm, 1)
                group[0] += 1

            tile_wait("in", 0, 0)
            for k in range(4):
                projection(0, lambda c: ring[:, 0, c, k * P:(k + 1) * P], lambda c: h[:, c, :], T)
            tile_done()
            tile_wait("in", 0, 1)
            for k in range(4):
                projection(1, lambda c: ring[:, 1, c, k * P:(k + 1) * P], lambda c: h[:, c, :], T)
            for k in range(4):
                projection(1, lambda c: ring[:, 1, c, k * P:(k + 1) * P], lambda c: cx[:, c, :], CTX)
            tile_done()
            tile_wait("in", 1, 0)
            for k in range(KCH):
                tok = (lambda c: cx[:, c, k * P:(k + 1) * P]) if k < 2 else (lambda c: h[:, c, (k - 2) * P:(k - 1) * P])
                projection(0, tok, lambda c: ring[:, 0, c, :], TN)
            tile_done()
            tile_wait("in", 1, 1)
            for k in range(4):
                projection(1, lambda c: ring[:, 1, c, k * P:(k + 1) * P], lambda c: h[:, c, :], T)
            tile_done()

            pe.wait_ge(qkv_evac, 22)
            for j in range(8):
                src = qT[:, j, :] if j < 4 else kT[:, j - 4, CTX:KEYS]
                nc.tensor.matmul(PS[:, j, :], rope_rot, src, start=True, stop=True).then_inc(rope_mm, 1)

            pe.wait_ge(rope_done, 8)
            pe.wait_ge(in_mix, 16 * 6)
            for g in range(GROUPS):
                if g:
                    pe.wait_ge(ab_evac, 2 * g)
                for t in range(TC):
                    mm = nc.tensor.matmul(PS[:, t // 2, (t % 2) * 256:(t % 2 + 1) * 256], fT[:, g, t * P:(t + 1) * P],
                                          dft_ch, start=True, stop=True)
                    if t % 2:
                        mm.then_inc(ab_mm, 1)
                pe.wait_ge(ab_evac, 2 * g + 2)
                for t in range(TC):
                    nc.tensor.matmul(PS[:, 2, :], fab[:, g % 2, t, 0:P], dft_c[:, t, :], start=(t == 0), stop=False)
                    mm = nc.tensor.matmul(PS[:, 2, :], fab[:, g % 2, t, P:2 * P], dft_s[:, t, :], start=False,
                                          stop=(t == TC - 1))
                mm.then_inc(fr_mm, 1)
                pe.wait_ge(fr_evac, g + 1)
                if g:
                    pe.wait_ge(fo_evac, g)
                nc.tensor.matmul(PS[:, 3, :], wfour[:, g, :], fre, start=True, stop=True).then_inc(fo_mm, 1)

            def scores(n):
                hd, qc = n // TC, n % TC
                if n:
                    pe.wait_ge(exp_done, 2 * n)
                for m in range(2):
                    half = slice(m * DH, (m + 1) * DH)
                    q = qT[half, hd, qc * P:(qc + 1) * P]
                    nc.tensor.matmul(PS[:, 2 * m, :], q, kT[half, hd, 0:512], start=True, stop=True)
                    nc.tensor.matmul(PS[:, 2 * m + 1, 0:KEYS - 512], q, kT[half, hd, 512:KEYS], start=True,
                                     stop=True).then_inc(score_mm, 1)

            pe.wait_ge(fo_evac, GROUPS)
            scores(0)
            for n in range(HEADS * TC):
                hd, qc = n // TC, n % TC
                if n + 1 < HEADS * TC:
                    scores(n + 1)
                pe.wait_ge(a_ready, n + 1)
                if n:
                    pe.wait_ge(at_evac, n)
                for k in range(KCH):
                    mm = nc.tensor.transpose(PS[:, 4 + k // 4, (k % 4) * P:(k % 4 + 1) * P],
                                             attn_a[:, n % 2, k * P:(k + 1) * P], eye)
                mm.then_inc(at_mm, 1)
                if qc == TC - 1:
                    pe.wait_ge(at_evac, n + 1)
                    if hd:
                        pe.wait_ge(head_done, hd)
                    for k in range(KCH):
                        mm = nc.tensor.matmul(PS[:, 6, :], vtok[:, k, hd * P:(hd + 1) * P], aT[:, k, :],
                                              start=(k == 0), stop=(k == KCH - 1))
                    mm.then_inc(pv_mm, 1)
                    pe.wait_ge(osq_ready, hd + 1)
                    nc.tensor.matmul(PS[:, 7, :], ones[:], oSq, start=True, stop=True).then_inc(oms_done, 1)

            pe.wait_ge(head_done, HEADS)
            for s in range(2):
                tile_wait("out", 0, s)
                for k in range(4):
                    for c in range(KC):
                        mm = nc.tensor.matmul(PS[:, 4 * s + k, :], ring[:, s, c, k * P:(k + 1) * P], h[:, c, :],
                                              start=(c == 0), stop=(c == KC - 1))
                    mm.then_inc(proj_mm, 1)
                tile_done()

            pe.wait_ge(x1_ready, KC)
            norm_sum(2, h, T)
            pe.wait_ge(h_ready, 3 * KC)
            pe.wait_ge(in_late, 32)
            for t in range(TC):
                for c in range(KC):
                    mm = nc.tensor.matmul(PS[:, 1, t * 36:(t + 1) * 36], h[:, c, t * P:(t + 1) * P], w_router[:, c, :],
                                          start=(c == 0), stop=(c == KC - 1))
            mm.then_inc(lg_mm, 1)
            for t in range(TC):
                if t >= 2:
                    pe.wait_ge(hrow_evac, t - 1)
                for c in range(KC):
                    mm = nc.tensor.transpose(PS[:, 2 + 2 * (t % 2) + c // 4, (c % 4) * P:(c % 4 + 1) * P],
                                             h[:, c, t * P:(t + 1) * P], eye)
                mm.then_inc(hrow_mm, 1)
            pe.wait_ge(chosen_ready, 1)
            for t in range(TC):
                for before in range(t):
                    nc.tensor.matmul(PS[:, 6, t * EXPERTS:(t + 1) * EXPERTS], ones[:], chosen[:, before, :],
                                     start=(before == 0), stop=False)
                nc.tensor.matmul(PS[:, 6, t * EXPERTS:(t + 1) * EXPERTS], tri, chosen[:, t, :], start=(t == 0), stop=True)
            for t in range(TC):
                mm = nc.tensor.matmul(PS[:, 6, TC * EXPERTS:(TC + 1) * EXPERTS], ones[:], chosen[:, t, :],
                                      start=(t == 0), stop=(t == TC - 1))
            mm.then_inc(rank_mm, 1)

            pe.wait_ge(route_ready, 1)
            pe.wait_ge(hrow_evac, TC)
            pairs = pe.value_load(route_i[0:1, BLOCKS:BLOCKS + 1], min_val=1, max_val=BLOCKS // 2)
            for freed in (gate_mm, up_mm, down_mm, xT_mm):
                pe.sem_inc(freed, 2)

            def turn_tokens(i, s):
                pe.wait_ge(xb_loaded[s], i * 16 + 16)
                pe.wait_ge(xT_evac, i * 2 + (s + 1))
                for c in range(KC):
                    mm = nc.tensor.transpose(PS[:, c // 4, (c % 4) * P:(c % 4 + 1) * P], xb[:, s, c * P:(c + 1) * P], eye)
                mm.then_inc(xT_mm, 1)

            def gate_up(i, s):
                pe.wait_ge(xT_evac, i * 2 + (s + 2))
                pe.wait_ge(hid_ready, i * 2 + (s + 1))
                for loaded, w, bank, done in ((gate_loaded[s], expert_w[s][0], 2, gate_mm),
                                              (up_loaded[s], expert_w[s][1], 3, up_mm)):
                    pe.wait_ge(loaded, i * 16 + 16)
                    for c in range(KC):
                        mm = nc.tensor.matmul(PS[:, bank, :], xbT[:, s, c, :], w[:, c, :], start=(c == 0),
                                              stop=(c == KC - 1))
                    mm.then_inc(done, 1)

            def turn_hidden(i, s):
                pe.wait_ge(hid_ready, i * 2 + (s + 2))
                pe.wait_ge(hT_evac, i * 2 + (s + 1))
                for c in range(4):
                    mm = nc.tensor.transpose(PS[:, 4, c * P:(c + 1) * P], hid[:, s, c * P:(c + 1) * P], eye)
                mm.then_inc(hT_mm, 1)

            def down(i, s):
                pe.wait_ge(hT_evac, i * 2 + (s + 2))
                pe.wait_ge(y_ready, i * 2 + (s + 1))
                pe.wait_ge(down_loaded[s], i * 16 + 16)
                for n in range(2):
                    for c in range(4):
                        mm = nc.tensor.matmul(PS[:, 5 + n, :], hidT[:, s, c, :], expert_w[s][2][:, c, n * 512:(n + 1) * 512],
                                              start=(c == 0), stop=(c == 3))
                mm.then_inc(down_mm, 1)

            with pe.Fori(0, pairs) as i:
                turn_tokens(i, 0)
                gate_up(i, 0)
                turn_tokens(i, 1)
                turn_hidden(i, 0)
                down(i, 0)
                gate_up(i, 1)
                turn_hidden(i, 1)
                down(i, 1)
            pe.wait_ge(moe_done, 1)
            for t in range(TC):
                pe.wait_ge(ysum_ready, t + 1)
                if t >= 2:
                    pe.wait_ge(yT_used, t - 1)
                for c in range(KC):
                    mm = nc.tensor.transpose(PS[:, 2 * (t % 2) + c // 4, (c % 4) * P:(c % 4 + 1) * P],
                                             ysum[:, t % 2, c * P:(c + 1) * P], eye)
                mm.then_inc(yT_mm, 1)
            pe.wait_ge(x2_ready, 1)
            norm_sum(3, h, T)

            norm_sum(4, h, T)
            pe.wait_ge(h_ready, 5 * KC)
            for s in range(2):
                tile_wait("s5_in", 0, s)
                for k in range(4):
                    for c in range(KC):
                        mm = nc.tensor.matmul(PS[:, 4 * s + k, :], ring[:, s, c, k * P:(k + 1) * P], h[:, c, :],
                                              start=(c == 0), stop=(c == KC - 1))
                    mm.then_inc(proj_mm, 1)
                tile_done()
            pe.wait_ge(u_evac, KC)
            pe.sem_inc(bu_mm, 4)
            pe.sem_inc(s5_mm, 1)
            with pe.Fori(0, KC) as q:
                pe.wait_ge(ub_staged, q + 1)
                for a in range(4):
                    pe.wait_ge(bu_used, q * 4 + (5 if a == 3 else 4))
                    for r in range(2):
                        mm = nc.tensor.matmul(PS[:, 2 * (a % 3) + r, :], b_now[32 * a:32 * a + 32, r, :],
                                              u_now[32 * a:32 * a + 32, :], start=True, stop=True)
                    mm.then_inc(bu_mm, 1)
                pe.wait_ge(c_staged, q + 1)
                pe.wait_ge(s5_used, q + 1)
                c_pad = c_now.rearrange("p a n -> p (a n)")
                for a in range(4):
                    pe.wait_ge(state_ready, q * 4 + (a + 1))
                    for r in range(2):
                        at = (2 * a + r) * P
                        mm = nc.tensor.matmul(PS[:, 6, :], c_pad[:, at:at + P], scan_h[:, a, r, :],
                                              start=(a == 0 and r == 0), stop=(a == 3 and r == 1))
                mm.then_inc(s5_mm, 1)
            pe.wait_ge(gelu_done, KC)
            for i in range(2):
                if i:
                    pe.wait_ge(glu_used, 4)
                for s in range(2):
                    tile_wait("glu", i, s)
                    for k in range(4):
                        for c in range(KC):
                            mm = nc.tensor.matmul(PS[:, 4 * s + k, :], ring[:, s, c, k * P:(k + 1) * P], h[:, c, :],
                                                  start=(c == 0), stop=(c == KC - 1))
                        mm.then_inc(glu_mm, 1)
                    tile_done()

            def gemm_loop(name, n, rhs, done, freed, base):
                with pe.Fori(0, n) as i:
                    for s in range(2):
                        tile_wait(name, i, s)
                        for k in range(4):
                            pe.wait_ge(freed, i * 8 + (base + 4 * s + k + 1))
                            for c in range(KC):
                                mm = nc.tensor.matmul(PS[:, 4 * s + k, :], ring[:, s, c, k * P:(k + 1) * P], rhs[:, c, :],
                                                      start=(c == 0), stop=(c == KC - 1))
                            mm.then_inc(done, 1)
                        tile_done()

            def mlp(layer, k_norm):
                norm_sum(k_norm, h, T)
                pe.wait_ge(h_ready, (k_norm + 1) * KC)
                gemm_loop(f"mlp1_{layer}", 4, h, mlp1_mm, relu_done, 32 * layer)
                for half in range(2):
                    for pair in range(2):
                        for s in range(2):
                            part = 2 * pair + s
                            pe.wait_ge(sqr_done, 32 * layer + 8 * (part + 1))
                            tile_wait(f"mlp2_{layer}", 2 * half + pair, s)
                            for k in range(4):
                                if part == 0:
                                    pe.wait_ge(relu_done, 32 * layer + 32 + 4 * half + k + 1)
                                for c in range(KC):
                                    mm = nc.tensor.matmul(PS[:, 4 * half + k, :], ring[:, s, c, k * P:(k + 1) * P],
                                                          mlp_h[:, 8 * part + c, :], start=(part == 0 and c == 0),
                                                          stop=(part == 3 and c == KC - 1))
                                if part == 3:
                                    mm.then_inc(mlp2_mm, 1)
                            tile_done()

            pe.wait_ge(glu_used, KC)
            mlp(0, 5)

            pe.wait_ge(mlp_added, KC)
            norm_sum(6, h, T)
            pe.wait_ge(h_ready, 7 * KC)
            gemm_loop("xbc", 3, h, xbc_mm, conv_done, 0)
            pe.wait_ge(conv_done, 8 + M2_CC)
            pe.wait_ge(in_late, 80)
            for c in range(KC):
                mm = nc.tensor.matmul(PS[0:M2_HEADS, 0, :], w_dt[:, c, :], h[:, c, :], start=(c == 0), stop=(c == KC - 1))
            mm.then_inc(dt_mm, 1)
            pe.wait_ge(step_dve, 2)
            for c in range(M2_NC):
                for n, rows_of in enumerate((dt_t, a_cs)):
                    nc.tensor.transpose(PS[:, 1, (4 * n + c) * M2_HEADS:(4 * n + c + 1) * M2_HEADS],
                                        rows_of[:, c * M2_Q:(c + 1) * M2_Q], eye[0:M2_HEADS, 0:M2_HEADS])
            nc.tensor.matmul(PS[:, 2, 0:M2_NC * M2_HEADS], ones[0:M2_HEADS, :], last_diag.rearrange("p c h -> p (c h)"),
                             start=True, stop=True).then_inc(tok_mm, 1)
            pe.wait_ge(step_act, 2)
            pe.wait_ge(xs_ready, M2_CC)
            pe.sem_inc(y7_mm, 2)
            pe.sem_inc(y_turned, 2)
            with pe.Fori(0, M2_NC) as c:
                pe.wait_ge(ssd_staged, c + 1)
                for j in range(M2_XC):
                    mm = nc.tensor.transpose(PS[:, j // 4, (j % 4) * P:(j % 4 + 1) * P], xs_now[:, j, :], eye)
                    if j % 4 == 3:
                        mm.then_inc(xs_tok_mm, 1)
                for g in range(M2_G):
                    mm = nc.tensor.transpose(PS[:, 4, g * P:(g + 1) * P], xs_now[:, M2_XC + g, :], eye)
                mm.then_inc(b_tok_mm, 1)
                for g in range(M2_G):
                    mm = nc.tensor.matmul(PS[:, 5, g * P:(g + 1) * P], xs_now[:, M2_XC + g, :], xs_now[:, M2_XC + M2_G + g, :],
                                          start=True, stop=True)
                mm.then_inc(cb_mm, 1)

                def spread_sums(q):
                    if q:
                        pe.wait_ge(diff_ready, c * 8 + q)
                        pe.wait_ge(exp_cs_ready, c * 8 + q)
                    for k in range(4):
                        n = 4 * q + k
                        mm = nc.tensor.matmul(PS[:, 6, k * P:(k + 1) * P], eye[0:M2_HEADS, n:n + 1].broadcast_to([M2_HEADS, P]),
                                              sums_now, start=True, stop=True)
                    mm.then_inc(cs_mm, 1)

                def turn_y(q):
                    pe.wait_ge(y_tok_evac, c * 8 + (q + 2))
                    pe.wait_ge(b_tok_evac, c + 1)
                    pe.wait_ge(y_added, c * 8 + (q + 1))
                    for j in range(2):
                        mm = nc.tensor.transpose(PS[:, 4, j * P:(j + 1) * P], y_tok[:, q % 2, j * P:(j + 1) * P], eye)
                    mm.then_inc(y_turned, 1)

                spread_sums(0)
                for q in range(8):
                    if q < 7:
                        spread_sums(q + 1)
                    pe.wait_ge(m_ready, c * 8 + (q + 1))
                    pe.wait_ge(c_dec_ready, c * 8 + (q + 3))
                    pe.wait_ge(xdt_ready, c * 4 + (q // 2 + 1))
                    pe.wait_ge(y_tok_evac, c * 8 + (q + 1))
                    for k in range(4):
                        at = (4 * q + k) * 64
                        nc.tensor.matmul(PS[:, 7, k * 64:(k + 1) * 64], m_now[:, q % 2, k, :], xdt[:, at:at + 64], start=True,
                                         stop=False)
                        mm = nc.tensor.matmul(PS[:, 7, k * 64:(k + 1) * 64], c_dec[:, q % 2, k, :], state[:, at:at + 64],
                                              start=False, stop=True)
                    mm.then_inc(y7_mm, 1)
                    if q:
                        turn_y(q - 1)
                turn_y(7)
                pe.wait_ge(xdt_dec_ready, c + 1)
                for g in range(M2_G):
                    mm = nc.tensor.matmul(PS[:, g, :], b_tok[:, g, :], xdt_dec[:, g * 512:(g + 1) * 512], start=True, stop=True)
                mm.then_inc(st_mm, 1)
            pe.wait_ge(state_new, 1 + M2_NC)
            gemm_loop("z", 2, h, z_mm, z_ready, 0)
            for g in range(M2_G):
                for j in range(4):
                    pe.wait_ge(osq_ready, HEADS + 4 * g + j + 1)
                    mm = nc.tensor.matmul(PS[:, g, :], ones[:], m2_sq[:, 4 * g + j, :], start=(j == 0), stop=(j == 3))
                mm.then_inc(oms_done, 1)
            pe.wait_ge(yn_ready, M2_XC)
            for half in range(2):
                for s in range(2):
                    tile_wait("m2_out", half, s)
                    for k in range(4):
                        for c in range(KC):
                            mm = nc.tensor.matmul(PS[:, 4 * half + k, :], ring[:, s, c, k * P:(k + 1) * P], xs[:, 8 * s + c, :],
                                                  start=(s == 0 and c == 0), stop=(s == 1 and c == KC - 1))
                        if s:
                            mm.then_inc(proj_mm, 1)
                    tile_done()
            pe.wait_ge(x5_ready, KC)
            mlp(1, 7)
            pe.wait_ge(mlp_added, 2 * KC)
            norm_sum(8, h, T)

        @block.scalar
        def _(act):
            def copy(out, in_):
                return nc.scalar.activation(out, in_, ACT.Copy)

            def norm_squares(src, sq):
                for c in range(KC):
                    nc.scalar.activation(sq[:, c, :], src[:, c, :], ACT.Square).then_inc(sq_ready, 1)

            def norm_root(k, n):
                act.wait_ge(var_ready, k + 1)
                nc.scalar.activation(rstd[:, 0:n], var[:, 0:n], ACT.Sqrt).then_inc(std_ready, 1)

            def norm_affine(k, dst, scale, shift):
                for c in range(KC):
                    act.wait_ge(xn_ready, KC * k + c + 1)
                    nc.scalar.activation(dst[:, c, :], dst[:, c, :], ACT.Identity, scale=scale[:, c:c + 1],
                                         bias=shift[:, c:c + 1] if shift is not None else 0.0).then_inc(h_ready, 1)

            act.wait_ge(in_cond, 32)
            nc.scalar.activation(cond1, cond1, ACT.Silu).then_inc(cond_ready, 1)
            nc.scalar.activation(cond2[:], cond2[:], ACT.Silu).then_inc(cond_ready, 1)
            act.wait_ge(in_x, 32)
            norm_squares(x, h)
            norm_squares(cx, csq)
            norm_root(0, T)
            act.wait_ge(exp_in, 1)
            nc.scalar.activation(lam_d[:, 2:4], lam_d[:, 0:2], ACT.Exp).then_inc(exp_out, 1)
            act.wait_ge(mods_ready, 1)
            norm_affine(0, h, gain[:, 0, :], mod1[:, 0:KC])
            norm_root(1, CTX)
            norm_affine(1, cx, gain[:, 1, :], modc[:, 0:KC])

            for e in range(22):
                act.wait_ge(qkv_mm, e + 1)
                if e < 4:
                    dst, n = qT[:, e, :], T
                elif e < 8:
                    dst, n = kT[:, e - 4, CTX:KEYS], T
                elif e < 12:
                    dst, n = kT[:, e - 8, 0:CTX], CTX
                elif e < 18:
                    dst, n = vtok[:, e - 12, :], TN
                else:
                    dst, n = fT[:, e - 18, :], T
                copy(dst, PS[:, e % 8, 0:n]).then_inc(qkv_evac, 1)

            for g in range(GROUPS):
                for b in range(2):
                    act.wait_ge(ab_mm, 2 * g + b + 1)
                    if g >= 2:
                        act.wait_ge(fr_mm, g - 1)
                    copy(fab[:, g % 2, 2 * b:2 * b + 2, :], PS[:, b, :].rearrange("p (t n) -> p t n", n=256)) \
                        .then_inc(ab_evac, 1)
                act.wait_ge(fr_mm, g + 1)
                if g:
                    act.wait_ge(fo_mm, g)
                copy(fre, PS[:, 2, :]).then_inc(fr_evac, 1)
                act.wait_ge(fo_mm, g + 1)
                copy(h[:, HEADS + g, :], PS[:, 3, :]).then_inc(fo_evac, 1)

            def exps(n):
                for m in range(2):
                    act.wait_ge(negmax_ready, 2 * n + m + 1)
                    if n >= 2:
                        act.wait_ge(a_ready, n - 1)
                    nc.scalar.activation(probs[:, n % 2, m, :],
                                         PS[:, 2 * m:2 * m + 2, :].rearrange("p a b -> p (a b)")[:, 0:KEYS], ACT.Exp,
                                         bias=negmax[:, n % 2, m:m + 1], scale=DH ** -0.5,
                                         accum_out=rowsum[:, n % 2, m:m + 1]).then_inc(exp_done, 1)

            exps(0)
            for n in range(HEADS * TC):
                hd, qc = n // TC, n % TC
                if n + 1 < HEADS * TC:
                    exps(n + 1)
                act.wait_ge(at_mm, n + 1)
                if hd and qc == 0:
                    act.wait_ge(pv_mm, hd)
                copy(aT[:, :, qc * P:(qc + 1) * P],
                     PS[:, 4:6, :].rearrange("p a (b q) -> p (a b) q", q=P)[:, 0:KCH, :]).then_inc(at_evac, 1)
                if qc == TC - 1:
                    act.wait_ge(o_ready, hd + 1)
                    nc.scalar.activation(oSq, oT, ACT.Square).then_inc(osq_ready, 1)
                    act.wait_ge(ovar_ready, hd + 1)
                    nc.scalar.activation(rstd, var, ACT.Sqrt).then_inc(ostd_ready, 1)

            act.wait_ge(x1_ready, KC)
            norm_squares(x, h)
            norm_root(2, T)
            norm_affine(2, h, gain[:, 2, :], mod1[:, 3 * KC:4 * KC])
            for t in range(TC):
                act.wait_ge(hrow_mm, t + 1)
                if t >= 2:
                    act.wait_ge(hrow_stored[t % 2], 16)
                copy(hrow[:, t % 2, :].rearrange("p (a b) -> p a b", a=2),
                     PS[:, 2 + 2 * (t % 2):4 + 2 * (t % 2), :]).then_inc(hrow_evac, 1)
                act.wait_ge(hrow_evac, t + 1)
                act.dma_start(h_rows[t * P:(t + 1) * P, :], hrow[:, t % 2, :]).then_inc(hrow_stored[t % 2], 16)
            act.wait_ge(exp_in, 2)
            nc.scalar.activation(g_exp, g_exp, ACT.Exp).then_inc(exp_out, 1)
            act.wait_ge(exp_in, 3)
            nc.scalar.activation(e2, e2, ACT.Exp).then_inc(exp_out, 1)

            act.wait_ge(route_ready, 1)
            pairs = act.value_load(route_i[0:1, BLOCKS:BLOCKS + 1], min_val=1, max_val=BLOCKS // 2)
            for freed in (xT_evac, hT_evac):
                act.sem_inc(freed, 1)
            act.wait_ge(y_zeroed, 48)
            act.wait_ge(y_stored[0], 16)

            def tokens_turned(i, s):
                act.wait_ge(xT_mm, i * 2 + (s + 3))
                copy(xbT[:, s, :, :].rearrange("p (a c) q -> p a (c q)", a=2), PS[:, 0:2, :]).then_inc(xT_evac, 1)

            def gate_silu(i, s):
                act.wait_ge(gate_mm, i * 2 + (s + 3))
                nc.scalar.activation(silu_b[:, s, :], PS[:, 2, :], ACT.Silu).then_inc(silu_done, 1)

            def hidden_turned(i, s):
                act.wait_ge(hT_mm, i * 2 + (s + 1))
                copy(hidT[:, s, :, :].rearrange("p c q -> p (c q)"), PS[:, 4, :]).then_inc(hT_evac, 1)

            def store_last(i, s):
                act.wait_ge(y_ready, i * 2 + (s + 1))
                act.dma_start(y_rows[bass.ds(i * (2 * P) + s * P, P), :], yb[:, 1 - s, :]).then_inc(y_stored[1 - s], 16)

            with act.Fori(0, pairs) as i:
                tokens_turned(i, 0)
                gate_silu(i, 0)
                store_last(i, 0)
                tokens_turned(i, 1)
                hidden_turned(i, 0)
                gate_silu(i, 1)
                store_last(i, 1)
                hidden_turned(i, 1)
            act.wait_ge(y_ready, pairs * 2 + 1)
            act.dma_start(y_rows[bass.ds(pairs * (2 * P), P), :], yb[:, 1, :]).then_inc(y_stored[1], 16)
            for s in range(2):
                act.wait_ge(y_stored[s], pairs * 16 + 16)
            act.sem_inc(moe_done, 1)

            act.wait_ge(x2_ready, 1)
            norm_squares(x, h)
            norm_root(3, T)
            norm_affine(3, x, col("g_final", 0, KC), None)

            act.wait_ge(h_ready, 4 * KC)
            norm_squares(x, h)
            act.wait_ge(in_small, 16 * 5)
            nc.scalar.activation(s5_dt, col("log_dt", 0, S5_TILES), ACT.Exp).then_inc(dt_exp, 1)
            norm_root(4, T)
            norm_affine(4, h, gain[:, 3, :], mod2[:, 0, 0:KC])
            act.wait_ge(angle_ready, 1)
            nc.scalar.activation(radius, s5_a, ACT.Exp)
            nc.scalar.activation(half_sin, s5_r, ACT.Sin)
            nc.scalar.activation(half_cos, s5_ab, ACT.Sin).then_inc(trig_ready, 1)
            for k in range(KC):
                act.wait_ge(proj_mm, KC + k + 1)
                copy(uT[:, k, :], PS[:, k, :]).then_inc(u_evac, 1)
            act.wait_ge(in_late, 64)
            act.wait_ge(u_evac, KC)
            act.wait_ge(c_zero, 1)
            act.wait_ge(c_ready, 1)
            with act.Fori(0, KC) as q:
                act.wait_ge(bu_mm, q * 4 + 4)
                copy(u_now, uT[:, bass.ds(q, 1), :].rearrange("p a n -> p (a n)"))
                copy(b_now, s5_b[:, bass.ds(q, 1), :, :].rearrange("p a r n -> p (a r) n")).then_inc(ub_staged, 1)
                act.wait_ge(s5_mm, q + 1)
                for g in range(2):
                    part = slice(64 * g, 64 * g + 64)
                    for r in range(2):
                        last = copy(c_now[part, :, r * P + HP * g:r * P + HP * (g + 1)],
                                    s5_cf[part, bass.ds(q * 4, 4), r, :])
                last.then_inc(c_staged, 1)
            for k in range(KC):
                act.wait_ge(s5_used, k + 2)
                nc.scalar.activation(h[:, k, :], h[:, k, :], ACT.Gelu_apprx_tanh).then_inc(gelu_done, 1)
            for i in range(2):
                for k in range(4):
                    n = 4 * i + k
                    act.wait_ge(glu_mm, 8 * i + 4 + k + 1)
                    if n >= 2:
                        act.wait_ge(glu_used, n - 1)
                    nc.scalar.activation(glu_gate[:, n % 2, :], PS[:, 4 + k, :], ACT.Sigmoid, bias=col("b_glu", KC + n)) \
                        .then_inc(gate_sig, 1)

            def mlp(layer, k_norm):
                norm_squares(x, h)
                norm_root(k_norm, T)
                norm_affine(k_norm, h, gain[:, 4 + 2 * layer, :], mod2[:, layer, 3 * KC:4 * KC])
                with act.Fori(0, 4) as i:
                    for k in range(8):
                        act.wait_ge(relu_done, i * 8 + (32 * layer + 8 + k + 1))
                        chunk = mlp_h[:, bass.ds(i * 8 + k, 1), :]
                        nc.scalar.activation(chunk, chunk, ACT.Square).then_inc(sqr_done, 1)

            act.wait_ge(glu_used, KC)
            mlp(0, 5)

            act.wait_ge(mlp_added, KC)
            norm_squares(x, h)
            norm_root(6, T)
            norm_affine(6, h, gain[:, 5, :], mod2[:, 1, 0:KC])
            with act.Fori(0, 3) as i:
                for k in range(8):
                    act.wait_ge(conv_done, i * 8 + (8 + k + 1))
                    chunk = xs[:, bass.ds(i * 8 + k, 1), :]
                    nc.scalar.activation(chunk, chunk, ACT.Silu, bias=cols[:, bass.ds(i * 8 + (COLS["conv_b"][0] + k), 1)]) \
                        .then_inc(xs_ready, 1)
            act.wait_ge(step_dve, 1)
            nc.scalar.activation(dt_abs, dt_raw, ACT.Abs)
            act.drain()
            nc.scalar.activation(dt_abs, dt_abs, ACT.Exp, scale=-1.0)
            nc.scalar.activation(a_pos, col("a_log")[0:M2_HEADS, :], ACT.Exp)
            act.drain()
            nc.scalar.activation(dt_abs, dt_abs, ACT.Ln, bias=1.0).then_inc(step_act, 1)
            act.wait_ge(step_dve, 3)
            nc.scalar.activation(dec_tok, dec_tok, ACT.Exp)
            nc.scalar.activation(dec_chunk, PS[:, 2, 0:M2_NC * M2_HEADS].rearrange("p (c h) -> p c h", h=M2_HEADS), ACT.Exp) \
                .then_inc(step_act, 1)
            act.sem_inc(y_tok_evac, 1)
            act.wait_ge(xs_ready, M2_CC)
            with act.Fori(0, M2_NC) as c:
                act.wait_ge(state_new, c + 1)
                copy(sums_now, a_cs[:, bass.ds(c * M2_Q, M2_Q)])
                copy(xs_now, xs[:, :, bass.ds(c * M2_Q, M2_Q)]).then_inc(ssd_staged, 1)
                act.wait_ge(b_tok_mm, c + 1)
                copy(b_tok.rearrange("p g n -> p (g n)"), PS[:, 4, :]).then_inc(b_tok_evac, 1)

                def exponentials(q):
                    act.wait_ge(cs_mm, c * 8 + (q + 1))
                    act.wait_ge(c_dec_ready, c * 8 + (q + 1))
                    nc.scalar.activation(exp_cs[:, q % 2, :, :].rearrange("p k n -> p (k n)"), PS[:, 6, :], ACT.Exp) \
                        .then_inc(exp_cs_ready, 1)
                    act.wait_ge(diff_ready, c * 8 + (q + 1))
                    nc.scalar.activation(decay[:, q % 2, :, :], decay[:, q % 2, :, :], ACT.Exp).then_inc(decay_ready, 1)

                exponentials(0)
                for q in range(8):
                    if q < 7:
                        exponentials(q + 1)
                    act.wait_ge(y7_mm, c * 8 + (q + 3))
                    act.wait_ge(y_turned, c * 8 + (q + 1))
                    copy(y_tok[:, q % 2, :], PS[:, 7, 0:2 * P]).then_inc(y_tok_evac, 1)
            act.sem_inc(z_ready, 8)
            with act.Fori(0, 2) as i:
                for k in range(8):
                    act.wait_ge(z_mm, i * 8 + (k + 1))
                    act.wait_ge(z_used, i * 8 + (k + 1))
                    nc.scalar.activation(z_silu[:, k % 2, :], PS[:, k, :], ACT.Silu).then_inc(z_ready, 1)
            for g in range(M2_G):
                for j in range(4):
                    n = 4 * g + j
                    act.wait_ge(z_used, 2 + n + 1)
                    nc.scalar.activation(m2_sq[:, n, :], xs[:, n, :], ACT.Square).then_inc(osq_ready, 1)
            for g in range(M2_G):
                act.wait_ge(ovar_ready, HEADS + g + 1)
                nc.scalar.activation(rstd, var, ACT.Sqrt).then_inc(ostd_ready, 1)
            act.wait_ge(x5_ready, KC)
            mlp(1, 7)
            act.wait_ge(mlp_added, 2 * KC)
            norm_squares(x, h)
            norm_root(8, T)
            norm_affine(8, x, col("fin", 0, KC), None)

        @block.vector
        def _(dve):
            tt, ts, stt = nc.vector.tensor_tensor, nc.vector.tensor_scalar, nc.vector.scalar_tensor_tensor

            def norm_var(k, n, eps):
                dve.wait_ge(ms_done, k + 1)
                ts(var[:, 0:n], PS[:, k % 2, 0:n], 1.0 / D, eps, ALU.mult, ALU.add).then_inc(var_ready, 1)

            def norm_divide(k, src, dst, n):
                dve.wait_ge(std_ready, k + 1)
                nc.vector.reciprocal(rstd[:, 0:n], rstd[:, 0:n])
                dve.drain()
                for c in range(KC):
                    tt(dst[:, c, :], src[:, c, :], rstd[:, 0:n], ALU.mult).then_inc(xn_ready, 1)

            def modulation(pairs, base, cond_row, bias, dst, buf=ada_buf):
                with dve.Fori(*pairs) as i:
                    for s in range(2):
                        dve.wait_ge(ada_loaded[s], i * 16 + 16 * (base // 2 + 1))
                        for n in range(4):
                            w = buf[s][:, n, :]
                            last = stt(w, w, 1.0, cond_row, ALU.mult, ALU.mult,
                                       accum_out=dst[:, bass.ds(i * 8 + (4 * s + n), 1)])
                        last.then_inc(ada_used, 1)
                dve.drain()
                done = slice(8 * pairs[0], 8 * pairs[1])
                tt(dst[:, done], dst[:, done], bias[:, done], ALU.add)

            def modulation_both(i, s):
                dve.wait_ge(ada_loaded[s], 16 * (i + 1))
                for n in range(4):
                    w, k = ada_buf[s][:, n, :], 8 * i + 4 * s + n
                    dve.drain()
                    stt(norm_buf[:], w, 1.0, cond1[:, 1, :], ALU.mult, ALU.mult, accum_out=modc[:, k:k + 1])
                    dve.drain()
                    last = stt(norm_buf[:], w, 1.0, cond1[:, 0, :], ALU.mult, ALU.mult, accum_out=mod1[:, k:k + 1])
                last.then_inc(ada_used, 1)

            def norm_gain(n, scale, g):
                stt(gain[:, n, :], scale, 1.0, col(g, 0, KC), ALU.add, ALU.mult)

            dve.wait_ge(in_small, 16 * 5)
            dve.wait_ge(cond_ready, 1)
            for i in range(2):
                for s in range(2):
                    modulation_both(i, s)
            dve.drain()
            tt(mod1[:, 0:2 * KC], mod1[:, 0:2 * KC], col("b_ada", 0, 16), ALU.add)
            tt(modc[:], modc[:], col("b_ada", 0, 16), ALU.add)
            dve.drain()
            norm_gain(0, mod1[:, KC:2 * KC], "g_mix")
            norm_gain(1, modc[:, KC:2 * KC], "g_mix")
            ts(gsub, col("g_subln"), 1.0 - LAMBDA_INIT, None, ALU.mult)
            tt(lam_t[:, 0, :], lam4[:, 0, :], lam4[:, 1, :], ALU.mult)
            tt(lam_t[:, 1, :], lam4[:, 2, :], lam4[:, 3, :], ALU.mult).then_inc(mods_ready, 1)
            dve.drain()
            nc.vector.tensor_reduce(lam_d[:, 0:2], lam_t, AX, ALU.add).then_inc(exp_in, 1)
            norm_var(0, T, 1e-6)
            norm_divide(0, x, h, T)
            dve.wait_ge(exp_out, 1)
            tt(neglam, lam_d[:, 3:4], lam_d[:, 2:3], ALU.subtract)
            dve.drain()
            ts(neglam, neglam, -LAMBDA_INIT, None, ALU.add)
            dve.wait_ge(h_ready, KC)
            norm_var(1, CTX, 1e-6)
            norm_divide(1, cx, cx, CTX)

            modulation((2, ADA_TILES // 2), 0, cond1[:, 0, :], col("b_ada", 0, 48), mod1)
            dve.wait_ge(cond_ready, 2)
            modulation((0, ADA_TILES // 2), ADA_TILES, cond2[:], col("ada_b0", 0, 48), mod2[:, 0, :])
            dve.drain()
            norm_gain(2, mod1[:, 4 * KC:5 * KC], "g_ffn")
            norm_gain(3, mod2[:, 0, KC:2 * KC], "nmix0")
            norm_gain(4, mod2[:, 0, 4 * KC:5 * KC], "nmlp0")

            dve.wait_ge(in_mix, 16 * 6)
            for j in range(8):
                dve.wait_ge(rope_mm, j + 1)
                src = qT[:, j, :] if j < 4 else kT[:, j - 4, CTX:KEYS]
                tt(rope_t[:, j % 2, 0, :], src, rope_c, ALU.mult)
                tt(rope_t[:, j % 2, 1, :], PS[:, j, :], rope_s, ALU.mult)
                dve.drain()
                tt(src, rope_t[:, j % 2, 0, :], rope_t[:, j % 2, 1, :], ALU.add).then_inc(rope_done, 1)

            def maxima(n):
                for m in range(2):
                    dve.wait_ge(score_mm, 2 * n + m + 1)
                    nc.vector.tensor_reduce(rowmax[:, n % 2, m:m + 1],
                                            PS[:, 2 * m:2 * m + 2, :].rearrange("p a b -> p (a b)")[:, 0:KEYS], AX, ALU.max)
                    dve.drain()
                    ts(negmax[:, n % 2, m:m + 1], rowmax[:, n % 2, m:m + 1], -DH ** -0.5, None, ALU.mult) \
                        .then_inc(negmax_ready, 1)

            maxima(0)
            for n in range(HEADS * TC):
                hd, qc, b = n // TC, n % TC, n % 2
                if n + 1 < HEADS * TC:
                    maxima(n + 1)
                dve.wait_ge(exp_done, 2 * n + 2)
                nc.vector.reciprocal(rsum[:, b, :], rowsum[:, b, :])
                dve.drain()
                tt(rneg[:, b, 1:2], rsum[:, b, 1:2], neglam, ALU.mult)
                dve.drain()
                ts(attn_t, probs[:, b, 1, :], rneg[:, b, 1:2], None, ALU.mult)
                dve.drain()
                if n >= 2:
                    dve.wait_ge(at_mm, n - 1)
                stt(attn_a[:, b, :], probs[:, b, 0, :], rsum[:, b, 0:1], attn_t, ALU.mult, ALU.add).then_inc(a_ready, 1)
                if qc == TC - 1:
                    dve.wait_ge(pv_mm, hd + 1)
                    nc.vector.tensor_copy(oT, PS[:, 6, :]).then_inc(o_ready, 1)
                    dve.wait_ge(oms_done, hd + 1)
                    ts(var, PS[:, 7, :], 1.0 / P, 1e-6, ALU.mult, ALU.add).then_inc(ovar_ready, 1)
                    dve.wait_ge(ostd_ready, hd + 1)
                    nc.vector.reciprocal(rstd, rstd)
                    dve.drain()
                    stt(h[:, hd, :], oT, gsub, rstd, ALU.mult, ALU.mult).then_inc(head_done, 1)

            for c in range(KC):
                dve.wait_ge(proj_mm, c + 1)
                stt(x[:, c, :], PS[:, c, :], mod1[:, 2 * KC + c:2 * KC + c + 1], x[:, c, :], ALU.mult, ALU.add).then_inc(x1_ready, 1)

            norm_var(2, T, 1e-6)
            norm_divide(2, x, h, T)
            dve.wait_ge(in_late, 32)
            dve.wait_ge(lg_mm, 1)

            def per_token(v, n):
                return v.unsqueeze(2).broadcast_to([P, TC, n])

            def first_max(v, n, peak, eq, ids, least, onehot):
                nc.vector.tensor_reduce(peak, v, AX, ALU.max)
                dve.drain()
                tt(eq, v, per_token(peak, n), ALU.is_equal)
                dve.drain()
                stt(ids, eq, -float(P), iota[:, 0:n].unsqueeze(1).broadcast_to([P, TC, n]), ALU.mult, ALU.add)
                dve.drain()
                nc.vector.tensor_reduce(least, ids, AX, ALU.min)
                dve.drain()
                tt(onehot, ids, per_token(least, n), ALU.is_equal)
                dve.drain()

            tt(logits, PS[:, 1, 0:TC * 36].rearrange("p (t n) -> p t n", n=36),
               b_router.unsqueeze(1).broadcast_to([P, TC, 36]), ALU.add)
            dve.drain()
            first_max(logits[:, :, 0:4], 4, g_max, g_eq, g_id, g_idx, g_hot)
            tt(g_exp, logits[:, :, 0:4], per_token(g_max, 4), ALU.subtract).then_inc(exp_in, 1)
            tt(e_all, logits[:, :, 4:36].rearrange("p t (g e) -> p t g e", e=EPG),
               g_hot.unsqueeze(3).broadcast_to([P, TC, 4, EPG]), ALU.mult)
            dve.drain()
            nc.vector.tensor_reduce(e_in, e_all.rearrange("p t g e -> p t e g"), AX, ALU.add)
            dve.drain()
            first_max(e_in, EPG, top1, e_eq, e_id, e_idx, e_hot[:, 0, :, :])
            stt(e_left, e_hot[:, 0, :, :], -1e30, e_in, ALU.mult, ALU.add)
            dve.drain()
            first_max(e_left, EPG, top2, e_eq, e_id, e_idx, e_hot[:, 1, :, :])
            tt(e2, top2, top1, ALU.subtract).then_inc(exp_in, 1)
            for k in range(2):
                tt(hot[:, k, :, :].rearrange("p t (g e) -> p t g e", e=EPG),
                   g_hot.unsqueeze(3).broadcast_to([P, TC, 4, EPG]),
                   e_hot[:, k, :, :].unsqueeze(2).broadcast_to([P, TC, 4, EPG]), ALU.mult)
            dve.drain()
            tt(chosen, hot[:, 0, :, :], hot[:, 1, :, :], ALU.add).then_inc(chosen_ready, 1)
            dve.wait_ge(exp_out, 2)
            nc.vector.tensor_reduce(g_sum, g_exp, AX, ALU.add)
            dve.wait_ge(exp_out, 3)
            ts(e_sum, e2, 1.0, None, ALU.add)
            dve.drain()
            tt(g_sum, g_sum, e_sum, ALU.mult)
            dve.drain()
            nc.vector.reciprocal(gates[:, 0, :], g_sum)
            dve.drain()
            tt(gates[:, 1, :], gates[:, 0, :], e2, ALU.mult)
            nc.vector.memset(ones_e, 1.0)
            dve.wait_ge(rank_mm, 1)
            count = PS[:, 6, TC * EXPERTS:(TC + 1) * EXPERTS]
            ts(n_blk, count, 0.0, None, ALU.is_gt)
            for n in range(1, TC):
                dve.drain()
                stt(n_blk, count, float(n * P), n_blk, ALU.is_gt, ALU.add)
            dve.drain()
            nc.vector.tensor_tensor_scan(blk_end, ones_e, n_blk, 0.0, ALU.mult, ALU.add)
            dve.drain()
            tt(blk_start, blk_end, n_blk, ALU.subtract)
            dve.drain()
            stt(place, blk_start.unsqueeze(1).broadcast_to([P, TC, EXPERTS]), float(P),
                PS[:, 6, 0:TC * EXPERTS].rearrange("p (t e) -> p t e", e=EXPERTS), ALU.mult, ALU.add)
            dve.drain()
            for k in range(2):
                tt(hot[:, k, :, :], hot[:, k, :, :], place, ALU.mult)
            dve.drain()
            nc.vector.tensor_reduce(dest, hot, AX, ALU.add)
            dve.drain()
            nc.vector.tensor_copy(slot_part[:, 0, :, :], dest)
            ts(slot_of[:], dest, float(P), None, ALU.add)
            dve.drain()
            ts(slot_part[:, 1, :, :], slot_part[:, 0, :, :], 7, None, ALU.arith_shift_right)
            dve.drain()
            ts(slot_part[:, 0, :, :], slot_part[:, 0, :, :], P - 1, None, ALU.bitwise_and)
            dve.drain()
            stt(slot_at[:], slot_part[:, 0, :, :], float(BLOCKS), slot_part[:, 1, :, :], ALU.mult, ALU.add)
            tt(blk_cmp, blk_end.unsqueeze(1).broadcast_to([P, BLOCKS, EXPERTS]),
               iota[:, 0:BLOCKS].unsqueeze(2).broadcast_to([P, BLOCKS, EXPERTS]), ALU.is_le)
            ts(pair_cmp, iota[:, 0:BLOCKS // 2], 2.0, blk_end[:, EXPERTS - 1:EXPERTS], ALU.mult, ALU.is_lt)
            dve.drain()
            nc.vector.tensor_reduce(blk_exp, blk_cmp, AX, ALU.add)
            nc.vector.tensor_reduce(n_pairs, pair_cmp, AX, ALU.add)
            nc.vector.memset(yb[:, 1, :], 0.0)
            dve.drain()
            ts(route_i[:, 0:BLOCKS], blk_exp, float(EXPERTS - 1), None, ALU.min)
            nc.vector.tensor_copy(route_i[:, BLOCKS:BLOCKS + 1], n_pairs)
            dve.drain()
            dve.sem_inc(route_ready, 1)

            pairs = dve.value_load(route_i[0:1, BLOCKS:BLOCKS + 1], min_val=1, max_val=BLOCKS // 2)
            for freed in (hid_ready, y_ready):
                dve.sem_inc(freed, 1)

            def hidden(i, s):
                dve.wait_ge(silu_done, i * 2 + (s + 1))
                dve.wait_ge(up_mm, i * 2 + (s + 3))
                tt(hid[:, s, :], silu_b[:, s, :], PS[:, 3, :], ALU.mult).then_inc(hid_ready, 1)

            def result(i, s):
                dve.wait_ge(down_mm, i * 2 + (s + 3))
                dve.wait_ge(y_stored[s], i * 16 + 16)
                nc.vector.tensor_copy(yb[:, s, :].rearrange("p (a b) -> p a b", a=2), PS[:, 5:7, :]).then_inc(y_ready, 1)

            with dve.Fori(0, pairs) as i:
                hidden(i, 0)
                result(i, 0)
                hidden(i, 1)
                result(i, 1)
            dve.wait_ge(moe_done, 1)
            for t in range(TC):
                dve.wait_ge(y_loaded, 32 * TC)
                if t >= 2:
                    dve.wait_ge(yT_mm, t - 1)
                ts(y_of[:, 0, t, :], y_of[:, 0, t, :], gates[:, 0, t:t + 1], None, ALU.mult)
                dve.drain()
                stt(ysum[:, t % 2, :], y_of[:, 1, t, :], gates[:, 1, t:t + 1], y_of[:, 0, t, :], ALU.mult, ALU.add) \
                    .then_inc(ysum_ready, 1)
                dve.wait_ge(yT_mm, t + 1)
                for c in range(KC):
                    xc = x[:, c, t * P:(t + 1) * P]
                    last = stt(xc, PS[:, 2 * (t % 2) + c // 4, (c % 4) * P:(c % 4 + 1) * P],
                               mod1[:, 5 * KC + c:5 * KC + c + 1], xc, ALU.mult, ALU.add)
                last.then_inc(yT_used, 1)
            dve.drain()
            dve.sem_inc(x2_ready, 1)
            norm_var(3, T, 1e-6)
            norm_divide(3, x, x, T)

            norm_var(4, T, 1e-5)
            norm_divide(4, x, h, T)
            re, im = col("lam_re", 0, S5_TILES), col("lam_im", 0, S5_TILES)

            def step(op, *args):
                op(*args)
                dve.drain()

            dve.wait_ge(dt_exp, 1)
            step(tt, s5_a, re, s5_dt, ALU.mult)
            step(tt, s5_th, im, s5_dt, ALU.mult)
            step(ts, s5_th, s5_th, 0.5, None, ALU.mult)
            step(ts, s5_k, s5_th, 1.0 / (2 * np.pi), ROUND, ALU.mult, ALU.add)
            step(ts, s5_k, s5_k, -ROUND, None, ALU.add)
            step(stt, s5_r, s5_k, -TWO_PI_HI, s5_th, ALU.mult, ALU.add)
            step(stt, s5_r, s5_k, -TWO_PI_LO, s5_r, ALU.mult, ALU.add)
            step(ts, s5_r, s5_r, PI_BELOW, -PI_BELOW, ALU.min, ALU.max)
            step(ts, s5_t, s5_r, -1.0, None, ALU.mult)
            step(tt, s5_ab, s5_r, s5_t, ALU.max)
            ts(s5_ab, s5_ab, -1.0, np.pi / 2, ALU.mult, ALU.add).then_inc(angle_ready, 1)
            dve.wait_ge(trig_ready, 1)
            step(tt, s5_s2, half_sin, half_sin, ALU.mult)
            step(ts, cos1, s5_s2, -2.0, 1.0, ALU.mult, ALU.add)
            step(stt, sin1, half_sin, 2.0, half_cos, ALU.mult, ALU.mult)
            step(stt, num_re, radius, -1.0, cos1, ALU.add, ALU.mult)
            step(stt, num_re, s5_s2, -2.0, num_re, ALU.mult, ALU.add)
            step(tt, num_im, radius, sin1, ALU.mult)
            step(tt, s5_den, re, re, ALU.mult)
            step(tt, s5_t, im, im, ALU.mult)
            step(tt, s5_den, s5_den, s5_t, ALU.add)
            step(nc.vector.reciprocal, s5_den, s5_den)
            step(tt, f_re, num_re, re, ALU.mult)
            step(tt, s5_t, num_im, im, ALU.mult)
            step(tt, f_re, f_re, s5_t, ALU.add)
            step(tt, f_re, f_re, s5_den, ALU.mult)
            step(tt, f_im, num_im, re, ALU.mult)
            step(tt, s5_t, num_re, im, ALU.mult)
            step(tt, f_im, f_im, s5_t, ALU.subtract)
            step(tt, f_im, f_im, s5_den, ALU.mult)
            dve.wait_ge(in_late, 64)
            ctmp = [v[:, 0:8, :].rearrange("p a n -> p (a n)").rearrange("p (t n) -> p t n", n=HP) for v in turn_t]
            for n, (part, f) in enumerate(((0, f_re), (1, f_im), (0, f_im), (1, f_re))):
                tt(ctmp[n], s5_c[:, :, part, :], f.unsqueeze(2).broadcast_to([P, S5_TILES, HP]), ALU.mult)
            dve.drain()
            tt(s5_cf[:, :, 0, :], ctmp[0], ctmp[1], ALU.subtract)
            step(tt, s5_cf[:, :, 1, :], ctmp[2], ctmp[3], ALU.add)
            ts(s5_cf[:, :, 1, :], s5_cf[:, :, 1, :], -1.0, None, ALU.mult).then_inc(c_ready, 1)
            nc.vector.tensor_copy(turn[:, 0, :, 0:1], cos1.unsqueeze(2))
            nc.vector.tensor_copy(turn[:, 1, :, 0:1], sin1.unsqueeze(2))
            n = 1
            while n < S5_Q:
                dve.drain()
                by = [turn[:, r, :, n - 1:n].broadcast_to([P, S5_TILES, n]) for r in range(2)]
                for k, (part, f) in enumerate(((0, 0), (1, 1), (0, 1), (1, 0))):
                    tt(turn_t[k][:, :, 0:n], turn[:, part, :, 0:n], by[f], ALU.mult)
                dve.drain()
                tt(turn[:, 0, :, n:2 * n], turn_t[0][:, :, 0:n], turn_t[1][:, :, 0:n], ALU.subtract)
                tt(turn[:, 1, :, n:2 * n], turn_t[2][:, :, 0:n], turn_t[3][:, :, 0:n], ALU.add)
                n *= 2
            dve.drain()
            dve.sem_inc(bu_used, 4)
            dve.sem_inc(s5_used, 1)
            dve.wait_ge(u_evac, KC)

            def chunked(v):
                return v.rearrange("p (c t) -> p c t", t=S5_Q)

            with dve.Fori(0, KC) as q:
                def turns(a, r):
                    return turn[:, r, bass.ds(q * 4 + a, 1), :].broadcast_to([P, S5_NC, S5_Q])

                for a in range(4):
                    dve.wait_ge(bu_mm, q * 4 + (4 + a + 1))
                    bu = [chunked(PS[:, 2 * (a % 3) + r, :]) for r in range(2)]
                    t = [chunked(rot[:, a % 2, n, :]) for n in range(4)]
                    tt(t[0], bu[0], turns(a, 0), ALU.mult)
                    tt(t[1], bu[1], turns(a, 1), ALU.mult)
                    tt(t[2], bu[1], turns(a, 0), ALU.mult)
                    tt(t[3], bu[0], turns(a, 1), ALU.mult).then_inc(bu_used, 1)
                    dve.drain()
                    tt(chunked(scan_g[:, a, 0, :]), t[0], t[1], ALU.add)
                    tt(chunked(scan_g[:, a, 1, :]), t[2], t[3], ALU.subtract)
                dve.drain()
                for c in range(S5_NC):
                    for a in range(4):
                        for r in range(2):
                            g = scan_g[:, a, r, c * S5_Q:(c + 1) * S5_Q]
                            nc.vector.tensor_tensor_scan(g, radius[:, bass.ds(q * 4 + a, 1)].broadcast_to([P, S5_Q]), g,
                                                         carry[:, r, a:a + 1] if c else 0.0, ALU.mult, ALU.add)
                    dve.drain()
                    if c < S5_NC - 1:
                        ends = [scan_g[:, :, r, (c + 1) * S5_Q - 1] for r in range(2)]
                        by = [turn[:, r, bass.ds(q * 4, 4), S5_Q - 1] for r in range(2)]
                        for k, (part, f) in enumerate(((0, 0), (1, 1), (0, 1), (1, 0))):
                            tt(carry_t[:, k, :], ends[part], by[f], ALU.mult)
                        dve.drain()
                        tt(carry[:, 0, :], carry_t[:, 0, :], carry_t[:, 1, :], ALU.subtract)
                        tt(carry[:, 1, :], carry_t[:, 2, :], carry_t[:, 3, :], ALU.add)
                        dve.drain()
                dve.wait_ge(s5_mm, q + 1)
                for a in range(4):
                    g = [chunked(scan_g[:, a, r, :]) for r in range(2)]
                    t = [chunked(rot[:, a % 2, n, :]) for n in range(4)]
                    tt(t[0], g[0], turns(a, 0), ALU.mult)
                    tt(t[1], g[1], turns(a, 1), ALU.mult)
                    tt(t[2], g[0], turns(a, 1), ALU.mult)
                    tt(t[3], g[1], turns(a, 0), ALU.mult)
                    dve.drain()
                    tt(chunked(scan_h[:, a, 0, :]), t[0], t[1], ALU.subtract)
                    tt(chunked(scan_h[:, a, 1, :]), t[2], t[3], ALU.add).then_inc(state_ready, 1)
                dve.wait_ge(s5_mm, q + 2)
                stt(h[:, bass.ds(q, 1), :], uT[:, bass.ds(q, 1), :], cols[:, bass.ds(q + COLS["s5_d"][0], 1)],
                    PS[:, 6:7, :], ALU.mult, ALU.add).then_inc(s5_used, 1)
            for n in range(KC):
                dve.wait_ge(gate_sig, n + 1)
                stt(glu_t[:, n % 2, :], PS[:, n % 4, :], col("b_glu", n), glu_gate[:, n % 2, :], ALU.add, ALU.mult)
                dve.drain()
                stt(x[:, n, :], glu_t[:, n % 2, :], mod2[:, 0, 2 * KC + n:2 * KC + n + 1], x[:, n, :], ALU.mult, ALU.add) \
                    .then_inc(glu_used, 1)

            def mlp(layer, k_norm):
                norm_var(k_norm, T, 1e-5)
                norm_divide(k_norm, x, h, T)
                if layer == 0:
                    dve.sem_inc(relu_done, 8)
                with dve.Fori(0, 4) as i:
                    for k in range(8):
                        dve.wait_ge(mlp1_mm, i * 8 + (32 * layer + k + 1))
                        ts(mlp_h[:, bass.ds(i * 8 + k, 1), :], PS[:, k:k + 1, :], 0.0, None, ALU.max).then_inc(relu_done, 1)
                if layer == 0:
                    modulation((0, ADA_TILES // 2), 2 * ADA_TILES, cond2[:], col("ada_b1", 0, 48), mod2[:, 1, :], ada_buf1)
                    dve.drain()
                    norm_gain(5, mod2[:, 1, KC:2 * KC], "nmix1")
                    norm_gain(6, mod2[:, 1, 4 * KC:5 * KC], "nmlp1")
                for n in range(KC):
                    dve.wait_ge(mlp2_mm, KC * layer + n + 1)
                    stt(x[:, n, :], PS[:, n, :], mod2[:, layer, 5 * KC + n:5 * KC + n + 1], x[:, n, :], ALU.mult, ALU.add) \
                        .then_inc(mlp_added, 1)

            mlp(0, 5)

            norm_var(6, T, 1e-5)
            norm_divide(6, x, h, T)
            dve.sem_inc(conv_done, 8)
            with dve.Fori(0, 3) as i:
                def tap(n, k):
                    return cols[:, bass.ds(i * 8 + (COLS["conv_w"][0] + M2_CC * n + k), 1)]

                for k in range(8):
                    dve.wait_ge(xbc_mm, i * 8 + (k + 1))
                    ts(xs[:, bass.ds(i * 8 + k, 1), :], PS[:, k:k + 1, :], tap(3, k), None, ALU.mult)
                    for back in range(1, 4):
                        dve.drain()
                        late = xs[:, bass.ds(i * 8 + k, 1), back:T]
                        last = stt(late, PS[:, k:k + 1, 0:T - back], tap(3 - back, k), late, ALU.mult, ALU.add)
                    last.then_inc(conv_done, 1)
            dve.wait_ge(dt_mm, 1)
            ts(dt_raw, PS[0:M2_HEADS, 0, :], col("dt_bias")[0:M2_HEADS, :], None, ALU.add).then_inc(step_dve, 1)
            nc.vector.memset(state, 0.0)
            nc.vector.memset(z_silu[0:M2_HEADS, 0, :], 1.0)
            dve.wait_ge(step_act, 1)
            step(stt, dt_t, dt_raw, 0.0, dt_abs, ALU.max, ALU.add)
            step(ts, a_dt, dt_t, a_pos, -1.0, ALU.mult, ALU.mult)
            for c in range(M2_NC):
                at = slice(c * M2_Q, (c + 1) * M2_Q)
                nc.vector.tensor_tensor_scan(a_cs[:, at], z_silu[0:M2_HEADS, 0, at], a_dt[:, at], 0.0, ALU.mult, ALU.add)
            dve.drain()
            for c in range(M2_NC):
                last = ts(last_diag[:, c, :], eye[0:M2_HEADS, 0:M2_HEADS], a_cs[:, (c + 1) * M2_Q - 1:(c + 1) * M2_Q], None,
                          ALU.mult)
            last.then_inc(step_dve, 1)
            dve.wait_ge(tok_mm, 1)
            by_token = PS[:, 1, 0:2 * M2_NC * M2_HEADS].rearrange("p (n c h) -> p n c h", c=M2_NC, h=M2_HEADS)
            nc.vector.tensor_copy(dt_tok, by_token[:, 0, :, :])
            step(nc.vector.tensor_copy, cs_tok, by_token[:, 1, :, :])
            tt(dec_tok, PS[:, 2, 0:M2_NC * M2_HEADS].rearrange("p (c h) -> p c h", h=M2_HEADS), cs_tok, ALU.subtract) \
                .then_inc(step_dve, 1)
            dve.wait_ge(step_act, 2)
            dve.sem_inc(c_dec_ready, 2)
            dve.sem_inc(y_added, 1)
            dve.sem_inc(state_new, 1)
            with dve.Fori(0, M2_NC) as c:
                def heads(v, first, count):
                    return v[:, bass.ds(c, 1), first:first + count].rearrange("p c h -> p (c h)")

                for b in range(4):
                    dve.wait_ge(xs_tok_mm, c * 4 + (b + 1))
                    tt(xdt[:, b * 512:(b + 1) * 512].rearrange("p (h n) -> p h n", n=64),
                       PS[:, b, :].rearrange("p (h n) -> p h n", n=64),
                       heads(dt_tok, 8 * b, 8).unsqueeze(2).broadcast_to([P, 8, 64]), ALU.mult).then_inc(xdt_ready, 1)
                dve.wait_ge(cb_mm, c + 1)
                tt(cb, PS[:, 5, :].rearrange("p (g n) -> p g n", n=P), causal.unsqueeze(1).broadcast_to([P, M2_G, P]), ALU.mult)
                dve.drain()

                def differences(q):
                    dve.wait_ge(exp_cs_ready, c * 8 + (q + 1))
                    for k in range(4):
                        last = ts(decay[:, q % 2, k, :], PS[:, 6, k * P:(k + 1) * P], heads(cs_tok, 4 * q + k, 1), 0.0,
                                  ALU.subtract, ALU.min)
                    last.then_inc(diff_ready, 1)

                def add_y(q):
                    dve.wait_ge(y_turned, c * 8 + (q + 3))
                    for j in range(2):
                        n = 2 * q + j
                        xc = xs[:, n, bass.ds(c * M2_Q, M2_Q)]
                        last = stt(xc, xc, col("m2_d", n), PS[:, 4, j * P:(j + 1) * P], ALU.mult, ALU.add)
                    last.then_inc(y_added, 1)

                differences(0)
                tt(xdt_dec.rearrange("p (h n) -> p h n", n=64), xdt.rearrange("p (h n) -> p h n", n=64),
                   heads(dec_tok, 0, M2_HEADS).unsqueeze(2).broadcast_to([P, M2_HEADS, 64]), ALU.mult).then_inc(xdt_dec_ready, 1)
                for q in range(8):
                    if q < 7:
                        differences(q + 1)
                    dve.wait_ge(y7_mm, c * 8 + (q + 1))
                    dve.wait_ge(decay_ready, c * 8 + (q + 1))
                    tt(m_now[:, q % 2, :, :], decay[:, q % 2, :, :], cb[:, q // 2:q // 2 + 1, :].broadcast_to([P, 4, P]),
                       ALU.mult).then_inc(m_ready, 1)
                    tt(c_dec[:, q % 2, :, :], exp_cs[:, q % 2, :, :],
                       xs_now[:, M2_XC + M2_G + q // 2:M2_XC + M2_G + q // 2 + 1, :].broadcast_to([P, 4, P]), ALU.mult) \
                        .then_inc(c_dec_ready, 1)
                    if q:
                        add_y(q - 1)
                add_y(7)
                dve.wait_ge(st_mm, c + 1)
                tt(state.rearrange("p (h n) -> p h n", n=64), state.rearrange("p (h n) -> p h n", n=64),
                   heads(dec_chunk, 0, M2_HEADS).unsqueeze(2).broadcast_to([P, M2_HEADS, 64]), ALU.mult)
                dve.drain()
                for g in range(M2_G):
                    part = state[:, g * 512:(g + 1) * 512]
                    last = tt(part, part, PS[:, g, :], ALU.add)
                last.then_inc(state_new, 1)
            dve.drain()
            dve.sem_inc(z_used, 2)
            with dve.Fori(0, 2) as i:
                for k in range(8):
                    dve.wait_ge(z_ready, i * 8 + (8 + k + 1))
                    chunk = xs[:, bass.ds(i * 8 + k, 1), :]
                    tt(chunk, chunk, z_silu[:, k % 2:k % 2 + 1, :], ALU.mult).then_inc(z_used, 1)
            for g in range(M2_G):
                dve.wait_ge(oms_done, HEADS + g + 1)
                ts(var, PS[:, g, :], 1.0 / 512, 1e-5, ALU.mult, ALU.add).then_inc(ovar_ready, 1)
                dve.wait_ge(ostd_ready, HEADS + g + 1)
                nc.vector.reciprocal(rstd, rstd)
                dve.drain()
                for j in range(4):
                    n = 4 * g + j
                    last = stt(xs[:, n, :], xs[:, n, :], col("m2_norm", n), rstd, ALU.mult, ALU.mult)
                    last.then_inc(yn_ready, 1)
            for n in range(KC):
                dve.wait_ge(proj_mm, 2 * KC + n + 1)
                stt(x[:, n, :], PS[:, n, :], mod2[:, 1, 2 * KC + n:2 * KC + n + 1], x[:, n, :], ALU.mult, ALU.add) \
                    .then_inc(x5_ready, 1)
            mlp(1, 7)
            norm_var(8, T, 1e-5)
            norm_divide(8, x, x, T)


def _constants():
    f = np.float32
    p = np.arange(P)
    rot = np.zeros((P, P), f)
    for m in range(P):
        rot[m + 16 if m % 32 < 16 else m - 16, m] = -1.0 if m % 32 < 16 else 1.0
    mats = np.stack([np.eye(P, dtype=f), (p[:, None] < p[None, :]).astype(f), (p[:, None] <= p[None, :]).astype(f), rot], 1)
    t = np.arange(T)
    pos = np.stack([t // 64, t % 64], -1).astype(f)
    axis = DH // 2
    freq = (f(10000.0) ** (-np.arange(0, axis, 2, dtype=f) / f(axis))).astype(f)
    ang = (pos[:, :, None] * freq).astype(f)
    ang = np.concatenate([ang, ang], -1).reshape(T, DH)
    ang = np.concatenate([ang, ang], -1).T
    tt = 2 * np.pi * ((t[:, None] * t[None, :]) % T) / T
    cc = 2 * np.pi * ((p[:, None] * p[None, :]) % P) / P
    ortho = 1.0 / np.sqrt(T * P)

    def token_rows(a):
        return np.ascontiguousarray(a.astype(f).reshape(TC, P, T).transpose(1, 0, 2))

    return {
        "mats": mats, "rope_c": np.cos(ang).astype(f), "rope_s": np.sin(ang).astype(f),
        "dft_c": token_rows(np.cos(tt) * ortho), "dft_s": token_rows(-np.sin(tt) * ortho),
        "dft_ch": np.concatenate([np.cos(cc), np.sin(cc)], 1).astype(f),
        "iota": np.tile(np.arange(64, dtype=f), (P, 1)),
        "tokid": (p[:, None] + P * np.arange(TC)[None, :]).astype(np.uint32),
    }


def _layout(a):
    def chunks(v):
        return np.asarray(v).reshape(-1, P).T

    def features(m):
        m = np.asarray(m)
        return m.T.reshape(-1, P, m.shape[0]).transpose(1, 0, 2)

    def rows(w):
        return np.asarray(w).reshape(-1, P, w.shape[-1]).transpose(1, 0, 2)

    def padded(v):
        return np.concatenate([np.asarray(v), np.zeros(P - len(v), np.float32)])[:, None]

    def states(v):
        return np.asarray(v).reshape(S5_TILES, P).T

    packed = {
        "b_ada": chunks(a["b_ada"][0]), "ada_b0": chunks(a["ada_b_2"][0]), "ada_b1": chunks(a["ada_b_2"][1]),
        "g_mix": chunks(a["g_mix_norm"][0]), "g_ffn": chunks(a["g_ffn_norm"][0]), "g_final": chunks(a["g_final"]),
        "g_subln": chunks(a["g_subln"][0]), "nmix0": chunks(a["norm_mix_g_2"][0]), "nmix1": chunks(a["norm_mix_g_2"][1]),
        "nmlp0": chunks(a["norm_mlp_g_2"][0]), "nmlp1": chunks(a["norm_mlp_g_2"][1]), "s5_d": chunks(a["s5_d_2"][0]),
        "b_glu": chunks(a["s5_b_glu_2"][0]),
        "conv_w": np.concatenate([chunks(a["m2_conv_w_2"][0][k]) for k in range(4)], 1),
        "conv_b": chunks(a["m2_conv_b_2"][0]), "m2_d": chunks(np.repeat(np.asarray(a["m2_d_2"][0]), 64)),
        "m2_norm": chunks(a["m2_norm_g_2"][0]), "fin": chunks(a["final_norm_g_2"]),
        "dt_bias": padded(a["m2_dt_bias_2"][0]), "a_log": padded(a["m2_a_log_2"][0]),
        "lam_re": states(a["s5_lambda_re_2"][0]), "lam_im": states(a["s5_lambda_im_2"][0]),
        "log_dt": states(np.repeat(np.asarray(a["s5_log_dt_2"][0])[:, None], 64, 1)),
    }
    s5_b = np.zeros((4, 2, HP, 8, 2, 2, 64), np.float32)
    s5_c = np.empty((2, 64, S5_TILES, 2, HP), np.float32)
    for r, (bname, cname) in enumerate((("s5_b_re_2", "s5_c_re_2"), ("s5_b_im_2", "s5_c_im_2"))):
        b = np.asarray(a[bname][0]).reshape(8, 4, 2, 64, HP)
        for g in range(2):
            s5_b[:, g, :, :, r, g, :] = b[:, :, g].transpose(1, 3, 0, 2)
        s5_c[:, :, :, r, :] = np.asarray(a[cname][0]).reshape(S5_TILES, 2, HP, 64).transpose(1, 3, 0, 2)
    m2_in = np.asarray(a["m2_w_in_2"][0])
    lams = np.stack([a[n][0] for n in ("lambda_q1", "lambda_k1", "lambda_q2", "lambda_k2")])
    return {
        "xT": features(a["x"][0]), "ctxT": features(a["ctx"][0]),
        "c_rows": np.stack([a["c"][0], a["c_ctx"], a["c_2"][0]]),
        "cols": np.concatenate([packed[n] for n in COLS], 1),
        "lam4": np.tile(lams[None], (P, 1, 1)),
        "w_adaT": np.asarray(a["w_ada"][0]).T, "ada_w_2T": np.asarray(a["ada_w_2"]).transpose(0, 2, 1),
        "w_in": a["w_in"][0], "w_out": a["w_out"][0],
        "wfour": np.asarray(a["w_fourier"][0]).transpose(1, 0, 2),
        "w_router": rows(np.concatenate([a["w_router_group"][0], a["w_router_expert"][0]], 1)),
        "b_router": np.tile(np.concatenate([a["b_router_group"][0], a["b_router_expert"][0]])[None], (P, 1)),
        "w_gate": a["w_gate"][0], "w_up": a["w_up"][0], "w_down": a["w_down"][0],
        "s5_w_in": a["s5_w_in_2"][0], "s5_b": s5_b.reshape(P, 8, 2, P), "s5_c": s5_c.reshape(P, S5_TILES, 2, HP),
        "w_glu": a["s5_w_glu_2"][0], "mlp_w1": a["mlp_w1_2"], "mlp_w2": a["mlp_w2_2"],
        "m2_w_in": m2_in, "m2_w_dt": rows(m2_in[:, M2_IN + M2_XBC:]), "m2_w_out": a["m2_w_out_2"][0],
    }


def kernel(**inputs):
    import concourse.bacc as bacc
    from concourse.bass_utils import run_bass_kernel_spmd

    nc = bacc.Bacc("TRN2", target_bir_lowering=False, num_devices=1)
    arrays = {name: np.ascontiguousarray(v) for name, v in {**_layout(inputs), **_constants()}.items()}
    handles = {name: nc.dram_tensor(f"in_{name}", v.shape, mybir.dt.from_np(v.dtype), kind="ExternalInput").ap()
               for name, v in arrays.items()}
    out = nc.dram_tensor("outT", [P, KC, T], F32, kind="ExternalOutput").ap()
    build(nc, handles, out)
    r = run_bass_kernel_spmd(nc, [{f"in_{name}": v for name, v in arrays.items()}], core_ids=[0])
    got = np.asarray(r.results[0]["outT"])
    return got.transpose(2, 1, 0).reshape(1, T, D)
```

```python
from contextlib import ExitStack

import numpy as np

import concourse.bass as bass
from concourse import mybir

F32 = mybir.dt.float32
F32R = mybir.dt.float32r
BF16 = mybir.dt.bfloat16
I32 = mybir.dt.int32
U32 = mybir.dt.uint32
ALU = mybir.AluOpType
ACT = mybir.ActivationFunctionType
AX = mybir.AxisListType.X

P = 128
D = 1024
KC = D // P
T = 512
TC = T // P
CTX = 256
KEYS = CTX + T
KCH = KEYS // P
HEADS = 4
DH = 64
GROUPS = 4
EPG = 8
EXPERTS = GROUPS * EPG
DE = 512
BLOCKS = T * 2 // P + EXPERTS
NMOD = 6
TN = 512
ADA_TILES = NMOD * KC // 4
DFF = 4096
LAMBDA_INIT = 0.8 - 0.6 * 1.0
S5_TILES = 32
S5_Q = 128
S5_NC = T // S5_Q
ROUND = 1.5 * 2.0 ** 23
TWO_PI_HI = 6.28125
TWO_PI_LO = 2 * np.pi - TWO_PI_HI
PI_BELOW = 3.1415925
HP = 16
M2_IN = 2048
M2_XBC = 3072
M2_HEADS = 32
M2_XC = M2_IN // P
M2_CC = M2_XBC // P
M2_G = 4
M2_Q = 128
M2_NC = T // M2_Q
SUM_BANKS = (6, 0, 1, 2, 3)

COLS = {}
for _name, _count in (
    ("b_ada", 48), ("ada_b0", 48), ("ada_b1", 48), ("g_mix", 8), ("g_ffn", 8), ("g_final", 8), ("g_subln", 1),
    ("nmix0", 8), ("nmix1", 8), ("nmlp0", 8), ("nmlp1", 8), ("s5_d", 8), ("b_glu", 16), ("conv_w", 96),
    ("conv_b", 24), ("m2_d", 16), ("m2_norm", 16), ("fin", 8), ("dt_bias", 1), ("a_log", 1),
    ("lam_re", 32), ("lam_im", 32), ("log_dt", 32),
):
    COLS[_name] = (sum(n for _, n in COLS.values()), _count)
NCOLS = sum(n for _, n in COLS.values())


def build(nc, A, out):
    with ExitStack() as ctx:
        def sb(name, shape, dt=F32):
            return ctx.enter_context(nc.sbuf_tensor(name, shape, dt))

        TWIN = KC * T

        def sb_twice(name, shape):
            at, n = -(-nc.sbuf_base // 32) * 32, int(np.prod(shape[1:]))
            return sb(name, shape), [nc.alloc_sbuf_tensor_at(f"{name}_f32r{k}", [P, TWIN], F32R, offset=at + 4 * k * TWIN)
                                     for k in range(n // TWIN)]

        def sem(name):
            return ctx.enter_context(nc.semaphore(name))

        PS = ctx.enter_context(nc.psum_tensor("PS", [P, 8, 512], F32))
        ring, ring_r = sb_twice("ring", [P, 2, KC, TN])
        work, work_r = sb_twice("work", [P, 32768])
        x = sb("x", [P, KC, T])
        h, h_r = sb_twice("h", [P, KC, T])
        cols = sb("cols_sb", [P, NCOLS])
        cond2 = sb("cond2", [P, D])
        mats = sb("mats_sb", [P, 4, P])
        ones = sb("ones", [P, P])
        mod1 = sb("mod1", [P, NMOD * KC])
        modc = sb("modc", [P, 2 * KC])
        mod2 = sb("mod2", [P, 2, NMOD * KC])
        gain = sb("gain", [P, 7, KC])
        norm_buf = sb("norm_buf", [P, 2 * T])
        var, rstd = norm_buf[:, 0:T], norm_buf[:, T:2 * T]
        iota = sb("iota_sb", [P, 64])
        tokid = sb("tokid_sb", [P, TC], U32)
        route_i = sb("route_i", [P, 64], I32)
        slot_of = sb("slot_of", [P, 2, TC], I32)
        gates = sb("gates", [P, 2, TC])
        eye, tri, causal, rope_rot = (mats[:, n, :] for n in range(4))

        def wk(at, *shape):
            n = int(np.prod(shape))
            v = work[:, at:at + n]
            if len(shape) == 2:
                return v.rearrange("p (a b) -> p a b", b=shape[1])
            if len(shape) == 3:
                return v.rearrange("p (a b c) -> p a b c", b=shape[1], c=shape[2])
            return v

        def col(name, n=0, count=1):
            first = COLS[name][0] + n
            return cols[:, first:first + count]

        qT, kT, vtok, fT, cx = wk(0, 4, T), wk(2048, 4, KEYS), wk(5120, KCH, 512), wk(8192, 4, T), wk(10240, KC, CTX)
        rope_c, rope_s = wk(12288, T), wk(12800, T)
        dft_c, dft_s, dft_ch = wk(13312, TC, T), wk(15360, TC, T), wk(17408, 256)
        fab, fre = wk(17664, 2, 4, 256), wk(19712, T)
        attn_a, attn_t = wk(20224, 2, KEYS), wk(21760, KEYS)
        aT, oT, oSq = wk(22528, KCH, T), wk(25600, T), wk(26112, T)
        rope_t = wk(26624, 2, 2, T)
        probs = wk(28672, 2, 2, KEYS)
        ada_buf = [wk(20224, 4, D), wk(24320, 4, D)]
        cond1 = wk(28672, 2, D)
        lam_t = wk(30720, 2, 64)
        wfour = wk(31744, GROUPS, P)
        lam4 = wk(32256, 4, 64)
        csq = wk(0, KC, CTX)
        sm = sb("sm", [P, 64])
        rowmax, negmax, rowsum, rsum, rneg = (sm[:, 4 * n:4 * n + 4].rearrange("p (a b) -> p a b", b=2) for n in range(5))
        lam_d, neglam = sm[:, 24:28], sm[:, 28:29]
        gsub = sm[:, 29:30]

        expert_w = [(ring[:, 0, :, :], ring[:, 1, :, :], wk(0, 4, D)),
                    (wk(4096, KC, DE), wk(8192, KC, DE), wk(12288, 4, D))]
        xb, xbT, silu_b = wk(16384, 2, D), wk(18432, 2, KC, P), wk(20480, 2, DE)
        hid, hidT, yb = wk(21504, 2, DE), wk(22528, 2, 4, P), wk(23552, 2, D)
        hrow = wk(25600, 2, D)
        y_of = wk(0, 2, TC, D)
        ysum = wk(16384, 2, D)
        routing_at = [27648]

        def rt(*shape):
            n = int(np.prod(shape))
            routing_at[0] += n
            return wk(routing_at[0] - n, *shape)

        w_router, b_router = rt(KC, GROUPS + EXPERTS), rt(GROUPS + EXPERTS)
        logits, g_exp, g_eq, g_id, g_hot = rt(TC, GROUPS + EXPERTS), rt(TC, 4), rt(TC, 4), rt(TC, 4), rt(TC, 4)
        e_all, e_in, e_eq, e_id, e_hot = rt(TC, 4, EPG), rt(TC, EPG), rt(TC, EPG), rt(TC, EPG), rt(2, TC, EPG)
        e_left, hot, chosen = rt(TC, EPG), rt(2, TC, EXPERTS), rt(TC, EXPERTS)
        place, n_blk, blk_end, blk_start, ones_e = (rt(TC, EXPERTS), rt(EXPERTS), rt(EXPERTS), rt(EXPERTS), rt(EXPERTS))
        blk_cmp, blk_exp, pair_cmp, n_pairs = rt(BLOCKS, EXPERTS), rt(BLOCKS), rt(BLOCKS // 2), rt(1)
        g_max, g_sum, g_idx, top1, top2, e_idx = (rt(TC) for _ in range(6))
        e2, e_sum, dest = rt(TC), rt(TC), rt(2, TC)
        assert routing_at[0] <= 32768
        idx_all = sb("idx_all", [P, BLOCKS], U32)
        idx = [sb(f"idx{s}", [P, 1], U32) for s in range(2)]
        slot_at = sb("slot_at", [P, 2, TC], U32)
        slot_part = sb("slot_part", [P, 2, 2, TC], I32)
        zeros = sb("zeros", [P, 256])
        h_rows = nc.dram_tensor("h_rows", [T + 1, D], F32, kind="Internal").ap()
        slot_tok = nc.dram_tensor("slot_tok", [P * BLOCKS, 1], U32, kind="Internal").ap()
        y_rows = nc.dram_tensor("y_rows", [(BLOCKS + 2) * P, D], F32, kind="Internal").ap()

        turn = wk(0, 2, S5_TILES, S5_Q)
        uT, s5_b, s5_c, s5_cf = wk(8192, KC, T), wk(12288, KC, 2, P), wk(14336, S5_TILES, 2, HP), wk(15360, S5_TILES, 2, HP)
        scan_g, rot, turned = wk(16384, S5_NC, 8, S5_Q), wk(20480, 2, 4, T), wk(24576, 2, 4, T)
        turn_t = [wk(16384 + 2048 * n, S5_TILES, 64) for n in range(4)]
        u_now, b_now, c_now = wk(28672, T), wk(29184, 2, P), wk(29440, 4, 288)
        s5_at = [30592]

        def s5p():
            s5_at[0] += S5_TILES
            return wk(s5_at[0] - S5_TILES, S5_TILES)

        (s5_dt, s5_a, s5_th, s5_k, s5_r, s5_ab, radius, half_sin, half_cos, s5_s2, cos1, sin1, num_re, num_im, f_re, f_im,
         s5_den, s5_t) = (s5p() for _ in range(18))
        carry, carry_t = wk(s5_at[0], 4, 2), wk(s5_at[0] + 8, 4, 4)
        carry_by = wk(s5_at[0] + 32, 2, S5_TILES)
        decay_now = wk(s5_at[0] + 96, 4, 2, S5_Q)
        glu_gate, glu_t = wk(0, 2, T), wk(1024, 2, T)
        ring_hi = wk(20480, 2, KC, TN)
        glu_lo = wk(8192, KC, T)
        mlp_hi, mlp_lo, mlp_h_lo = wk(0, KC, T), wk(4096, KC, T), wk(8192, KC, T)
        ada_buf1 = [wk(12288, 3, D), wk(15360, 3, D)]
        xs, xs_now = wk(0, M2_CC, T), wk(12288, M2_CC, P)
        xdt, xdt_dec, state, b_tok = wk(15360, M2_IN), wk(17408, M2_IN), wk(19456, M2_IN), wk(21504, M2_G, P)
        decay, m_now = wk(22528, 2, 4, P), wk(23552, 2, 4, P)
        y_off, y_tok = wk(24576, M2_IN), wk(26624, 2, 2 * P)
        dt_t, a_dt, a_cs, dt_raw, dt_abs = (wk(27136 + 512 * n, T)[0:M2_HEADS, :] for n in range(5))
        cs_neg, dt_tok, dec_tok, dec_chunk = (wk(29696 + 128 * n, M2_NC, M2_HEADS) for n in range(4))
        last_diag = wk(30208, M2_NC, M2_HEADS)[0:M2_HEADS, :, :]
        w_dt = wk(30336, KC, M2_HEADS)
        z_silu = wk(30592, 2, T)
        a_pos, sums_now = wk(31616, 1)[0:M2_HEADS, :], wk(31620, M2_Q)[0:M2_HEADS, :]
        xbc_h_lo, z_h_hi = wk(12288, KC, T), wk(12288, KC, T)
        exp_cs_tok = wk(31752, M2_NC, M2_HEADS)
        eye16, mask16 = wk(31880, 64).bitcast(BF16), wk(31944, 64).bitcast(BF16)
        m2_sq, y_lo = wk(12288, M2_XC, T), wk(12288, M2_XC, T)

        twins = {"ring": ring_r, "work": work_r, "h": h_r}

        def f32r(v):
            return bass.AP(twins[v.tensor.name][v.offset // TWIN], v.offset % TWIN, [(TWIN, P), *v.ap[1:]])

        def chunked(v):
            return v.rearrange("p (c t) -> p c t", t=S5_Q)

        in_cond, in_small, in_x, in_mix, in_late = (sem(n) for n in ("in_cond", "in_small", "in_x", "in_mix", "in_late"))
        tile_loaded = [sem(f"tile_loaded{n}") for n in range(4)]
        tile_used = sem("tile_used")
        w_hi, w_split, lo_ready = sem("w_hi"), sem("w_split"), sem("lo_ready")
        ada_loaded, ada_used = [sem("ada_loaded0"), sem("ada_loaded1")], sem("ada_used")
        consts_set, cond_ready, mods_ready = sem("consts_set"), sem("cond_ready"), sem("mods_ready")
        sq_ready, ms_done, var_ready, std_ready = sem("sq_ready"), sem("ms_done"), sem("var_ready"), sem("std_ready")
        xn_ready, h_ready = sem("xn_ready"), sem("h_ready")
        exp_in, exp_out = sem("exp_in"), sem("exp_out")
        proj_mm = sem("proj_mm")
        qkv_mm, qkv_evac, rope_mm, rope_done = sem("qkv_mm"), sem("qkv_evac"), sem("rope_mm"), sem("rope_done")
        ab_mm, ab_evac, fr_mm, fr_evac = sem("ab_mm"), sem("ab_evac"), sem("fr_mm"), sem("fr_evac")
        fo_mm, fo_evac = sem("fo_mm"), sem("fo_evac")
        score_mm, negmax_ready, exp_done, a_ready = sem("score_mm"), sem("negmax_ready"), sem("exp_done"), sem("a_ready")
        at_mm, at_evac, pv_mm, o_ready = sem("at_mm"), sem("at_evac"), sem("pv_mm"), sem("o_ready")
        osq_ready, oms_done, ovar_ready, ostd_ready = sem("osq_ready"), sem("oms_done"), sem("ovar_ready"), sem("ostd_ready")
        head_done, x1_ready, out_stored = sem("head_done"), sem("x1_ready"), sem("out_stored")
        idx_filled, zero_row, lg_mm = sem("idx_filled"), sem("zero_row"), sem("lg_mm")
        hrow_mm, hrow_evac, hrow_stored = sem("hrow_mm"), sem("hrow_evac"), [sem("hrow_stored0"), sem("hrow_stored1")]
        chosen_ready, rank_mm, route_ready = sem("chosen_ready"), sem("rank_mm"), sem("route_ready")
        idx_set, idx_stored, idx_loaded = sem("idx_set"), sem("idx_stored"), sem("idx_loaded")
        gate_loaded, up_loaded, down_loaded, xb_loaded, y_stored = (
            [sem(f"{n}{s}") for s in range(2)] for n in ("gate_loaded", "up_loaded", "down_loaded", "xb_loaded", "y_stored"))
        xT_mm, xT_evac, gate_mm, up_mm, silu_done = sem("xT_mm"), sem("xT_evac"), sem("gate_mm"), sem("up_mm"), sem("silu_done")
        hid_ready, hT_mm, hT_evac, down_mm, y_ready = sem("hid_ready"), sem("hT_mm"), sem("hT_evac"), sem("down_mm"), sem("y_ready")
        moe_done, y_loaded, ysum_ready, yT_mm, yT_used = sem("moe_done"), sem("y_loaded"), sem("ysum_ready"), sem("yT_mm"), sem("yT_used")
        y_zeroed, x2_ready = sem("y_zeroed"), sem("x2_ready")
        u_evac, dt_exp, angle_ready, trig_ready = (sem(n) for n in ("u_evac", "dt_exp", "angle_ready", "trig_ready"))
        c_zero, c_ready, ub_staged, c_staged = (sem(n) for n in ("c_zero", "c_ready", "ub_staged", "c_staged"))
        bu_mm, bu_used, state_ready, s5_mm, s5_used, gelu_done = (
            sem(n) for n in ("bu_mm", "bu_used", "state_ready", "s5_mm", "s5_used", "gelu_done"))
        g_added, decay_set = sem("g_added"), sem("decay_set")
        glu_mm, gate_sig, glu_used = sem("glu_mm"), sem("gate_sig"), sem("glu_used")
        mlp1_mm, relu_done, sqr_done, mlp_split, mlp2_mm, mlp_added = (
            sem(n) for n in ("mlp1_mm", "relu_done", "sqr_done", "mlp_split", "mlp2_mm", "mlp_added"))
        xbc_mm, conv_done, xs_ready, dt_mm, tok_mm = (sem(n) for n in ("xbc_mm", "conv_done", "xs_ready", "dt_mm", "tok_mm"))
        step_dve = sem("step_dve")
        step_act = sem("step_act")
        ssd_staged, xs_tok_mm, xdt_ready, xdt_dec_ready, b_tok_mm, b_tok_evac, cb_mm = (
            sem(n) for n in ("ssd_staged", "xs_tok_mm", "xdt_ready", "xdt_dec_ready", "b_tok_mm", "b_tok_evac", "cb_mm"))
        cs_mm, decay_ready, m_ready, off_mm, off_used = (sem(n) for n in ("cs_mm", "decay_ready", "m_ready", "off_mm", "off_used"))
        y7_mm, y_tok_evac, y_turned, y_added, st_mm, state_new = (
            sem(n) for n in ("y7_mm", "y_tok_evac", "y_turned", "y_added", "st_mm", "state_new"))
        z_mm, z_ready, z_used, yn_ready, x5_ready = (sem(n) for n in ("z_mm", "z_ready", "z_used", "yn_ready", "x5_ready"))
        y_hi_ready = sem("y_hi_ready")

        PAIRS, SPLITS, LOWS = {}, {}, {}
        for name, n in (("in", 2), ("out", 1), ("s5_in", 1), ("glu", 2), ("mlp0", 8), ("xbc", 3), ("z", 2), ("m2_out", 2),
                        ("mlp1", 8)):
            PAIRS[name] = (sum(m for _, m in PAIRS.values()), n)
        for name, n in (("glu", KC), ("mlp0", KC), ("xbc", KC), ("z", KC), ("m2_out", M2_XC), ("mlp1", KC)):
            SPLITS[name] = 4 * (PAIRS[name][0] - PAIRS["glu"][0])
            LOWS[name] = (sum(m for _, m in LOWS.values()), n)

        def rows(w):
            return w.rearrange("(c p) n -> p c n", p=P)

        block = ctx.enter_context(nc.Block())

        @block.sync
        def _(sp):
            sp.dma_start(cond1, A["c_rows"][0:2, :].partition_broadcast(P)).then_inc(in_cond, 16)
            sp.dma_start(cond2[:], A["c_rows"][2, :].partition_broadcast(P)).then_inc(in_cond, 16)
            for name, tile in (("cols", cols), ("mats", mats), ("iota", iota), ("tokid", tokid)):
                sp.dma_start(tile[:], A[name]).then_inc(in_small, 16)
            sp.dma_start(lam4, A["lam4"]).then_inc(in_small, 16)

            def load_pair(pair, i, source):
                for s in range(2):
                    for half in range(2):
                        sp.wait_ge(tile_used, pair * 4 + (2 * s + half + 1))
                        sp.dma_start(ring[:, s, 4 * half:4 * half + 4, :], source(i, s)[:, 4 * half:4 * half + 4, :]) \
                            .then_inc(tile_loaded[2 * s + half], 16)

            def load_pairs(name, source):
                first, count = PAIRS[name]
                with sp.Fori(0, count) as i:
                    load_pair(i + first, i, source)

            def columns(w, first=0):
                return lambda i, s: rows(w)[:, :, bass.ds(i * (2 * TN) + (first + s * TN), TN)]

            sp.dma_start(x[:], A["xT"]).then_inc(in_x, 16)
            sp.dma_start(cx, A["ctxT"]).then_inc(in_x, 16)
            for name, tile in (("rope_c", rope_c), ("rope_s", rope_s), ("dft_c", dft_c), ("dft_s", dft_s),
                               ("dft_ch", dft_ch), ("wfour", wfour)):
                sp.dma_start(tile, A[name]).then_inc(in_mix, 16)
            load_pairs("in", columns(A["w_in"]))
            load_pairs("out", columns(A["w_out"]))

            sp.wait_ge(consts_set, 2)
            sp.dma_start(h_rows[T:T + 1, :].rearrange("o (q n) -> o q n", n=256),
                         zeros[0:1, :].unsqueeze(1).broadcast_to([1, 4, 256])).then_inc(zero_row, 16)
            y_quarters = y_rows.rearrange("(b p) (q n) -> q p b n", p=P, n=256)
            for q in range(4):
                sp.dma_start(y_quarters[q], zeros[:].unsqueeze(1).broadcast_to([P, BLOCKS + 2, 256])) \
                    .then_inc(y_stored[0] if q == 3 else y_zeroed, 16)
            sp.wait_ge(x1_ready, KC)
            sp.dma_start(w_router, A["w_router"]).then_inc(in_late, 16)
            sp.dma_start(b_router, A["b_router"]).then_inc(in_late, 16)
            sp.wait_ge(route_ready, 1)
            pairs = sp.value_load(route_i[0:1, BLOCKS:BLOCKS + 1], min_val=1, max_val=BLOCKS // 2)
            with sp.Fori(0, pairs) as i:
                for s in range(2):
                    e = sp.value_load(route_i[0:1, bass.ds(i * 2 + s, 1)], min_val=0, max_val=EXPERTS - 1)
                    for w, tile, used, loaded in (("w_gate", expert_w[s][0], gate_mm, gate_loaded[s]),
                                                  ("w_up", expert_w[s][1], up_mm, up_loaded[s]),
                                                  ("w_down", expert_w[s][2], down_mm, down_loaded[s])):
                        sp.wait_ge(used, i * 2 + (s + 1))
                        sp.dma_start(tile, A[w][bass.ds(e, 1), :, :].rearrange("o (c p) n -> p (o c) n", p=P)) \
                            .then_inc(loaded, 16)

            sp.wait_ge(ysum_ready, TC)
            sp.dma_start(s5_b, A["s5_b"]).then_inc(in_late, 16)
            sp.dma_start(s5_c, A["s5_c"]).then_inc(in_late, 16)
            load_pairs("s5_in", columns(A["s5_w_in"]))
            load_pairs("glu", lambda i, s: rows(A["w_glu"])[:, :, bass.ds(i * TN + s * D, TN)])

            def load_mlp(layer):
                first = PAIRS[f"mlp{layer}"][0]
                with sp.Fori(0, 4) as i:
                    load_pair(i * 2 + first, i, columns(A["mlp_w1"][layer, :, :]))
                    load_pair(i * 2 + (first + 1), i, lambda i, s: A["mlp_w2"][
                        layer, bass.ds(i * D, D), s * TN:(s + 1) * TN].rearrange("(c p) n -> p c n", p=P))

            load_mlp(0)
            sp.dma_start(w_dt, A["m2_w_dt"]).then_inc(in_late, 16)
            load_pairs("xbc", columns(A["m2_w_in"], M2_IN))
            load_pairs("z", columns(A["m2_w_in"]))
            load_pairs("m2_out", lambda i, s: A["m2_w_out"][s * D:(s + 1) * D, bass.ds(i * TN, TN)]
                       .rearrange("(c p) n -> p c n", p=P))
            load_mlp(1)
            sp.wait_ge(h_ready, 10 * KC)
            sp.dma_start(out, x[:]).then_inc(out_stored, 16)
            sp.wait_ge(out_stored, 16)

        @block.gpsimd
        def _(pool):
            pool.memset(ones[:], 1.0).then_inc(consts_set, 1)
            pool.memset(zeros[:], 0.0).then_inc(consts_set, 1)
            pool.iota(idx_all[:], [[0, BLOCKS]], base=T, channel_multiplier=0).then_inc(idx_set, 1)
            pool.wait_ge(idx_set, 1)
            pool.dma_start(slot_tok.rearrange("(p b) o -> p (b o)", b=BLOCKS), idx_all[:]).then_inc(idx_filled, 16)
            pool.sem_inc(ada_used, 2)
            for first, w in ((0, A["w_adaT"]), (1, A["ada_w_2T"][0, :, :])):
                with pool.Fori(0, ADA_TILES // 2) as i:
                    for s in range(2):
                        pool.wait_ge(ada_used, i * 2 + (ADA_TILES * first + s + 1))
                        pool.dma_start(ada_buf[s], w[bass.ds(i * (8 * P) + s * 4 * P, 4 * P), :]
                                       .rearrange("(n p) k -> p n k", p=P)).then_inc(ada_loaded[s], 16)

            pool.wait_ge(idx_filled, 16)
            pool.wait_ge(route_ready, 1)
            for k in range(2):
                for t in range(TC):
                    pool.indirect_dma_start(slot_tok, bass.IndirectOffsetOnAxis(slot_at[:, k, t:t + 1], 0),
                                            tokid[:, t:t + 1], None).then_inc(idx_stored, 16)
            pool.wait_ge(idx_stored, 16 * 2 * TC)
            pool.dma_start(idx_all[:], slot_tok.rearrange("(p b) o -> p (b o)", b=BLOCKS)).then_inc(idx_loaded, 16)
            pairs = pool.value_load(route_i[0:1, BLOCKS:BLOCKS + 1], min_val=1, max_val=BLOCKS // 2)
            pool.wait_ge(idx_loaded, 16)
            pool.wait_ge(zero_row, 16)
            for s in range(2):
                pool.wait_ge(hrow_stored[s], 32)
            with pool.Fori(0, pairs) as i:
                for s in range(2):
                    pool.wait_ge(xT_mm, i * 2 + (s + 1))
                    pool.tensor_copy(idx[s][:], idx_all[:, bass.ds(i * 2 + s, 1)])
                    pool.drain()
                    pool.indirect_dma_start(xb[:, s, :], None, h_rows, bass.IndirectOffsetOnAxis(idx[s][:, 0:1], 0)) \
                        .then_inc(xb_loaded[s], 16)
            pool.wait_ge(moe_done, 1)
            for t in range(TC):
                for k in range(2):
                    pool.indirect_dma_start(y_of[:, k, t, :], None, y_rows,
                                            bass.IndirectOffsetOnAxis(slot_of[:, k, t:t + 1].bitcast(U32), 0)) \
                        .then_inc(y_loaded, 16)
            pool.wait_ge(ysum_ready, TC)
            pool.memset(wk(29440, 1152), 0.0).then_inc(c_zero, 1)
            pool.memset(decay_now, 0.0).then_inc(c_zero, 1)
            pool.sem_inc(g_added, 2)
            with pool.Fori(0, KC) as q:
                for a in range(3):
                    pool.wait_ge(bu_used, q * 4 + (4 + a + 1))
                    t = [chunked(rot[:, a % 2, n, :]) for n in range(4)]
                    nc.gpsimd.tensor_tensor(scan_g[:, :, 2 * a, :], t[0], t[1], ALU.add)
                    nc.gpsimd.tensor_tensor(scan_g[:, :, 2 * a + 1, :], t[2], t[3], ALU.subtract).then_inc(g_added, 1)
            pool.wait_ge(glu_used, KC)
            with pool.Fori(0, 4) as i:
                for j in range(4):
                    pool.wait_ge(ada_used, i * 4 + (2 * ADA_TILES + j + 1))
                    pool.dma_start(ada_buf1[j % 2], A["ada_w_2T"][1, bass.ds(i * (12 * P) + j * 3 * P, 3 * P), :]
                                   .rearrange("(n p) k -> p n k", p=P)).then_inc(ada_loaded[j % 2], 16)

        @block.tensor
        def _(pe):
            pe.sem_inc(tile_used, 4)

            def tile_wait(name, i, s):
                for half in range(2):
                    pe.wait_ge(tile_loaded[2 * s + half], i * 16 + 16 * (PAIRS[name][0] + 1))

            def tile_done():
                pe.drain().then_inc(tile_used, 2)

            def split_half(n, s, half, bank, hi, lo, first, last, freed=None, done=None):
                pe.wait_ge(w_split, n + (2 * s + half + 1))
                for k in range(4):
                    if freed is not None:
                        pe.wait_ge(*freed(k))
                    for c in range(4):
                        at = slice(k * P, (k + 1) * P)
                        w_of, wlo = ring_hi[:, s, 4 * half + c, at], ring[:, s, 4 * half + c, at]
                        nc.tensor.matmul(PS[:, bank + k, :], f32r(w_of), f32r(hi(c)), start=first and c == 0, stop=False)
                        nc.tensor.matmul(PS[:, bank + k, :], f32r(wlo), f32r(hi(c)), start=False, stop=False)
                        mm = nc.tensor.matmul(PS[:, bank + k, :], f32r(w_of), f32r(lo(c)), start=False, stop=last and c == 3)
                    if done is not None:
                        mm.then_inc(done, 1)
                pe.drain().then_inc(tile_used, 1)

            def split_tile(n, s, bank, hi, lo, freed, done):
                for half in range(2):
                    split_half(n, s, half, bank, lambda c: hi[:, 4 * half + c, :], lambda c: lo[:, 4 * half + c, :],
                               half == 0, half == 1, freed if half == 0 else None, done if half == 1 else None)

            def lows_wait(name):
                pe.wait_ge(lo_ready, sum(LOWS[name]))

            def norm_sum(k, sq, n, last=KC):
                for c in range(KC):
                    pe.wait_ge(sq_ready, KC * k + c + 1)
                    mm = nc.tensor.matmul(PS[:, k % 2, 0:n], ones[:], sq[:, c, 0:n], start=(c == 0), stop=(c == KC - 1))
                mm.then_inc(ms_done, 1)

            pe.wait_ge(consts_set, 1)
            norm_sum(0, h, T)
            norm_sum(1, csq, CTX)

            pe.wait_ge(h_ready, 2 * KC)
            group = [0]

            def projection(s, cols_of, rhs_of, n):
                e = group[0]
                if e >= 8:
                    pe.wait_ge(qkv_evac, e - 7)
                for c in range(KC):
                    mm = nc.tensor.matmul(PS[:, e % 8, 0:n], cols_of(c), rhs_of(c), start=(c == 0), stop=(c == KC - 1))
                mm.then_inc(qkv_mm, 1)
                group[0] += 1

            tile_wait("in", 0, 0)
            for k in range(4):
                projection(0, lambda c: ring[:, 0, c, k * P:(k + 1) * P], lambda c: h[:, c, :], T)
            tile_done()
            tile_wait("in", 0, 1)
            for k in range(4):
                projection(1, lambda c: ring[:, 1, c, k * P:(k + 1) * P], lambda c: h[:, c, :], T)
            for k in range(4):
                projection(1, lambda c: ring[:, 1, c, k * P:(k + 1) * P], lambda c: cx[:, c, :], CTX)
            tile_done()
            tile_wait("in", 1, 0)
            for k in range(KCH):
                tok = (lambda c: cx[:, c, k * P:(k + 1) * P]) if k < 2 else (lambda c: h[:, c, (k - 2) * P:(k - 1) * P])
                projection(0, tok, lambda c: ring[:, 0, c, :], TN)
            tile_done()
            tile_wait("in", 1, 1)
            for k in range(4):
                projection(1, lambda c: ring[:, 1, c, k * P:(k + 1) * P], lambda c: h[:, c, :], T)
            tile_done()

            pe.wait_ge(qkv_evac, 22)
            for j in range(8):
                src = qT[:, j, :] if j < 4 else kT[:, j - 4, CTX:KEYS]
                nc.tensor.matmul(PS[:, j, :], rope_rot, src, start=True, stop=True).then_inc(rope_mm, 1)

            pe.wait_ge(rope_done, 8)
            pe.wait_ge(in_mix, 16 * 6)
            for g in range(GROUPS):
                if g:
                    pe.wait_ge(ab_evac, 2 * g)
                for t in range(TC):
                    mm = nc.tensor.matmul(PS[:, t // 2, (t % 2) * 256:(t % 2 + 1) * 256], fT[:, g, t * P:(t + 1) * P],
                                          dft_ch, start=True, stop=True)
                    if t % 2:
                        mm.then_inc(ab_mm, 1)
                pe.wait_ge(ab_evac, 2 * g + 2)
                for t in range(TC):
                    nc.tensor.matmul(PS[:, 2, :], fab[:, g % 2, t, 0:P], dft_c[:, t, :], start=(t == 0), stop=False)
                    mm = nc.tensor.matmul(PS[:, 2, :], fab[:, g % 2, t, P:2 * P], dft_s[:, t, :], start=False,
                                          stop=(t == TC - 1))
                mm.then_inc(fr_mm, 1)
                pe.wait_ge(fr_evac, g + 1)
                if g:
                    pe.wait_ge(fo_evac, g)
                nc.tensor.matmul(PS[:, 3, :], wfour[:, g, :], fre, start=True, stop=True).then_inc(fo_mm, 1)

            def scores(n):
                hd, qc = n // TC, n % TC
                if n:
                    pe.wait_ge(exp_done, 2 * n)
                for m in range(2):
                    half = slice(m * DH, (m + 1) * DH)
                    q = qT[half, hd, qc * P:(qc + 1) * P]
                    nc.tensor.matmul(PS[:, 2 * m, :], q, kT[half, hd, 0:512], start=True, stop=True)
                    nc.tensor.matmul(PS[:, 2 * m + 1, 0:KEYS - 512], q, kT[half, hd, 512:KEYS], start=True,
                                     stop=True).then_inc(score_mm, 1)

            pe.wait_ge(fo_evac, GROUPS)
            scores(0)
            for n in range(HEADS * TC):
                hd, qc = n // TC, n % TC
                if n + 1 < HEADS * TC:
                    scores(n + 1)
                pe.wait_ge(a_ready, n + 1)
                if n:
                    pe.wait_ge(at_evac, n)
                for k in range(KCH):
                    mm = nc.tensor.transpose(PS[:, 4 + k // 4, (k % 4) * P:(k % 4 + 1) * P],
                                             attn_a[:, n % 2, k * P:(k + 1) * P], eye)
                mm.then_inc(at_mm, 1)
                if qc == TC - 1:
                    pe.wait_ge(at_evac, n + 1)
                    if hd:
                        pe.wait_ge(head_done, hd)
                    for k in range(KCH):
                        mm = nc.tensor.matmul(PS[:, 6, :], vtok[:, k, hd * P:(hd + 1) * P], aT[:, k, :],
                                              start=(k == 0), stop=(k == KCH - 1))
                    mm.then_inc(pv_mm, 1)
                    pe.wait_ge(osq_ready, hd + 1)
                    nc.tensor.matmul(PS[:, 7, :], ones[:], oSq, start=True, stop=True).then_inc(oms_done, 1)

            pe.wait_ge(head_done, HEADS)
            for s in range(2):
                tile_wait("out", 0, s)
                for k in range(4):
                    for c in range(KC):
                        mm = nc.tensor.matmul(PS[:, 4 * s + k, :], ring[:, s, c, k * P:(k + 1) * P], h[:, c, :],
                                              start=(c == 0), stop=(c == KC - 1))
                    mm.then_inc(proj_mm, 1)
                tile_done()

            pe.wait_ge(x1_ready, KC)
            norm_sum(2, h, T)
            pe.wait_ge(h_ready, 3 * KC)
            pe.wait_ge(in_late, 32)
            for t in range(TC):
                for c in range(KC):
                    mm = nc.tensor.matmul(PS[:, 1, t * 36:(t + 1) * 36], h[:, c, t * P:(t + 1) * P], w_router[:, c, :],
                                          start=(c == 0), stop=(c == KC - 1))
            mm.then_inc(lg_mm, 1)
            for t in range(TC):
                if t >= 2:
                    pe.wait_ge(hrow_evac, t - 1)
                for c in range(KC):
                    mm = nc.tensor.transpose(PS[:, 2 + 2 * (t % 2) + c // 4, (c % 4) * P:(c % 4 + 1) * P],
                                             h[:, c, t * P:(t + 1) * P], eye)
                mm.then_inc(hrow_mm, 1)
            pe.wait_ge(chosen_ready, 1)
            for t in range(TC):
                for before in range(t):
                    nc.tensor.matmul(PS[:, 6, t * EXPERTS:(t + 1) * EXPERTS], ones[:], chosen[:, before, :],
                                     start=(before == 0), stop=False)
                nc.tensor.matmul(PS[:, 6, t * EXPERTS:(t + 1) * EXPERTS], tri, chosen[:, t, :], start=(t == 0), stop=True)
            for t in range(TC):
                mm = nc.tensor.matmul(PS[:, 6, TC * EXPERTS:(TC + 1) * EXPERTS], ones[:], chosen[:, t, :],
                                      start=(t == 0), stop=(t == TC - 1))
            mm.then_inc(rank_mm, 1)

            pe.wait_ge(route_ready, 1)
            pe.wait_ge(hrow_evac, TC)
            pairs = pe.value_load(route_i[0:1, BLOCKS:BLOCKS + 1], min_val=1, max_val=BLOCKS // 2)
            for freed in (gate_mm, up_mm, down_mm, xT_mm):
                pe.sem_inc(freed, 2)

            def turn_tokens(i, s):
                pe.wait_ge(xb_loaded[s], i * 16 + 16)
                pe.wait_ge(xT_evac, i * 2 + (s + 1))
                for c in range(KC):
                    mm = nc.tensor.transpose(PS[:, c // 4, (c % 4) * P:(c % 4 + 1) * P], xb[:, s, c * P:(c + 1) * P], eye)
                mm.then_inc(xT_mm, 1)

            def gate_up(i, s):
                pe.wait_ge(xT_evac, i * 2 + (s + 2))
                pe.wait_ge(hid_ready, i * 2 + (s + 1))
                for loaded, w, bank, done in ((gate_loaded[s], expert_w[s][0], 2, gate_mm),
                                              (up_loaded[s], expert_w[s][1], 3, up_mm)):
                    pe.wait_ge(loaded, i * 16 + 16)
                    for c in range(KC):
                        mm = nc.tensor.matmul(PS[:, bank, :], xbT[:, s, c, :], w[:, c, :], start=(c == 0),
                                              stop=(c == KC - 1))
                    mm.then_inc(done, 1)

            def turn_hidden(i, s):
                pe.wait_ge(hid_ready, i * 2 + (s + 2))
                pe.wait_ge(hT_evac, i * 2 + (s + 1))
                for c in range(4):
                    mm = nc.tensor.transpose(PS[:, 4, c * P:(c + 1) * P], hid[:, s, c * P:(c + 1) * P], eye)
                mm.then_inc(hT_mm, 1)

            def down(i, s):
                pe.wait_ge(hT_evac, i * 2 + (s + 2))
                pe.wait_ge(y_ready, i * 2 + (s + 1))
                pe.wait_ge(down_loaded[s], i * 16 + 16)
                for n in range(2):
                    for c in range(4):
                        mm = nc.tensor.matmul(PS[:, 5 + n, :], hidT[:, s, c, :], expert_w[s][2][:, c, n * 512:(n + 1) * 512],
                                              start=(c == 0), stop=(c == 3))
                mm.then_inc(down_mm, 1)

            with pe.Fori(0, pairs) as i:
                turn_tokens(i, 0)
                gate_up(i, 0)
                turn_tokens(i, 1)
                turn_hidden(i, 0)
                down(i, 0)
                gate_up(i, 1)
                turn_hidden(i, 1)
                down(i, 1)
            pe.wait_ge(moe_done, 1)
            for t in range(TC):
                pe.wait_ge(ysum_ready, t + 1)
                if t >= 2:
                    pe.wait_ge(yT_used, t - 1)
                for c in range(KC):
                    mm = nc.tensor.transpose(PS[:, 2 * (t % 2) + c // 4, (c % 4) * P:(c % 4 + 1) * P],
                                             ysum[:, t % 2, c * P:(c + 1) * P], eye)
                mm.then_inc(yT_mm, 1)
            pe.wait_ge(x2_ready, 1)
            norm_sum(3, h, T)

            norm_sum(4, h, T)
            pe.wait_ge(h_ready, 5 * KC)
            for s in range(2):
                tile_wait("s5_in", 0, s)
                for k in range(4):
                    for c in range(KC):
                        mm = nc.tensor.matmul(PS[:, 4 * s + k, :], ring[:, s, c, k * P:(k + 1) * P], h[:, c, :],
                                              start=(c == 0), stop=(c == KC - 1))
                    mm.then_inc(proj_mm, 1)
                tile_done()
            pe.wait_ge(u_evac, KC)
            pe.sem_inc(bu_mm, 4)
            pe.sem_inc(s5_mm, 2)

            def inputs_to_states(q, a):
                pe.wait_ge(bu_used, q * 4 + (5 if a == 3 else 4))
                for part in range(2):
                    mm = nc.tensor.matmul(PS[:, 2 * (a % 3) + part, :], b_now[32 * a:32 * a + 32, part, :],
                                          u_now[32 * a:32 * a + 32, :], start=True, stop=True)
                mm.then_inc(bu_mm, 1)

            def s5_quad(q, last):
                inputs_to_states(q, 3)
                if not last:
                    pe.wait_ge(ub_staged, q + 2)
                    for a in range(3):
                        inputs_to_states(q + 1, a)
                pe.wait_ge(c_staged, q + 1)
                pe.wait_ge(s5_used, q + 1)
                c_pad = c_now.rearrange("p a n -> p (a n)")
                for a in range(4):
                    pe.wait_ge(state_ready, q * 4 + (a + 2))
                    for n in range(4):
                        at = (2 * a + n // 2) * P
                        mm = nc.tensor.matmul(PS[:, 6, :], c_pad[:, at:at + P], turned[:, a % 2, n, :],
                                              start=(a == 0 and n == 0), stop=(a == 3 and n == 3))
                    mm.then_inc(s5_mm, 1)

            pe.wait_ge(ub_staged, 1)
            for a in range(3):
                inputs_to_states(0, a)
            with pe.Fori(0, KC - 1) as q:
                s5_quad(q, False)
            s5_quad(KC - 1, True)
            lows_wait("glu")
            for i in range(2):
                for s in range(2):
                    split_tile(SPLITS["glu"] + 4 * i, s, 4 * s, h, glu_lo, (lambda k: (glu_used, k + 1)) if i else None, glu_mm)

            def mlp(layer, k_norm):
                name = f"mlp{layer}"
                norm_sum(k_norm, h, T)
                lows_wait(name)
                with pe.Fori(0, 4) as i:
                    for s in range(2):
                        split_tile(i * 8 + SPLITS[name], s, 4 * s, h, mlp_h_lo,
                                   lambda k: (mlp_added, i * 8 + (32 * layer + 4 * s + k + 1)), mlp1_mm)
                    for s in range(2):
                        for half in range(2):
                            if s == 0:
                                pe.wait_ge(mlp_split, i * 8 + (32 * layer + 4 * half + 4))
                            split_half(i * 8 + (SPLITS[name] + 4), s, half, 4 * s, lambda c: mlp_hi[:, 4 * half + c, :],
                                       lambda c: mlp_lo[:, 4 * half + c, :], half == 0, half == 1,
                                       (lambda k: (relu_done, i * 8 + (32 * layer + 4 * s + k + 1))) if half == 0 else None,
                                       mlp2_mm if half else None)

            pe.wait_ge(glu_used, KC)
            mlp(0, 5)

            norm_sum(6, h, T)
            lows_wait("xbc")
            with pe.Fori(0, 3) as i:
                for s in range(2):
                    split_tile(i * 4 + SPLITS["xbc"], s, 4 * s, h, xbc_h_lo,
                               lambda k: (conv_done, i * 8 + (4 * s + k + 1)), xbc_mm)
            pe.wait_ge(conv_done, 8 + M2_CC)
            pe.wait_ge(step_dve, 1)
            pe.wait_ge(in_late, 80)
            for c in range(KC):
                mm = nc.tensor.matmul(PS[0:M2_HEADS, 0, :], w_dt[:, c, :], h[:, c, :], start=(c == 0), stop=(c == KC - 1))
            mm.then_inc(dt_mm, 1)
            pe.wait_ge(step_dve, 3)
            for c in range(M2_NC):
                for n, rows_of in enumerate((dt_t, a_cs)):
                    nc.tensor.transpose(PS[:, 1, (4 * n + c) * M2_HEADS:(4 * n + c + 1) * M2_HEADS],
                                        rows_of[:, c * M2_Q:(c + 1) * M2_Q], eye[0:M2_HEADS, 0:M2_HEADS])
            nc.tensor.matmul(PS[:, 2, 0:M2_NC * M2_HEADS], ones[0:M2_HEADS, :], last_diag.rearrange("p c h -> p (c h)"),
                             start=True, stop=True).then_inc(tok_mm, 1)
            pe.wait_ge(step_act, 2)
            pe.wait_ge(xs_ready, M2_CC)
            pe.sem_inc(y7_mm, 2)
            pe.sem_inc(y_turned, 2)
            with pe.Fori(0, M2_NC) as c:
                pe.wait_ge(ssd_staged, c + 1)
                for j in range(M2_XC):
                    mm = nc.tensor.transpose(PS[:, j // 4, (j % 4) * P:(j % 4 + 1) * P], xs_now[:, j, :], eye)
                    if j % 4 == 3:
                        mm.then_inc(xs_tok_mm, 1)
                for g in range(M2_G):
                    mm = nc.tensor.transpose(PS[:, 4, g * P:(g + 1) * P], xs_now[:, M2_XC + g, :], eye)
                mm.then_inc(b_tok_mm, 1)
                for g in range(M2_G):
                    mm = nc.tensor.matmul(PS[:, 5, g * P:(g + 1) * P], xs_now[:, M2_XC + g, :], xs_now[:, M2_XC + M2_G + g, :],
                                          start=True, stop=True)
                mm.then_inc(cb_mm, 1)

                def spread_sums(q):
                    if 1 <= q <= 4:
                        pe.wait_ge(off_used, c * 4 + q)
                    elif q:
                        pe.wait_ge(decay_ready, c * 8 + (q - 4))
                    bank = SUM_BANKS[q % 5]
                    nc.tensor.matmul(PS[:, bank, :], eye16, mask16.unsqueeze(1).broadcast_to([P, 4, P]), start=True, stop=False)
                    for k in range(4):
                        n = 4 * q + k
                        mm = nc.tensor.matmul(PS[:, bank, k * P:(k + 1) * P], eye[0:M2_HEADS, n:n + 1].broadcast_to([M2_HEADS, P]),
                                              sums_now, start=False, stop=(k == 3))
                    mm.then_inc(cs_mm, 1)

                def turn_y(q):
                    pe.wait_ge(y_tok_evac, c * 8 + (q + 2))
                    pe.wait_ge(b_tok_evac, c + 1)
                    pe.wait_ge(y_added, c * 8 + (q + 1))
                    for j in range(2):
                        mm = nc.tensor.transpose(PS[:, 4, j * P:(j + 1) * P], y_tok[:, q % 2, j * P:(j + 1) * P], eye)
                    mm.then_inc(y_turned, 1)

                spread_sums(0)
                for g in range(M2_G):
                    pe.wait_ge(xdt_ready, c * 4 + (g + 1))
                    nc.tensor.matmul(PS[:, g, :], xs_now[:, M2_XC + M2_G + g, :], state[:, g * 512:(g + 1) * 512], start=True,
                                     stop=True).then_inc(off_mm, 1)
                spread_sums(1)
                spread_sums(2)
                for q in range(8):
                    pe.wait_ge(m_ready, c * 8 + (q + 3))
                    pe.wait_ge(y_tok_evac, c * 8 + (q + 1))
                    for k in range(4):
                        at = (4 * q + k) * 64
                        mm = nc.tensor.matmul(PS[:, 7, k * 64:(k + 1) * 64], m_now[:, q % 2, k, :], xdt[:, at:at + 64], start=True,
                                              stop=True)
                    mm.then_inc(y7_mm, 1)
                    if q < 5:
                        spread_sums(q + 3)
                    if q:
                        turn_y(q - 1)
                turn_y(7)
                pe.wait_ge(xdt_dec_ready, c + 1)
                for g in range(M2_G):
                    mm = nc.tensor.matmul(PS[:, g, :], b_tok[:, g, :], xdt_dec[:, g * 512:(g + 1) * 512], start=True, stop=True)
                mm.then_inc(st_mm, 1)
            pe.wait_ge(state_new, 1 + M2_NC)
            lows_wait("z")
            with pe.Fori(0, 2) as i:
                for s in range(2):
                    split_tile(i * 4 + SPLITS["z"], s, 4 * s, z_h_hi, h, lambda k: (z_ready, i * 8 + (4 * s + k + 1)), z_mm)
            for g in range(M2_G):
                for j in range(4):
                    pe.wait_ge(osq_ready, HEADS + 4 * g + j + 1)
                    mm = nc.tensor.matmul(PS[:, g, :], ones[:], m2_sq[:, 4 * g + j, :], start=(j == 0), stop=(j == 3))
                mm.then_inc(oms_done, 1)
            lows_wait("m2_out")
            for out_half in range(2):
                for s in range(2):
                    for half in range(2):
                        rows_at = 8 * s + 4 * half
                        split_half(SPLITS["m2_out"] + 4 * out_half, s, half, 4 * out_half, lambda c: xs[:, rows_at + c, :],
                                   lambda c: y_lo[:, rows_at + c, :], rows_at == 0, rows_at == 12, None,
                                   proj_mm if rows_at == 12 else None)
            pe.wait_ge(x5_ready, KC)
            mlp(1, 7)
            pe.wait_ge(mlp_added, 8 + 8 * KC)
            norm_sum(8, h, T)

        @block.scalar
        def _(act):
            def copy(out, in_):
                return nc.scalar.activation(out, in_, ACT.Copy)

            def norm_squares(src, sq):
                for c in range(KC):
                    nc.scalar.activation(sq[:, c, :], src[:, c, :], ACT.Square).then_inc(sq_ready, 1)

            def norm_root(k, n):
                act.wait_ge(var_ready, k + 1)
                nc.scalar.activation(rstd[:, 0:n], var[:, 0:n], ACT.Sqrt).then_inc(std_ready, 1)

            def norm_affine(k, dst, scale, shift):
                for c in range(KC):
                    act.wait_ge(xn_ready, KC * k + c + 1)
                    nc.scalar.activation(dst[:, c, :], dst[:, c, :], ACT.Identity, scale=scale[:, c:c + 1],
                                         bias=shift[:, c:c + 1] if shift is not None else 0.0).then_inc(h_ready, 1)

            def norm_affine_split(k, lo, scale, shift):
                for c in range(KC):
                    act.wait_ge(xn_ready, KC * k + c + 1)
                    for dst in (f32r(h[:, c, :]), lo[:, c, :]):
                        last = nc.scalar.activation(dst, lo[:, c, :], ACT.Identity, scale=scale[:, c:c + 1],
                                                    bias=shift[:, c:c + 1])
                    last.then_inc(h_ready, 1)

            def round_weights(pair, s):
                for half in range(2):
                    act.wait_ge(tile_loaded[2 * s + half], pair * 16 + 16)
                    at = slice(4 * half, 4 * half + 4)
                    copy(f32r(ring_hi[:, s, at, :]), ring[:, s, at, :]).then_inc(w_hi, 1)

            act.wait_ge(in_cond, 32)
            nc.scalar.activation(cond1, cond1, ACT.Silu).then_inc(cond_ready, 1)
            nc.scalar.activation(cond2[:], cond2[:], ACT.Silu).then_inc(cond_ready, 1)
            act.wait_ge(in_x, 32)
            norm_squares(x, h)
            norm_squares(cx, csq)
            norm_root(0, T)
            act.wait_ge(exp_in, 1)
            nc.scalar.activation(lam_d[:, 2:4], lam_d[:, 0:2], ACT.Exp).then_inc(exp_out, 1)
            act.wait_ge(mods_ready, 1)
            norm_affine(0, h, gain[:, 0, :], mod1[:, 0:KC])
            norm_root(1, CTX)
            norm_affine(1, cx, gain[:, 1, :], modc[:, 0:KC])

            for e in range(22):
                act.wait_ge(qkv_mm, e + 1)
                if e < 4:
                    dst, n = qT[:, e, :], T
                elif e < 8:
                    dst, n = kT[:, e - 4, CTX:KEYS], T
                elif e < 12:
                    dst, n = kT[:, e - 8, 0:CTX], CTX
                elif e < 18:
                    dst, n = vtok[:, e - 12, :], TN
                else:
                    dst, n = fT[:, e - 18, :], T
                copy(dst, PS[:, e % 8, 0:n]).then_inc(qkv_evac, 1)

            for g in range(GROUPS):
                for b in range(2):
                    act.wait_ge(ab_mm, 2 * g + b + 1)
                    if g >= 2:
                        act.wait_ge(fr_mm, g - 1)
                    copy(fab[:, g % 2, 2 * b:2 * b + 2, :], PS[:, b, :].rearrange("p (t n) -> p t n", n=256)) \
                        .then_inc(ab_evac, 1)
                act.wait_ge(fr_mm, g + 1)
                if g:
                    act.wait_ge(fo_mm, g)
                copy(fre, PS[:, 2, :]).then_inc(fr_evac, 1)
                act.wait_ge(fo_mm, g + 1)
                copy(h[:, HEADS + g, :], PS[:, 3, :]).then_inc(fo_evac, 1)

            def exps(n):
                for m in range(2):
                    act.wait_ge(negmax_ready, 2 * n + m + 1)
                    if n >= 2:
                        act.wait_ge(a_ready, n - 1)
                    nc.scalar.activation(probs[:, n % 2, m, :],
                                         PS[:, 2 * m:2 * m + 2, :].rearrange("p a b -> p (a b)")[:, 0:KEYS], ACT.Exp,
                                         bias=negmax[:, n % 2, m:m + 1], scale=DH ** -0.5,
                                         accum_out=rowsum[:, n % 2, m:m + 1]).then_inc(exp_done, 1)

            exps(0)
            for n in range(HEADS * TC):
                hd, qc = n // TC, n % TC
                if n + 1 < HEADS * TC:
                    exps(n + 1)
                act.wait_ge(at_mm, n + 1)
                if hd and qc == 0:
                    act.wait_ge(pv_mm, hd)
                copy(aT[:, :, qc * P:(qc + 1) * P],
                     PS[:, 4:6, :].rearrange("p a (b q) -> p (a b) q", q=P)[:, 0:KCH, :]).then_inc(at_evac, 1)
                if qc == TC - 1:
                    act.wait_ge(o_ready, hd + 1)
                    nc.scalar.activation(oSq, oT, ACT.Square).then_inc(osq_ready, 1)
                    act.wait_ge(ovar_ready, hd + 1)
                    nc.scalar.activation(rstd, var, ACT.Sqrt).then_inc(ostd_ready, 1)

            act.wait_ge(x1_ready, KC)
            norm_squares(x, h)
            norm_root(2, T)
            norm_affine(2, h, gain[:, 2, :], mod1[:, 3 * KC:4 * KC])
            for t in range(TC):
                act.wait_ge(hrow_mm, t + 1)
                if t >= 2:
                    act.wait_ge(hrow_stored[t % 2], 16)
                copy(hrow[:, t % 2, :].rearrange("p (a b) -> p a b", a=2),
                     PS[:, 2 + 2 * (t % 2):4 + 2 * (t % 2), :]).then_inc(hrow_evac, 1)
                act.wait_ge(hrow_evac, t + 1)
                act.dma_start(h_rows[t * P:(t + 1) * P, :], hrow[:, t % 2, :]).then_inc(hrow_stored[t % 2], 16)
            act.wait_ge(exp_in, 2)
            nc.scalar.activation(g_exp, g_exp, ACT.Exp).then_inc(exp_out, 1)
            act.wait_ge(exp_in, 3)
            nc.scalar.activation(e2, e2, ACT.Exp).then_inc(exp_out, 1)

            act.wait_ge(route_ready, 1)
            pairs = act.value_load(route_i[0:1, BLOCKS:BLOCKS + 1], min_val=1, max_val=BLOCKS // 2)
            for freed in (xT_evac, hT_evac):
                act.sem_inc(freed, 1)
            act.wait_ge(y_zeroed, 48)
            act.wait_ge(y_stored[0], 16)

            def tokens_turned(i, s):
                act.wait_ge(xT_mm, i * 2 + (s + 3))
                copy(xbT[:, s, :, :].rearrange("p (a c) q -> p a (c q)", a=2), PS[:, 0:2, :]).then_inc(xT_evac, 1)

            def gate_silu(i, s):
                act.wait_ge(gate_mm, i * 2 + (s + 3))
                nc.scalar.activation(silu_b[:, s, :], PS[:, 2, :], ACT.Silu).then_inc(silu_done, 1)

            def hidden_turned(i, s):
                act.wait_ge(hT_mm, i * 2 + (s + 1))
                copy(hidT[:, s, :, :].rearrange("p c q -> p (c q)"), PS[:, 4, :]).then_inc(hT_evac, 1)

            def store_last(i, s):
                act.wait_ge(y_ready, i * 2 + (s + 1))
                act.dma_start(y_rows[bass.ds(i * (2 * P) + s * P, P), :], yb[:, 1 - s, :]).then_inc(y_stored[1 - s], 16)

            with act.Fori(0, pairs) as i:
                tokens_turned(i, 0)
                gate_silu(i, 0)
                store_last(i, 0)
                tokens_turned(i, 1)
                hidden_turned(i, 0)
                gate_silu(i, 1)
                store_last(i, 1)
                hidden_turned(i, 1)
            act.wait_ge(y_ready, pairs * 2 + 1)
            act.dma_start(y_rows[bass.ds(pairs * (2 * P), P), :], yb[:, 1, :]).then_inc(y_stored[1], 16)
            for s in range(2):
                act.wait_ge(y_stored[s], pairs * 16 + 16)
            act.sem_inc(moe_done, 1)

            act.wait_ge(x2_ready, 1)
            norm_squares(x, h)
            norm_root(3, T)
            norm_affine(3, x, col("g_final", 0, KC), None)

            act.wait_ge(h_ready, 4 * KC)
            norm_squares(x, h)
            act.wait_ge(in_small, 16 * 5)
            nc.scalar.activation(s5_dt, col("log_dt", 0, S5_TILES), ACT.Exp).then_inc(dt_exp, 1)
            norm_root(4, T)
            norm_affine(4, h, gain[:, 3, :], mod2[:, 0, 0:KC])
            act.wait_ge(angle_ready, 1)
            nc.scalar.activation(radius, s5_a, ACT.Exp)
            nc.scalar.activation(half_sin, s5_r, ACT.Sin)
            nc.scalar.activation(half_cos, s5_ab, ACT.Sin).then_inc(trig_ready, 1)
            for k in range(KC):
                act.wait_ge(proj_mm, KC + k + 1)
                copy(uT[:, k, :], PS[:, k, :]).then_inc(u_evac, 1)
            act.wait_ge(in_late, 64)
            act.wait_ge(u_evac, KC)
            act.wait_ge(c_zero, 2)
            act.wait_ge(c_ready, 1)
            with act.Fori(0, KC) as q:
                act.wait_ge(bu_mm, q * 4 + 4)
                copy(u_now, uT[:, bass.ds(q, 1), :].rearrange("p a n -> p (a n)"))
                copy(b_now, s5_b[:, bass.ds(q, 1), :, :].rearrange("p a r n -> p (a r) n")).then_inc(ub_staged, 1)
                act.wait_ge(state_ready, q * 4 + 1)
                copy(decay_now[:, :, :, 1:S5_Q], radius[:, bass.ds(q * 4, 4)].unsqueeze(2).unsqueeze(3)
                     .broadcast_to([P, 4, 2, S5_Q - 1])).then_inc(decay_set, 1)
                act.wait_ge(s5_mm, q * 4 + 2)
                for g in range(2):
                    part = slice(64 * g, 64 * g + 64)
                    for r in range(2):
                        last = copy(c_now[part, :, r * P + HP * g:r * P + HP * (g + 1)],
                                    s5_cf[part, bass.ds(q * 4, 4), r, :])
                last.then_inc(c_staged, 1)
            act.wait_ge(s5_used, KC + 1)
            first = PAIRS["glu"][0]
            round_weights(first, 0)
            for k in range(KC):
                nc.scalar.activation(glu_lo[:, k, :], h[:, k, :], ACT.Gelu_apprx_tanh)
                nc.scalar.activation(f32r(h[:, k, :]), h[:, k, :], ACT.Gelu_apprx_tanh).then_inc(gelu_done, 1)
            round_weights(first, 1)
            for i in range(2):
                round_weights(first + 1, i)
                for k in range(4):
                    n = 4 * i + k
                    act.wait_ge(glu_mm, 8 * i + 4 + k + 1)
                    if n >= 2:
                        act.wait_ge(glu_used, n - 1)
                    nc.scalar.activation(glu_gate[:, n % 2, :], PS[:, 4 + k, :], ACT.Sigmoid, bias=col("b_glu", KC + n)) \
                        .then_inc(gate_sig, 1)

            def mlp(layer, k_norm):
                first = PAIRS[f"mlp{layer}"][0]
                norm_squares(x, h)
                round_weights(first, 0)
                norm_root(k_norm, T)
                norm_affine_split(k_norm, mlp_h_lo, gain[:, 4 + 2 * layer, :], mod2[:, layer, 3 * KC:4 * KC])

                def quarter(i, last):
                    for t in range(4):
                        if t < 3 or not last:
                            round_weights(i * 2 + (first + (t + 1) // 2), (t + 1) % 2)
                        if t < 2:
                            for n in range(4 * t, 4 * t + 4):
                                act.wait_ge(relu_done, i * 8 + (32 * layer + n + 1))
                                for dst in (f32r(mlp_hi[:, n, :]), mlp_lo[:, n, :]):
                                    done = nc.scalar.activation(dst, mlp_lo[:, n, :], ACT.Square)
                                done.then_inc(sqr_done, 1)

                with act.Fori(0, 3) as i:
                    quarter(i, False)
                quarter(3, True)

            act.wait_ge(glu_used, KC)
            mlp(0, 5)

            act.wait_ge(mlp_added, 8 + 4 * KC)
            first = PAIRS["xbc"][0]
            norm_squares(x, h)
            round_weights(first, 0)
            norm_root(6, T)
            norm_affine_split(6, xbc_h_lo, gain[:, 5, :], mod2[:, 1, 0:KC])

            def conv_out(i, last):
                for s in range(2):
                    if s == 0 or not last:
                        round_weights(i + (first + s), 1 - s)
                    for k in range(4 * s, 4 * s + 4):
                        act.wait_ge(conv_done, i * 8 + (8 + k + 1))
                        chunk = xs[:, bass.ds(i * 8 + k, 1), :]
                        nc.scalar.activation(chunk, chunk, ACT.Silu,
                                             bias=cols[:, bass.ds(i * 8 + (COLS["conv_b"][0] + k), 1)]).then_inc(xs_ready, 1)

            with act.Fori(0, 2) as i:
                conv_out(i, False)
            conv_out(2, True)
            act.wait_ge(step_dve, 2)
            nc.scalar.activation(dt_abs, dt_raw, ACT.Abs)
            act.drain()
            nc.scalar.activation(dt_abs, dt_abs, ACT.Exp, scale=-1.0)
            nc.scalar.activation(a_pos, col("a_log")[0:M2_HEADS, :], ACT.Exp)
            act.drain()
            nc.scalar.activation(dt_abs, dt_abs, ACT.Ln, bias=1.0).then_inc(step_act, 1)
            act.wait_ge(step_dve, 4)
            nc.scalar.activation(dec_tok, dec_tok, ACT.Exp)
            nc.scalar.activation(exp_cs_tok, cs_neg, ACT.Exp, scale=-1.0)
            nc.scalar.activation(dec_chunk, PS[:, 2, 0:M2_NC * M2_HEADS].rearrange("p (c h) -> p c h", h=M2_HEADS), ACT.Exp) \
                .then_inc(step_act, 1)
            act.wait_ge(xs_ready, M2_CC)
            with act.Fori(0, M2_NC) as c:
                act.wait_ge(state_new, c + 1)
                copy(sums_now, a_cs[:, bass.ds(c * M2_Q, M2_Q)])
                copy(xs_now, xs[:, :, bass.ds(c * M2_Q, M2_Q)]).then_inc(ssd_staged, 1)
                act.wait_ge(b_tok_mm, c + 1)
                copy(b_tok.rearrange("p g n -> p (g n)"), PS[:, 4, :]).then_inc(b_tok_evac, 1)

                for q in range(8):
                    act.wait_ge(cs_mm, c * 8 + (q + 1))
                    act.wait_ge(m_ready, c * 8 + (q + 1))
                    for k in range(4):
                        n = 4 * q + k
                        last = nc.scalar.activation(decay[:, q % 2, k, :], PS[:, SUM_BANKS[q % 5], k * P:(k + 1) * P], ACT.Exp,
                                                    bias=cs_neg[:, bass.ds(c, 1), n:n + 1].rearrange("p c h -> p (c h)"))
                    last.then_inc(decay_ready, 1)
            act.sem_inc(z_ready, 8)
            act.wait_ge(state_new, 1 + M2_NC)
            first = PAIRS["z"][0]
            round_weights(first, 0)
            for c in range(KC):
                copy(f32r(z_h_hi[:, c, :]), h[:, c, :]).then_inc(h_ready, 1)
            for t in range(4):
                if t < 3:
                    round_weights(first + (t + 1) // 2, (t + 1) % 2)
                for n in range(4 * t, 4 * t + 4):
                    act.wait_ge(z_mm, n + 1)
                    act.wait_ge(z_used, n + 1)
                    nc.scalar.activation(z_silu[:, n % 2, :], PS[:, n % 8, :], ACT.Silu).then_inc(z_ready, 1)
            for g in range(M2_G):
                for j in range(4):
                    n = 4 * g + j
                    act.wait_ge(z_used, 2 + n + 1)
                    nc.scalar.activation(m2_sq[:, n, :], xs[:, n, :], ACT.Square).then_inc(osq_ready, 1)
            first = PAIRS["m2_out"][0]
            round_weights(first, 0)
            round_weights(first, 1)
            for g in range(M2_G):
                act.wait_ge(ovar_ready, HEADS + g + 1)
                nc.scalar.activation(rstd, var, ACT.Sqrt).then_inc(ostd_ready, 1)
                for n in range(4 * g, 4 * g + 4):
                    act.wait_ge(yn_ready, n + 1)
                    copy(f32r(xs[:, n, :]), y_lo[:, n, :]).then_inc(y_hi_ready, 1)
            for s in range(2):
                round_weights(first + 1, s)
            act.wait_ge(x5_ready, KC)
            mlp(1, 7)
            act.wait_ge(mlp_added, 8 + 8 * KC)
            norm_squares(x, h)
            norm_root(8, T)
            norm_affine(8, x, col("fin", 0, KC), None)

        @block.vector
        def _(dve):
            tt, ts, stt = nc.vector.tensor_tensor, nc.vector.tensor_scalar, nc.vector.scalar_tensor_tensor

            def norm_var(k, n, eps):
                dve.wait_ge(ms_done, k + 1)
                ts(var[:, 0:n], PS[:, k % 2, 0:n], 1.0 / D, eps, ALU.mult, ALU.add).then_inc(var_ready, 1)

            def norm_divide(k, src, dst, n):
                dve.wait_ge(std_ready, k + 1)
                nc.vector.reciprocal(rstd[:, 0:n], rstd[:, 0:n])
                dve.drain()
                for c in range(KC):
                    tt(dst[:, c, :], src[:, c, :], rstd[:, 0:n], ALU.mult).then_inc(xn_ready, 1)

            def modulation(pairs, base, cond_row, bias, dst, buf=ada_buf):
                with dve.Fori(*pairs) as i:
                    for s in range(2):
                        dve.wait_ge(ada_loaded[s], i * 16 + 16 * (base // 2 + 1))
                        for n in range(4):
                            w = buf[s][:, n, :]
                            last = stt(w, w, 1.0, cond_row, ALU.mult, ALU.mult,
                                       accum_out=dst[:, bass.ds(i * 8 + (4 * s + n), 1)])
                        last.then_inc(ada_used, 1)
                dve.drain()
                done = slice(8 * pairs[0], 8 * pairs[1])
                tt(dst[:, done], dst[:, done], bias[:, done], ALU.add)

            def modulation_both(i, s):
                dve.wait_ge(ada_loaded[s], 16 * (i + 1))
                for n in range(4):
                    w, k = ada_buf[s][:, n, :], 8 * i + 4 * s + n
                    dve.drain()
                    stt(norm_buf[:], w, 1.0, cond1[:, 1, :], ALU.mult, ALU.mult, accum_out=modc[:, k:k + 1])
                    dve.drain()
                    last = stt(norm_buf[:], w, 1.0, cond1[:, 0, :], ALU.mult, ALU.mult, accum_out=mod1[:, k:k + 1])
                last.then_inc(ada_used, 1)

            def norm_gain(n, scale, g):
                stt(gain[:, n, :], scale, 1.0, col(g, 0, KC), ALU.add, ALU.mult)

            def split_weights(name, n, s):
                for half in range(2):
                    dve.wait_ge(w_hi, n + (SPLITS[name] + half + 1))
                    at = slice(4 * half, 4 * half + 4)
                    tt(f32r(ring[:, s, at, :]), ring[:, s, at, :], f32r(ring_hi[:, s, at, :]), ALU.subtract).then_inc(w_split, 1)

            def split_inputs(lo, hi, done, count):
                for c in range(KC):
                    dve.wait_ge(done, count + c + 1)
                    tt(f32r(lo[:, c, :]), lo[:, c, :], f32r(hi[:, c, :]), ALU.subtract).then_inc(lo_ready, 1)

            dve.wait_ge(in_small, 16 * 5)
            dve.wait_ge(cond_ready, 1)
            for i in range(2):
                for s in range(2):
                    modulation_both(i, s)
            dve.drain()
            tt(mod1[:, 0:2 * KC], mod1[:, 0:2 * KC], col("b_ada", 0, 16), ALU.add)
            tt(modc[:], modc[:], col("b_ada", 0, 16), ALU.add)
            dve.drain()
            norm_gain(0, mod1[:, KC:2 * KC], "g_mix")
            norm_gain(1, modc[:, KC:2 * KC], "g_mix")
            ts(gsub, col("g_subln"), 1.0 - LAMBDA_INIT, None, ALU.mult)
            tt(lam_t[:, 0, :], lam4[:, 0, :], lam4[:, 1, :], ALU.mult)
            tt(lam_t[:, 1, :], lam4[:, 2, :], lam4[:, 3, :], ALU.mult).then_inc(mods_ready, 1)
            dve.drain()
            nc.vector.tensor_reduce(lam_d[:, 0:2], lam_t, AX, ALU.add).then_inc(exp_in, 1)
            norm_var(0, T, 1e-6)
            norm_divide(0, x, h, T)
            dve.wait_ge(exp_out, 1)
            tt(neglam, lam_d[:, 3:4], lam_d[:, 2:3], ALU.subtract)
            dve.drain()
            ts(neglam, neglam, -LAMBDA_INIT, None, ALU.add)
            dve.wait_ge(h_ready, KC)
            norm_var(1, CTX, 1e-6)
            norm_divide(1, cx, cx, CTX)

            modulation((2, ADA_TILES // 2), 0, cond1[:, 0, :], col("b_ada", 0, 48), mod1)
            dve.wait_ge(cond_ready, 2)
            modulation((0, ADA_TILES // 2), ADA_TILES, cond2[:], col("ada_b0", 0, 48), mod2[:, 0, :])
            dve.drain()
            norm_gain(2, mod1[:, 4 * KC:5 * KC], "g_ffn")
            norm_gain(3, mod2[:, 0, KC:2 * KC], "nmix0")
            norm_gain(4, mod2[:, 0, 4 * KC:5 * KC], "nmlp0")

            dve.wait_ge(in_mix, 16 * 6)
            for j in range(8):
                dve.wait_ge(rope_mm, j + 1)
                src = qT[:, j, :] if j < 4 else kT[:, j - 4, CTX:KEYS]
                tt(rope_t[:, j % 2, 0, :], src, rope_c, ALU.mult)
                tt(rope_t[:, j % 2, 1, :], PS[:, j, :], rope_s, ALU.mult)
                dve.drain()
                tt(src, rope_t[:, j % 2, 0, :], rope_t[:, j % 2, 1, :], ALU.add).then_inc(rope_done, 1)

            def maxima(n):
                for m in range(2):
                    dve.wait_ge(score_mm, 2 * n + m + 1)
                    nc.vector.tensor_reduce(rowmax[:, n % 2, m:m + 1],
                                            PS[:, 2 * m:2 * m + 2, :].rearrange("p a b -> p (a b)")[:, 0:KEYS], AX, ALU.max)
                    dve.drain()
                    ts(negmax[:, n % 2, m:m + 1], rowmax[:, n % 2, m:m + 1], -DH ** -0.5, None, ALU.mult) \
                        .then_inc(negmax_ready, 1)

            maxima(0)
            for n in range(HEADS * TC):
                hd, qc, b = n // TC, n % TC, n % 2
                if n + 1 < HEADS * TC:
                    maxima(n + 1)
                dve.wait_ge(exp_done, 2 * n + 2)
                nc.vector.reciprocal(rsum[:, b, :], rowsum[:, b, :])
                dve.drain()
                tt(rneg[:, b, 1:2], rsum[:, b, 1:2], neglam, ALU.mult)
                dve.drain()
                ts(attn_t, probs[:, b, 1, :], rneg[:, b, 1:2], None, ALU.mult)
                dve.drain()
                if n >= 2:
                    dve.wait_ge(at_mm, n - 1)
                stt(attn_a[:, b, :], probs[:, b, 0, :], rsum[:, b, 0:1], attn_t, ALU.mult, ALU.add).then_inc(a_ready, 1)
                if qc == TC - 1:
                    dve.wait_ge(pv_mm, hd + 1)
                    nc.vector.tensor_copy(oT, PS[:, 6, :]).then_inc(o_ready, 1)
                    dve.wait_ge(oms_done, hd + 1)
                    ts(var, PS[:, 7, :], 1.0 / P, 1e-6, ALU.mult, ALU.add).then_inc(ovar_ready, 1)
                    dve.wait_ge(ostd_ready, hd + 1)
                    nc.vector.reciprocal(rstd, rstd)
                    dve.drain()
                    stt(h[:, hd, :], oT, gsub, rstd, ALU.mult, ALU.mult).then_inc(head_done, 1)

            for c in range(KC):
                dve.wait_ge(proj_mm, c + 1)
                stt(x[:, c, :], PS[:, c, :], mod1[:, 2 * KC + c:2 * KC + c + 1], x[:, c, :], ALU.mult, ALU.add).then_inc(x1_ready, 1)

            norm_var(2, T, 1e-6)
            norm_divide(2, x, h, T)
            dve.wait_ge(in_late, 32)
            dve.wait_ge(lg_mm, 1)

            def per_token(v, n):
                return v.unsqueeze(2).broadcast_to([P, TC, n])

            def first_max(v, n, peak, eq, ids, least, onehot):
                nc.vector.tensor_reduce(peak, v, AX, ALU.max)
                dve.drain()
                tt(eq, v, per_token(peak, n), ALU.is_equal)
                dve.drain()
                stt(ids, eq, -float(P), iota[:, 0:n].unsqueeze(1).broadcast_to([P, TC, n]), ALU.mult, ALU.add)
                dve.drain()
                nc.vector.tensor_reduce(least, ids, AX, ALU.min)
                dve.drain()
                tt(onehot, ids, per_token(least, n), ALU.is_equal)
                dve.drain()

            tt(logits, PS[:, 1, 0:TC * 36].rearrange("p (t n) -> p t n", n=36),
               b_router.unsqueeze(1).broadcast_to([P, TC, 36]), ALU.add)
            dve.drain()
            first_max(logits[:, :, 0:4], 4, g_max, g_eq, g_id, g_idx, g_hot)
            tt(g_exp, logits[:, :, 0:4], per_token(g_max, 4), ALU.subtract).then_inc(exp_in, 1)
            tt(e_all, logits[:, :, 4:36].rearrange("p t (g e) -> p t g e", e=EPG),
               g_hot.unsqueeze(3).broadcast_to([P, TC, 4, EPG]), ALU.mult)
            dve.drain()
            nc.vector.tensor_reduce(e_in, e_all.rearrange("p t g e -> p t e g"), AX, ALU.add)
            dve.drain()
            first_max(e_in, EPG, top1, e_eq, e_id, e_idx, e_hot[:, 0, :, :])
            stt(e_left, e_hot[:, 0, :, :], -1e30, e_in, ALU.mult, ALU.add)
            dve.drain()
            first_max(e_left, EPG, top2, e_eq, e_id, e_idx, e_hot[:, 1, :, :])
            tt(e2, top2, top1, ALU.subtract).then_inc(exp_in, 1)
            for k in range(2):
                tt(hot[:, k, :, :].rearrange("p t (g e) -> p t g e", e=EPG),
                   g_hot.unsqueeze(3).broadcast_to([P, TC, 4, EPG]),
                   e_hot[:, k, :, :].unsqueeze(2).broadcast_to([P, TC, 4, EPG]), ALU.mult)
            dve.drain()
            tt(chosen, hot[:, 0, :, :], hot[:, 1, :, :], ALU.add).then_inc(chosen_ready, 1)
            dve.wait_ge(exp_out, 2)
            nc.vector.tensor_reduce(g_sum, g_exp, AX, ALU.add)
            dve.wait_ge(exp_out, 3)
            ts(e_sum, e2, 1.0, None, ALU.add)
            dve.drain()
            tt(g_sum, g_sum, e_sum, ALU.mult)
            dve.drain()
            nc.vector.reciprocal(gates[:, 0, :], g_sum)
            dve.drain()
            tt(gates[:, 1, :], gates[:, 0, :], e2, ALU.mult)
            nc.vector.memset(ones_e, 1.0)
            dve.wait_ge(rank_mm, 1)
            count = PS[:, 6, TC * EXPERTS:(TC + 1) * EXPERTS]
            ts(n_blk, count, 0.0, None, ALU.is_gt)
            for n in range(1, TC):
                dve.drain()
                stt(n_blk, count, float(n * P), n_blk, ALU.is_gt, ALU.add)
            dve.drain()
            nc.vector.tensor_tensor_scan(blk_end, ones_e, n_blk, 0.0, ALU.mult, ALU.add)
            dve.drain()
            tt(blk_start, blk_end, n_blk, ALU.subtract)
            dve.drain()
            stt(place, blk_start.unsqueeze(1).broadcast_to([P, TC, EXPERTS]), float(P),
                PS[:, 6, 0:TC * EXPERTS].rearrange("p (t e) -> p t e", e=EXPERTS), ALU.mult, ALU.add)
            dve.drain()
            for k in range(2):
                tt(hot[:, k, :, :], hot[:, k, :, :], place, ALU.mult)
            dve.drain()
            nc.vector.tensor_reduce(dest, hot, AX, ALU.add)
            dve.drain()
            nc.vector.tensor_copy(slot_part[:, 0, :, :], dest)
            ts(slot_of[:], dest, float(P), None, ALU.add)
            dve.drain()
            ts(slot_part[:, 1, :, :], slot_part[:, 0, :, :], 7, None, ALU.arith_shift_right)
            dve.drain()
            ts(slot_part[:, 0, :, :], slot_part[:, 0, :, :], P - 1, None, ALU.bitwise_and)
            dve.drain()
            stt(slot_at[:], slot_part[:, 0, :, :], float(BLOCKS), slot_part[:, 1, :, :], ALU.mult, ALU.add)
            tt(blk_cmp, blk_end.unsqueeze(1).broadcast_to([P, BLOCKS, EXPERTS]),
               iota[:, 0:BLOCKS].unsqueeze(2).broadcast_to([P, BLOCKS, EXPERTS]), ALU.is_le)
            ts(pair_cmp, iota[:, 0:BLOCKS // 2], 2.0, blk_end[:, EXPERTS - 1:EXPERTS], ALU.mult, ALU.is_lt)
            dve.drain()
            nc.vector.tensor_reduce(blk_exp, blk_cmp, AX, ALU.add)
            nc.vector.tensor_reduce(n_pairs, pair_cmp, AX, ALU.add)
            nc.vector.memset(yb[:, 1, :], 0.0)
            dve.drain()
            ts(route_i[:, 0:BLOCKS], blk_exp, float(EXPERTS - 1), None, ALU.min)
            nc.vector.tensor_copy(route_i[:, BLOCKS:BLOCKS + 1], n_pairs)
            dve.drain()
            dve.sem_inc(route_ready, 1)

            pairs = dve.value_load(route_i[0:1, BLOCKS:BLOCKS + 1], min_val=1, max_val=BLOCKS // 2)
            for freed in (hid_ready, y_ready):
                dve.sem_inc(freed, 1)

            def hidden(i, s):
                dve.wait_ge(silu_done, i * 2 + (s + 1))
                dve.wait_ge(up_mm, i * 2 + (s + 3))
                tt(hid[:, s, :], silu_b[:, s, :], PS[:, 3, :], ALU.mult).then_inc(hid_ready, 1)

            def result(i, s):
                dve.wait_ge(down_mm, i * 2 + (s + 3))
                dve.wait_ge(y_stored[s], i * 16 + 16)
                nc.vector.tensor_copy(yb[:, s, :].rearrange("p (a b) -> p a b", a=2), PS[:, 5:7, :]).then_inc(y_ready, 1)

            with dve.Fori(0, pairs) as i:
                hidden(i, 0)
                result(i, 0)
                hidden(i, 1)
                result(i, 1)
            dve.wait_ge(moe_done, 1)
            for t in range(TC):
                dve.wait_ge(y_loaded, 32 * TC)
                if t >= 2:
                    dve.wait_ge(yT_mm, t - 1)
                ts(y_of[:, 0, t, :], y_of[:, 0, t, :], gates[:, 0, t:t + 1], None, ALU.mult)
                dve.drain()
                stt(ysum[:, t % 2, :], y_of[:, 1, t, :], gates[:, 1, t:t + 1], y_of[:, 0, t, :], ALU.mult, ALU.add) \
                    .then_inc(ysum_ready, 1)
                dve.wait_ge(yT_mm, t + 1)
                for c in range(KC):
                    xc = x[:, c, t * P:(t + 1) * P]
                    last = stt(xc, PS[:, 2 * (t % 2) + c // 4, (c % 4) * P:(c % 4 + 1) * P],
                               mod1[:, 5 * KC + c:5 * KC + c + 1], xc, ALU.mult, ALU.add)
                last.then_inc(yT_used, 1)
            dve.drain()
            dve.sem_inc(x2_ready, 1)
            norm_var(3, T, 1e-6)
            norm_divide(3, x, x, T)

            norm_var(4, T, 1e-5)
            norm_divide(4, x, h, T)
            re, im = col("lam_re", 0, S5_TILES), col("lam_im", 0, S5_TILES)

            def step(op, *args):
                op(*args)
                dve.drain()

            dve.wait_ge(dt_exp, 1)
            step(tt, s5_a, re, s5_dt, ALU.mult)
            step(tt, s5_th, im, s5_dt, ALU.mult)
            step(ts, s5_th, s5_th, 0.5, None, ALU.mult)
            step(ts, s5_k, s5_th, 1.0 / (2 * np.pi), ROUND, ALU.mult, ALU.add)
            step(ts, s5_k, s5_k, -ROUND, None, ALU.add)
            step(stt, s5_r, s5_k, -TWO_PI_HI, s5_th, ALU.mult, ALU.add)
            step(stt, s5_r, s5_k, -TWO_PI_LO, s5_r, ALU.mult, ALU.add)
            step(ts, s5_r, s5_r, PI_BELOW, -PI_BELOW, ALU.min, ALU.max)
            step(ts, s5_t, s5_r, -1.0, None, ALU.mult)
            step(tt, s5_ab, s5_r, s5_t, ALU.max)
            ts(s5_ab, s5_ab, -1.0, np.pi / 2, ALU.mult, ALU.add).then_inc(angle_ready, 1)
            dve.wait_ge(trig_ready, 1)
            step(tt, s5_s2, half_sin, half_sin, ALU.mult)
            step(ts, cos1, s5_s2, -2.0, 1.0, ALU.mult, ALU.add)
            step(stt, sin1, half_sin, 2.0, half_cos, ALU.mult, ALU.mult)
            step(stt, num_re, radius, -1.0, cos1, ALU.add, ALU.mult)
            step(stt, num_re, s5_s2, -2.0, num_re, ALU.mult, ALU.add)
            step(tt, num_im, radius, sin1, ALU.mult)
            step(tt, s5_den, re, re, ALU.mult)
            step(tt, s5_t, im, im, ALU.mult)
            step(tt, s5_den, s5_den, s5_t, ALU.add)
            step(nc.vector.reciprocal, s5_den, s5_den)
            step(tt, f_re, num_re, re, ALU.mult)
            step(tt, s5_t, num_im, im, ALU.mult)
            step(tt, f_re, f_re, s5_t, ALU.add)
            step(tt, f_re, f_re, s5_den, ALU.mult)
            step(tt, f_im, num_im, re, ALU.mult)
            step(tt, s5_t, num_re, im, ALU.mult)
            step(tt, f_im, f_im, s5_t, ALU.subtract)
            step(tt, f_im, f_im, s5_den, ALU.mult)
            dve.wait_ge(in_late, 64)
            ctmp = [v[:, 0:8, :].rearrange("p a n -> p (a n)").rearrange("p (t n) -> p t n", n=HP) for v in turn_t]
            for n, (part, f) in enumerate(((0, f_re), (1, f_im), (0, f_im), (1, f_re))):
                tt(ctmp[n], s5_c[:, :, part, :], f.unsqueeze(2).broadcast_to([P, S5_TILES, HP]), ALU.mult)
            dve.drain()
            tt(s5_cf[:, :, 0, :], ctmp[0], ctmp[1], ALU.subtract)
            step(tt, s5_cf[:, :, 1, :], ctmp[2], ctmp[3], ALU.add)
            ts(s5_cf[:, :, 1, :], s5_cf[:, :, 1, :], -1.0, None, ALU.mult).then_inc(c_ready, 1)
            nc.vector.tensor_copy(turn[:, 0, :, 0:1], cos1.unsqueeze(2))
            nc.vector.tensor_copy(turn[:, 1, :, 0:1], sin1.unsqueeze(2))
            n = 1
            while n < S5_Q:
                dve.drain()
                by = [turn[:, r, :, n - 1:n].broadcast_to([P, S5_TILES, n]) for r in range(2)]
                for k, (part, f) in enumerate(((0, 0), (1, 1), (0, 1), (1, 0))):
                    tt(turn_t[k][:, :, 0:n], turn[:, part, :, 0:n], by[f], ALU.mult)
                dve.drain()
                tt(turn[:, 0, :, n:2 * n], turn_t[0][:, :, 0:n], turn_t[1][:, :, 0:n], ALU.subtract)
                tt(turn[:, 1, :, n:2 * n], turn_t[2][:, :, 0:n], turn_t[3][:, :, 0:n], ALU.add)
                n *= 2
            dve.drain()
            dve.sem_inc(bu_used, 4)
            dve.sem_inc(s5_used, 1)
            dve.sem_inc(state_ready, 1)
            for part in range(2):
                tt(carry_by[:, part, :], turn[:, part, :, S5_Q - 1], radius, ALU.mult)
            dve.wait_ge(u_evac, KC)

            def add_feedthrough(q):
                dve.wait_ge(s5_mm, q * 4 + 6)
                stt(h[:, bass.ds(q, 1), :], uT[:, bass.ds(q, 1), :], cols[:, bass.ds(q + COLS["s5_d"][0], 1)],
                    PS[:, 6:7, :], ALU.mult, ALU.add).then_inc(s5_used, 1)

            def s5_quad(q, first_quad):
                def turns(a, r):
                    return turn[:, r, bass.ds(q * 4 + a, 1), :].broadcast_to([P, S5_NC, S5_Q])

                for a in range(4):
                    bu = [chunked(PS[:, 2 * (a % 3) + r, :]) for r in range(2)]
                    t = [chunked(rot[:, a % 2, n, :]) for n in range(4)]
                    if a < 2:
                        dve.wait_ge(g_added, q * 3 + (1 + a))
                    else:
                        dve.wait_ge(g_added, q * 3 + (a + 1))
                    dve.wait_ge(bu_mm, q * 4 + (4 + a + 1))
                    tt(t[0], bu[0], turns(a, 0), ALU.mult)
                    tt(t[1], bu[1], turns(a, 1), ALU.mult)
                    tt(t[2], bu[1], turns(a, 0), ALU.mult)
                    tt(t[3], bu[0], turns(a, 1), ALU.mult).then_inc(bu_used, 1)
                dve.drain()
                tt(scan_g[:, :, 6, :], t[0], t[1], ALU.add)
                tt(scan_g[:, :, 7, :], t[2], t[3], ALU.subtract)
                if not first_quad:
                    add_feedthrough(q - 1)
                dve.drain()
                dve.wait_ge(g_added, q * 3 + 5)
                dve.wait_ge(decay_set, q + 1)
                for c in range(S5_NC):
                    g = scan_g[:, c, :, :].rearrange("p n t -> p (n t)")
                    nc.vector.tensor_tensor_scan(g, decay_now.rearrange("p a r t -> p (a r t)"), g, 0.0, ALU.mult, ALU.add)
                    dve.drain()
                    if c < S5_NC - 1:
                        ends = [scan_g[:, c, r:8:2, S5_Q - 1] for r in range(2)]
                        by = [carry_by[:, r, bass.ds(q * 4, 4)] for r in range(2)]
                        for k, (part, f) in enumerate(((0, 0), (1, 1), (0, 1), (1, 0))):
                            tt(carry_t[:, k, :], ends[part], by[f], ALU.mult)
                        dve.drain()
                        tt(carry[:, :, 0], carry_t[:, 0, :], carry_t[:, 1, :], ALU.subtract)
                        tt(carry[:, :, 1], carry_t[:, 2, :], carry_t[:, 3, :], ALU.add)
                        dve.drain()
                        first = scan_g[:, c + 1, :, 0]
                        tt(first, first, carry.rearrange("p a r -> p (a r)"), ALU.add)
                        dve.drain()
                for a in range(4):
                    g = [scan_g[:, :, 2 * a + r, :] for r in range(2)]
                    t = [chunked(turned[:, a % 2, n, :]) for n in range(4)]
                    dve.wait_ge(s5_mm, q * 4 + (a + 1))
                    tt(t[0], g[0], turns(a, 0), ALU.mult)
                    stt(t[1], g[1], -1.0, turns(a, 1), ALU.mult, ALU.mult)
                    tt(t[2], g[0], turns(a, 1), ALU.mult)
                    tt(t[3], g[1], turns(a, 0), ALU.mult).then_inc(state_ready, 1)

            s5_quad(0, True)
            with dve.Fori(1, KC) as q:
                s5_quad(q, False)
            add_feedthrough(KC - 1)
            split_weights("glu", 0, 0)
            split_inputs(glu_lo, h, gelu_done, 0)
            split_weights("glu", 2, 1)
            for i in range(2):
                split_weights("glu", 4 + 2 * i, i)
                for n in range(4 * i, 4 * i + 4):
                    dve.wait_ge(gate_sig, n + 1)
                    stt(glu_t[:, n % 2, :], PS[:, n % 4, :], col("b_glu", n), glu_gate[:, n % 2, :], ALU.add, ALU.mult)
                    dve.drain()
                    stt(x[:, n, :], glu_t[:, n % 2, :], mod2[:, 0, 2 * KC + n:2 * KC + n + 1], x[:, n, :], ALU.mult, ALU.add) \
                        .then_inc(glu_used, 1)

            def mlp(layer, k_norm):
                name = f"mlp{layer}"
                norm_var(k_norm, T, 1e-5)
                split_weights(name, 0, 0)
                norm_divide(k_norm, x, mlp_h_lo, T)
                split_inputs(mlp_h_lo, h, h_ready, KC * k_norm + (KC if layer else 0))
                if layer == 0:
                    dve.sem_inc(mlp_added, 8)

                def quarter(i, last):
                    for t in range(4):
                        if t < 3 or not last:
                            split_weights(name, i * 8 + 2 * (t + 1), (t + 1) % 2)
                        if layer == 0:
                            dve.wait_ge(ada_loaded[t % 2], i * 32 + 16 * (ADA_TILES + t // 2 + 1))
                            for n in range(3):
                                w = ada_buf1[t % 2][:, n, :]
                                last_mod = stt(w, w, 1.0, cond2[:], ALU.mult, ALU.mult,
                                               accum_out=mod2[:, 1, bass.ds(i * 12 + (3 * t + n), 1)])
                            last_mod.then_inc(ada_used, 1)
                        if t < 2:
                            for n in range(4 * t, 4 * t + 4):
                                dve.wait_ge(mlp1_mm, i * 8 + (32 * layer + n + 1))
                                ts(mlp_lo[:, n, :], PS[:, n, :], 0.0, None, ALU.max).then_inc(relu_done, 1)
                            for n in range(4 * t, 4 * t + 4):
                                dve.wait_ge(sqr_done, i * 8 + (32 * layer + n + 1))
                                tt(f32r(mlp_lo[:, n, :]), mlp_lo[:, n, :], f32r(mlp_hi[:, n, :]), ALU.subtract).then_inc(mlp_split, 1)
                        else:
                            for n in range(4 * t - 8, 4 * t - 4):
                                dve.wait_ge(mlp2_mm, i * 8 + (32 * layer + n + 1))
                                stt(x[:, n, :], PS[:, n, :], mod2[:, layer, 5 * KC + n:5 * KC + n + 1], x[:, n, :], ALU.mult,
                                    ALU.add).then_inc(mlp_added, 1)

                with dve.Fori(0, 3) as i:
                    quarter(i, False)
                quarter(3, True)
                if layer == 0:
                    dve.drain()
                    tt(mod2[:, 1, :], mod2[:, 1, :], col("ada_b1", 0, 48), ALU.add)
                    dve.drain()
                    norm_gain(5, mod2[:, 1, KC:2 * KC], "nmix1")
                    norm_gain(6, mod2[:, 1, 4 * KC:5 * KC], "nmlp1")
                    dve.drain()

            mlp(0, 5)

            norm_var(6, T, 1e-5)
            split_weights("xbc", 0, 0)
            norm_divide(6, x, xbc_h_lo, T)
            split_inputs(xbc_h_lo, h, h_ready, KC * 6)
            dve.sem_inc(conv_done, 8)

            def convolution(i, last_pair):
                def tap(n, k):
                    return cols[:, bass.ds(i * 8 + (COLS["conv_w"][0] + M2_CC * n + k), 1)]

                for s in range(2):
                    if s == 0 or not last_pair:
                        split_weights("xbc", i * 4 + 2 * (s + 1), 1 - s)
                    for k in range(4 * s, 4 * s + 4):
                        dve.wait_ge(xbc_mm, i * 8 + (k + 1))
                        ts(xs[:, bass.ds(i * 8 + k, 1), :], PS[:, k:k + 1, :], tap(3, k), None, ALU.mult)
                        for back in range(1, 4):
                            dve.drain()
                            late = xs[:, bass.ds(i * 8 + k, 1), back:T]
                            last = stt(late, PS[:, k:k + 1, 0:T - back], tap(3 - back, k), late, ALU.mult, ALU.add)
                        last.then_inc(conv_done, 1)

            with dve.Fori(0, 2) as i:
                convolution(i, False)
            convolution(2, True)
            for c in range(KC):
                last = tt(h[:, c, :], f32r(h[:, c, :]), f32r(xbc_h_lo[:, c, :]), ALU.add)
            last.then_inc(step_dve, 1)
            dve.wait_ge(dt_mm, 1)
            ts(dt_raw, PS[0:M2_HEADS, 0, :], col("dt_bias")[0:M2_HEADS, :], None, ALU.add).then_inc(step_dve, 1)
            nc.vector.memset(state, 0.0)
            nc.vector.memset(z_silu[0:M2_HEADS, 0, :], 1.0)
            dve.wait_ge(step_act, 1)
            step(stt, dt_t, dt_raw, 0.0, dt_abs, ALU.max, ALU.add)
            step(ts, a_dt, dt_t, a_pos, -1.0, ALU.mult, ALU.mult)
            for c in range(M2_NC):
                at = slice(c * M2_Q, (c + 1) * M2_Q)
                nc.vector.tensor_tensor_scan(a_cs[:, at], z_silu[0:M2_HEADS, 0, at], a_dt[:, at], 0.0, ALU.mult, ALU.add)
            dve.drain()
            for c in range(M2_NC):
                last = ts(last_diag[:, c, :], eye[0:M2_HEADS, 0:M2_HEADS], a_cs[:, (c + 1) * M2_Q - 1:(c + 1) * M2_Q], None,
                          ALU.mult)
            last.then_inc(step_dve, 1)
            dve.wait_ge(tok_mm, 1)
            by_token = PS[:, 1, 0:2 * M2_NC * M2_HEADS].rearrange("p (n c h) -> p n c h", c=M2_NC, h=M2_HEADS)
            nc.vector.tensor_copy(dt_tok, by_token[:, 0, :, :])
            step(ts, cs_neg, by_token[:, 1, :, :], -1.0, None, ALU.mult)
            nc.vector.tensor_copy(eye16, eye)
            ts(mask16, causal, -1.0, 1e30, ALU.add, ALU.mult)
            tt(dec_tok, PS[:, 2, 0:M2_NC * M2_HEADS].rearrange("p (c h) -> p c h", h=M2_HEADS), cs_neg, ALU.add) \
                .then_inc(step_dve, 1)
            dve.wait_ge(step_act, 2)
            dve.sem_inc(m_ready, 2)
            dve.sem_inc(y_tok_evac, 1)
            dve.sem_inc(y_added, 1)
            dve.sem_inc(state_new, 1)
            with dve.Fori(0, M2_NC) as c:
                def heads(v, first, count):
                    return v[:, bass.ds(c, 1), first:first + count].rearrange("p c h -> p (c h)")

                for b in range(4):
                    dve.wait_ge(xs_tok_mm, c * 4 + (b + 1))
                    tt(xdt[:, b * 512:(b + 1) * 512].rearrange("p (h n) -> p h n", n=64),
                       PS[:, b, :].rearrange("p (h n) -> p h n", n=64),
                       heads(dt_tok, 8 * b, 8).unsqueeze(2).broadcast_to([P, 8, 64]), ALU.mult).then_inc(xdt_ready, 1)
                for g in range(M2_G):
                    dve.wait_ge(off_mm, c * 4 + (g + 1))
                    tt(y_off[:, g * 512:(g + 1) * 512].rearrange("p (h n) -> p h n", n=64),
                       PS[:, g, :].rearrange("p (h n) -> p h n", n=64),
                       heads(exp_cs_tok, 8 * g, 8).unsqueeze(2).broadcast_to([P, 8, 64]), ALU.mult).then_inc(off_used, 1)
                dve.wait_ge(cb_mm, c + 1)

                def weights(q):
                    dve.wait_ge(decay_ready, c * 8 + (q + 1))
                    dve.wait_ge(y7_mm, c * 8 + (q + 1))
                    g = q // 2
                    tt(m_now[:, q % 2, :, :], decay[:, q % 2, :, :],
                       PS[:, 5, g * P:(g + 1) * P].unsqueeze(1).broadcast_to([P, 4, P]), ALU.mult).then_inc(m_ready, 1)

                def sum_y(q):
                    dve.wait_ge(y7_mm, c * 8 + (q + 3))
                    dve.wait_ge(y_turned, c * 8 + (q + 1))
                    tt(y_tok[:, q % 2, :], PS[:, 7, 0:2 * P], y_off[:, q * 256:(q + 1) * 256], ALU.add).then_inc(y_tok_evac, 1)

                def add_y(q):
                    dve.wait_ge(y_turned, c * 8 + (q + 3))
                    for j in range(2):
                        n = 2 * q + j
                        xc = xs[:, n, bass.ds(c * M2_Q, M2_Q)]
                        last = stt(xc, xc, col("m2_d", n), PS[:, 4, j * P:(j + 1) * P], ALU.mult, ALU.add)
                    last.then_inc(y_added, 1)

                weights(0)
                for q in range(8):
                    if q < 7:
                        weights(q + 1)
                    sum_y(q)
                    if q == 0:
                        tt(xdt_dec.rearrange("p (h n) -> p h n", n=64), xdt.rearrange("p (h n) -> p h n", n=64),
                           heads(dec_tok, 0, M2_HEADS).unsqueeze(2).broadcast_to([P, M2_HEADS, 64]), ALU.mult) \
                            .then_inc(xdt_dec_ready, 1)
                    if q:
                        add_y(q - 1)
                add_y(7)
                dve.wait_ge(st_mm, c + 1)
                tt(state.rearrange("p (h n) -> p h n", n=64), state.rearrange("p (h n) -> p h n", n=64),
                   heads(dec_chunk, 0, M2_HEADS).unsqueeze(2).broadcast_to([P, M2_HEADS, 64]), ALU.mult)
                dve.drain()
                for g in range(M2_G):
                    part = state[:, g * 512:(g + 1) * 512]
                    last = tt(part, part, PS[:, g, :], ALU.add)
                last.then_inc(state_new, 1)
            dve.drain()
            dve.sem_inc(z_used, 2)
            split_weights("z", 0, 0)
            split_inputs(h, z_h_hi, h_ready, 7 * KC)
            for t in range(4):
                if t < 3:
                    split_weights("z", 2 * (t + 1), (t + 1) % 2)
                for n in range(4 * t, 4 * t + 4):
                    dve.wait_ge(z_ready, 8 + n + 1)
                    tt(xs[:, n, :], xs[:, n, :], z_silu[:, n % 2, :], ALU.mult).then_inc(z_used, 1)
            for s in range(2):
                split_weights("m2_out", 2 * s, s)
            for g in range(M2_G):
                dve.wait_ge(oms_done, HEADS + g + 1)
                ts(var, PS[:, g, :], 1.0 / 512, 1e-5, ALU.mult, ALU.add).then_inc(ovar_ready, 1)
                dve.wait_ge(ostd_ready, HEADS + g + 1)
                nc.vector.reciprocal(rstd, rstd)
                dve.drain()
                for j in range(4):
                    n = 4 * g + j
                    stt(y_lo[:, n, :], xs[:, n, :], col("m2_norm", n), rstd, ALU.mult, ALU.mult).then_inc(yn_ready, 1)
                for n in range(4 * g, 4 * g + 4):
                    dve.wait_ge(y_hi_ready, n + 1)
                    tt(f32r(y_lo[:, n, :]), y_lo[:, n, :], f32r(xs[:, n, :]), ALU.subtract).then_inc(lo_ready, 1)
            for s in range(2):
                split_weights("m2_out", 4 + 2 * s, s)
            for n in range(KC):
                dve.wait_ge(proj_mm, 2 * KC + n + 1)
                stt(x[:, n, :], PS[:, n, :], mod2[:, 1, 2 * KC + n:2 * KC + n + 1], x[:, n, :], ALU.mult, ALU.add) \
                    .then_inc(x5_ready, 1)
            mlp(1, 7)
            norm_var(8, T, 1e-5)
            norm_divide(8, x, x, T)


def _constants():
    f = np.float32
    p = np.arange(P)
    rot = np.zeros((P, P), f)
    for m in range(P):
        rot[m + 16 if m % 32 < 16 else m - 16, m] = -1.0 if m % 32 < 16 else 1.0
    mats = np.stack([np.eye(P, dtype=f), (p[:, None] < p[None, :]).astype(f), (p[:, None] <= p[None, :]).astype(f), rot], 1)
    t = np.arange(T)
    pos = np.stack([t // 64, t % 64], -1).astype(f)
    axis = DH // 2
    freq = (f(10000.0) ** (-np.arange(0, axis, 2, dtype=f) / f(axis))).astype(f)
    ang = (pos[:, :, None] * freq).astype(f)
    ang = np.concatenate([ang, ang], -1).reshape(T, DH)
    ang = np.concatenate([ang, ang], -1).T
    tt = 2 * np.pi * ((t[:, None] * t[None, :]) % T) / T
    cc = 2 * np.pi * ((p[:, None] * p[None, :]) % P) / P
    ortho = 1.0 / np.sqrt(T * P)

    def token_rows(a):
        return np.ascontiguousarray(a.astype(f).reshape(TC, P, T).transpose(1, 0, 2))

    return {
        "mats": mats, "rope_c": np.cos(ang).astype(f), "rope_s": np.sin(ang).astype(f),
        "dft_c": token_rows(np.cos(tt) * ortho), "dft_s": token_rows(-np.sin(tt) * ortho),
        "dft_ch": np.concatenate([np.cos(cc), np.sin(cc)], 1).astype(f),
        "iota": np.tile(np.arange(64, dtype=f), (P, 1)),
        "tokid": (p[:, None] + P * np.arange(TC)[None, :]).astype(np.uint32),
    }


def _layout(a):
    def chunks(v):
        return np.asarray(v).reshape(-1, P).T

    def features(m):
        m = np.asarray(m)
        return m.T.reshape(-1, P, m.shape[0]).transpose(1, 0, 2)

    def rows(w):
        return np.asarray(w).reshape(-1, P, w.shape[-1]).transpose(1, 0, 2)

    def padded(v):
        return np.concatenate([np.asarray(v), np.zeros(P - len(v), np.float32)])[:, None]

    def states(v):
        return np.asarray(v).reshape(S5_TILES, P).T

    packed = {
        "b_ada": chunks(a["b_ada"][0]), "ada_b0": chunks(a["ada_b_2"][0]), "ada_b1": chunks(a["ada_b_2"][1]),
        "g_mix": chunks(a["g_mix_norm"][0]), "g_ffn": chunks(a["g_ffn_norm"][0]), "g_final": chunks(a["g_final"]),
        "g_subln": chunks(a["g_subln"][0]), "nmix0": chunks(a["norm_mix_g_2"][0]), "nmix1": chunks(a["norm_mix_g_2"][1]),
        "nmlp0": chunks(a["norm_mlp_g_2"][0]), "nmlp1": chunks(a["norm_mlp_g_2"][1]), "s5_d": chunks(a["s5_d_2"][0]),
        "b_glu": chunks(a["s5_b_glu_2"][0]),
        "conv_w": np.concatenate([chunks(a["m2_conv_w_2"][0][k]) for k in range(4)], 1),
        "conv_b": chunks(a["m2_conv_b_2"][0]), "m2_d": chunks(np.repeat(np.asarray(a["m2_d_2"][0]), 64)),
        "m2_norm": chunks(a["m2_norm_g_2"][0]), "fin": chunks(a["final_norm_g_2"]),
        "dt_bias": padded(a["m2_dt_bias_2"][0]), "a_log": padded(a["m2_a_log_2"][0]),
        "lam_re": states(a["s5_lambda_re_2"][0]), "lam_im": states(a["s5_lambda_im_2"][0]),
        "log_dt": states(np.repeat(np.asarray(a["s5_log_dt_2"][0])[:, None], 64, 1)),
    }
    s5_b = np.zeros((4, 2, HP, 8, 2, 2, 64), np.float32)
    s5_c = np.empty((2, 64, S5_TILES, 2, HP), np.float32)
    for r, (bname, cname) in enumerate((("s5_b_re_2", "s5_c_re_2"), ("s5_b_im_2", "s5_c_im_2"))):
        b = np.asarray(a[bname][0]).reshape(8, 4, 2, 64, HP)
        for g in range(2):
            s5_b[:, g, :, :, r, g, :] = b[:, :, g].transpose(1, 3, 0, 2)
        s5_c[:, :, :, r, :] = np.asarray(a[cname][0]).reshape(S5_TILES, 2, HP, 64).transpose(1, 3, 0, 2)
    m2_in = np.asarray(a["m2_w_in_2"][0])
    lams = np.stack([a[n][0] for n in ("lambda_q1", "lambda_k1", "lambda_q2", "lambda_k2")])
    return {
        "xT": features(a["x"][0]), "ctxT": features(a["ctx"][0]),
        "c_rows": np.stack([a["c"][0], a["c_ctx"], a["c_2"][0]]),
        "cols": np.concatenate([packed[n] for n in COLS], 1),
        "lam4": np.tile(lams[None], (P, 1, 1)),
        "w_adaT": np.asarray(a["w_ada"][0]).T, "ada_w_2T": np.asarray(a["ada_w_2"]).transpose(0, 2, 1),
        "w_in": a["w_in"][0], "w_out": a["w_out"][0],
        "wfour": np.asarray(a["w_fourier"][0]).transpose(1, 0, 2),
        "w_router": rows(np.concatenate([a["w_router_group"][0], a["w_router_expert"][0]], 1)),
        "b_router": np.tile(np.concatenate([a["b_router_group"][0], a["b_router_expert"][0]])[None], (P, 1)),
        "w_gate": a["w_gate"][0], "w_up": a["w_up"][0], "w_down": a["w_down"][0],
        "s5_w_in": a["s5_w_in_2"][0], "s5_b": s5_b.reshape(P, 8, 2, P), "s5_c": s5_c.reshape(P, S5_TILES, 2, HP),
        "w_glu": a["s5_w_glu_2"][0], "mlp_w1": a["mlp_w1_2"], "mlp_w2": a["mlp_w2_2"],
        "m2_w_in": m2_in, "m2_w_dt": rows(m2_in[:, M2_IN + M2_XBC:]), "m2_w_out": a["m2_w_out_2"][0],
    }


def kernel(**inputs):
    import concourse.bacc as bacc
    from concourse.bass_utils import run_bass_kernel_spmd

    nc = bacc.Bacc("TRN2", target_bir_lowering=False, num_devices=1)
    arrays = {name: np.ascontiguousarray(v) for name, v in {**_layout(inputs), **_constants()}.items()}
    handles = {name: nc.dram_tensor(f"in_{name}", v.shape, mybir.dt.from_np(v.dtype), kind="ExternalInput").ap()
               for name, v in arrays.items()}
    out = nc.dram_tensor("outT", [P, KC, T], F32, kind="ExternalOutput").ap()
    build(nc, handles, out)
    r = run_bass_kernel_spmd(nc, [{f"in_{name}": v for name, v in arrays.items()}], core_ids=[0])
    got = np.asarray(r.results[0]["outT"])
    return got.transpose(2, 1, 0).reshape(1, T, D)
```

```python
from contextlib import ExitStack

import numpy as np

import concourse.bass as bass
from concourse import mybir

F32 = mybir.dt.float32
F32R = mybir.dt.float32r
BF16 = mybir.dt.bfloat16
I32 = mybir.dt.int32
U32 = mybir.dt.uint32
ALU = mybir.AluOpType
ACT = mybir.ActivationFunctionType
AX = mybir.AxisListType.X

P = 128
D = 1024
KC = D // P
T = 512
TC = T // P
CTX = 256
KEYS = CTX + T
KCH = KEYS // P
HEADS = 4
DH = 64
GROUPS = 4
EPG = 8
EXPERTS = GROUPS * EPG
DE = 512
BLOCKS = T * 2 // P + EXPERTS
NMOD = 6
TN = 512
ADA_TILES = NMOD * KC // 4
MOD_EARLY = 2 * KC
ADA_LATE = ADA_TILES - MOD_EARLY // 4
DFF = 4096
NORM_BANKS = (0, 1, 0, 1, 0, 0, 0, 0, 0)
LAMBDA_INIT = 0.8 - 0.6 * 1.0
S5_TILES = 32
S5_Q = 128
S5_NC = T // S5_Q
ROUND = 1.5 * 2.0 ** 23
TWO_PI_HI = 6.28125
TWO_PI_LO = 2 * np.pi - TWO_PI_HI
PI_BELOW = 3.1415925
HP = 16
M2_IN = 2048
M2_XBC = 3072
M2_HEADS = 32
M2_XC = M2_IN // P
M2_CC = M2_XBC // P
M2_G = 4
M2_Q = 128
M2_NC = T // M2_Q
SUM_BANKS = (6, 0, 1, 2, 3)

COLS = {}
for _name, _count in (
    ("b_ada", 48), ("ada_b0", 48), ("ada_b1", 48), ("g_mix", 8), ("g_ffn", 8), ("g_final", 8), ("g_subln", 1),
    ("nmix0", 8), ("nmix1", 8), ("nmlp0", 8), ("nmlp1", 8), ("s5_d", 8), ("b_glu", 16), ("conv_w", 96),
    ("conv_b", 24), ("m2_d", 16), ("m2_norm", 16), ("fin", 8), ("dt_bias", 1), ("a_log", 1),
    ("lam_re", 32), ("lam_im", 32), ("log_dt", 32),
):
    COLS[_name] = (sum(n for _, n in COLS.values()), _count)
NCOLS = sum(n for _, n in COLS.values())


def build(nc, A, out):
    with ExitStack() as ctx:
        def sb(name, shape, dt=F32):
            return ctx.enter_context(nc.sbuf_tensor(name, shape, dt))

        TWIN = KC * T

        def sb_twice(name, shape):
            at, n = -(-nc.sbuf_base // 32) * 32, int(np.prod(shape[1:]))
            return sb(name, shape), [nc.alloc_sbuf_tensor_at(f"{name}_f32r{k}", [P, TWIN], F32R, offset=at + 4 * k * TWIN)
                                     for k in range(n // TWIN)]

        def sem(name):
            return ctx.enter_context(nc.semaphore(name))

        PS = ctx.enter_context(nc.psum_tensor("PS", [P, 8, 512], F32))
        ring, ring_r = sb_twice("ring", [P, 2, KC, TN])
        work, work_r = sb_twice("work", [P, 32768])
        x = sb("x", [P, KC, T])
        h, h_r = sb_twice("h", [P, KC, T])
        cols = sb("cols_sb", [P, NCOLS])
        cond2 = sb("cond2", [P, D])
        mats = sb("mats_sb", [P, 4, P])
        ones = sb("ones", [P, P])
        mod1 = sb("mod1", [P, NMOD * KC])
        modc = sb("modc", [P, 2 * KC])
        mod2 = sb("mod2", [P, 2, NMOD * KC])
        gain = sb("gain", [P, 7, KC])
        norm_buf = sb("norm_buf", [P, 2 * T])
        var, rstd = norm_buf[:, 0:T], norm_buf[:, T:2 * T]
        iota = sb("iota_sb", [P, 64])
        tokid = sb("tokid_sb", [P, TC], U32)
        route_i = sb("route_i", [P, 64], I32)
        slot_of = sb("slot_of", [P, 2, TC], I32)
        gates = sb("gates", [P, 2, TC])
        eye, tri, causal, rope_rot = (mats[:, n, :] for n in range(4))

        def wk(at, *shape):
            n = int(np.prod(shape))
            v = work[:, at:at + n]
            if len(shape) == 2:
                return v.rearrange("p (a b) -> p a b", b=shape[1])
            if len(shape) == 3:
                return v.rearrange("p (a b c) -> p a b c", b=shape[1], c=shape[2])
            return v

        def col(name, n=0, count=1):
            first = COLS[name][0] + n
            return cols[:, first:first + count]

        qT, kT, vtok, fT, cx = wk(0, 4, T), wk(2048, 4, KEYS), wk(5120, KCH, 512), wk(8192, 4, T), wk(10240, KC, CTX)
        rope_c, rope_s = wk(12288, T), wk(12800, T)
        dft_c, dft_s, dft_ch = wk(13312, TC, T), wk(15360, TC, T), wk(17408, 256)
        fab, fre = wk(17664, 2, 4, 256), wk(19712, T)
        attn_a, attn_t = wk(20224, 2, KEYS), wk(21760, KEYS)
        x1_sq = wk(0, KC, T)
        aT = [wk(22528, KCH, T), wk(13312, KCH, T)]
        oT, oSq = wk(25600, T), wk(26112, T)
        rope_t = wk(28672, 2, 2, T)
        probs = wk(28672, 2, 2, KEYS)
        ada_buf = [wk(20224, 4, D), wk(24320, 4, D)]
        cond1 = wk(28672, D)
        c_cols = wk(30848, KC, 2)
        w_early = [wk(2048, KC, TN), wk(6144, KC, TN), wk(20224, KC, TN), wk(24320, KC, TN)]
        mod_rows = wk(17664, MOD_EARLY // 4, TN)[0:2]
        lam_t = wk(30720, 2, 64)
        wfour = wk(31744, GROUPS, P)
        lam4 = wk(32256, 4, 64)
        csq = wk(0, KC, CTX)
        sm = sb("sm", [P, 64])
        rowmax, negmax, rowsum, rsum = (sm[:, 4 * n:4 * n + 4].rearrange("p (a b) -> p a b", b=2) for n in range(4))
        lam_d, neglam = sm[:, 24:28], sm[:, 28:29]
        gsub = sm[:, 29:30]

        expert_w = [(ring[:, 0, :, :], ring[:, 1, :, :], wk(0, 4, D)),
                    (wk(4096, KC, DE), wk(8192, KC, DE), wk(12288, 4, D))]
        xb, xbT, silu_b = wk(16384, 2, D), wk(18432, 2, KC, P), wk(20480, 2, DE)
        hid, hidT, yb = wk(21504, 2, DE), wk(22528, 2, 4, P), wk(23552, 2, D)
        hrow = wk(25600, 2, D)
        y_of = wk(0, 2, TC, D)
        ysum = wk(16384, 2, D)
        routing_at = [27648]

        def rt(*shape):
            n = int(np.prod(shape))
            routing_at[0] += n
            return wk(routing_at[0] - n, *shape)

        w_router, b_router = rt(KC, GROUPS + EXPERTS), rt(GROUPS + EXPERTS)
        logits, g_exp, g_eq, g_id, g_hot = rt(TC, GROUPS + EXPERTS), rt(TC, 4), rt(TC, 4), rt(TC, 4), rt(TC, 4)
        e_all, e_in, e_eq, e_id, e_hot = rt(TC, 4, EPG), rt(TC, EPG), rt(TC, EPG), rt(TC, EPG), rt(2, TC, EPG)
        e_left, hot, chosen = rt(TC, EPG), rt(2, TC, EXPERTS), rt(TC, EXPERTS)
        place, n_blk, blk_end, blk_start, ones_e = (rt(TC, EXPERTS), rt(EXPERTS), rt(EXPERTS), rt(EXPERTS), rt(EXPERTS))
        blk_cmp, blk_exp, pair_cmp, n_pairs = rt(BLOCKS, EXPERTS), rt(BLOCKS), rt(BLOCKS // 2), rt(1)
        g_max, g_sum, g_idx, top1, top2, e_idx = (rt(TC) for _ in range(6))
        e2, e_sum, dest = rt(TC), rt(TC), rt(2, TC)
        assert routing_at[0] <= 32768
        idx_all = sb("idx_all", [P, BLOCKS], U32)
        idx = [sb(f"idx{s}", [P, 1], U32) for s in range(2)]
        slot_at = sb("slot_at", [P, 2, TC], U32)
        slot_part = sb("slot_part", [P, 2, 2, TC], I32)
        zeros = sb("zeros", [P, 256])
        h_rows = nc.dram_tensor("h_rows", [T + 1, D], F32, kind="Internal").ap()
        slot_tok = nc.dram_tensor("slot_tok", [P * BLOCKS, 1], U32, kind="Internal").ap()
        y_rows = nc.dram_tensor("y_rows", [(BLOCKS + 2) * P, D], F32, kind="Internal").ap()

        turn = wk(0, 2, S5_TILES, S5_Q)
        uT, s5_b, s5_c, s5_cf = wk(8192, KC, T), wk(12288, KC, 2, P), wk(14336, S5_TILES, 2, HP), wk(15360, S5_TILES, 2, HP)
        scan_g, rot, turned = wk(16384, S5_NC, 8, S5_Q), wk(20480, 2, 4, T), wk(24576, 2, 4, T)
        turn_t = [wk(16384 + 2048 * n, S5_TILES, 64) for n in range(4)]
        u_now, b_now, c_now = wk(28672, T), wk(29184, 2, P), wk(29440, 4, 288)
        s5_at = [30592]

        def s5p():
            s5_at[0] += S5_TILES
            return wk(s5_at[0] - S5_TILES, S5_TILES)

        (s5_dt, s5_a, s5_th, s5_k, s5_r, s5_ab, radius, half_sin, half_cos, s5_s2, cos1, sin1, num_re, num_im, f_re, f_im,
         s5_den, s5_t) = (s5p() for _ in range(18))
        carry, carry_t = wk(s5_at[0], 4, 2), wk(s5_at[0] + 8, 4, 4)
        carry_by = wk(s5_at[0] + 32, 2, S5_TILES)
        decay_now = wk(s5_at[0] + 96, 4, 2, S5_Q)
        glu_gate, glu_t = wk(0, 2, T), wk(1024, 2, T)
        ring_hi = wk(20480, 2, KC, TN)
        glu_lo, glu_sq = wk(8192, KC, T), wk(4096, KC, T)
        mlp_hi, mlp_lo, mlp_h_lo = wk(0, KC, T), wk(4096, KC, T), wk(8192, KC, T)
        ada_buf1 = [wk(12288, 3, D), wk(15360, 3, D)]
        xs, xs_now = wk(0, M2_CC, T), wk(12288, M2_CC, P)
        xdt, xdt_dec, state, b_tok = wk(15360, M2_IN), wk(17408, M2_IN), wk(19456, M2_IN), wk(21504, M2_G, P)
        decay, m_now = wk(22528, 2, 4, P), wk(23552, 2, 4, P)
        y_off, y_tok = wk(24576, M2_IN), wk(26624, 2, 2 * P)
        dt_t, a_dt, a_cs, dt_raw, dt_abs = (wk(27136 + 512 * n, T)[0:M2_HEADS, :] for n in range(5))
        cs_neg, dt_tok, dec_tok, dec_chunk = (wk(29696 + 128 * n, M2_NC, M2_HEADS) for n in range(4))
        last_diag = wk(30208, M2_NC, M2_HEADS)[0:M2_HEADS, :, :]
        w_dt = wk(30336, KC, M2_HEADS)
        z_silu = wk(31616, 2, T)
        a_pos, sums_now = wk(30592, 1)[0:M2_HEADS, :], wk(30596, M2_Q)[0:M2_HEADS, :]
        xbc_h_lo, z_h_hi = wk(12288, KC, T), wk(12288, KC, T)
        exp_cs_tok = wk(30728, M2_NC, M2_HEADS)
        eye16, mask16 = wk(30856, 64).bitcast(BF16), wk(30920, 64).bitcast(BF16)
        m2_sq, y_lo, m2_rstd = wk(16384, 8, T), wk(12288, M2_XC, T), wk(28672, M2_G, T)

        twins = {"ring": ring_r, "work": work_r, "h": h_r}

        def f32r(v):
            return bass.AP(twins[v.tensor.name][v.offset // TWIN], v.offset % TWIN, [(TWIN, P), *v.ap[1:]])

        def turned_back(a):
            return rot[:, 0, :, :] if a == 2 else turned[:, a % 3, :, :]

        def chunked(v):
            return v.rearrange("p (c t) -> p c t", t=S5_Q)

        in_cond, in_small, in_x, in_mix, in_late = (sem(n) for n in ("in_cond", "in_small", "in_x", "in_mix", "in_late"))
        tile_loaded = [sem(f"tile_loaded{n}") for n in range(4)]
        tile_used = sem("tile_used")
        w_hi, w_split, lo_ready = sem("w_hi"), sem("w_split"), sem("lo_ready")
        ada_loaded, ada_used = [sem("ada_loaded0"), sem("ada_loaded1")], sem("ada_used")
        consts_set, cond_ready, mods_ready = sem("consts_set"), sem("cond_ready"), sem("mods_ready")
        in_ctx, in_rows, in_mod = sem("in_ctx"), sem("in_rows"), [sem(f"in_mod{n}") for n in range(4)]
        mod_mm, mod_evac, mod_turned = (sem(n) for n in ("mod_mm", "mod_evac", "mod_turned"))
        sq_ready, ms_done, var_ready, std_ready = sem("sq_ready"), sem("ms_done"), sem("var_ready"), sem("std_ready")
        xn_ready, h_ready = sem("xn_ready"), sem("h_ready")
        exp_in, exp_out = sem("exp_in"), sem("exp_out")
        proj_mm = sem("proj_mm")
        qkv_mm, qkv_evac, rope_mm, rope_done = sem("qkv_mm"), sem("qkv_evac"), sem("rope_mm"), sem("rope_done")
        ab_mm, ab_evac, fr_mm, fr_evac = sem("ab_mm"), sem("ab_evac"), sem("fr_mm"), sem("fr_evac")
        fo_mm, fo_evac = sem("fo_mm"), sem("fo_evac")
        score_mm, negmax_ready, exp_done, a_ready = sem("score_mm"), sem("negmax_ready"), sem("exp_done"), sem("a_ready")
        at_mm, at_evac, pv_mm, o_ready = sem("at_mm"), sem("at_evac"), sem("pv_mm"), sem("o_ready")
        osq_ready, oms_done, ovar_ready, ostd_ready = sem("osq_ready"), sem("oms_done"), sem("ovar_ready"), sem("ostd_ready")
        head_done, x1_ready, out_stored = sem("head_done"), sem("x1_ready"), sem("out_stored")
        idx_filled, zero_row, route_mm = sem("idx_filled"), sem("zero_row"), sem("route_mm")
        hrow_mm, hrow_evac, hrow_stored = sem("hrow_mm"), sem("hrow_evac"), [sem("hrow_stored0"), sem("hrow_stored1")]
        chosen_ready, route_ready = sem("chosen_ready"), sem("route_ready")
        idx_set, idx_stored, idx_loaded = sem("idx_set"), sem("idx_stored"), sem("idx_loaded")
        gate_loaded, up_loaded, down_loaded, xb_loaded, y_stored = (
            [sem(f"{n}{s}") for s in range(2)] for n in ("gate_loaded", "up_loaded", "down_loaded", "xb_loaded", "y_stored"))
        xT_mm, xT_evac, gate_mm, up_mm, silu_done = sem("xT_mm"), sem("xT_evac"), sem("gate_mm"), sem("up_mm"), sem("silu_done")
        hid_ready, hT_mm, hT_evac, down_mm, y_ready = sem("hid_ready"), sem("hT_mm"), sem("hT_evac"), sem("down_mm"), sem("y_ready")
        moe_done, y_loaded, ysum_ready, yT_mm, yT_used = sem("moe_done"), sem("y_loaded"), sem("ysum_ready"), sem("yT_mm"), sem("yT_used")
        y_zeroed, x2_ready = sem("y_zeroed"), sem("x2_ready")
        u_evac = sem("u_evac")
        c_zero, c_ready, ub_staged, c_staged = (sem(n) for n in ("c_zero", "c_ready", "ub_staged", "c_staged"))
        bu_mm, bu_used, state_ready, s5_mm, s5_used, gelu_done = (
            sem(n) for n in ("bu_mm", "bu_used", "state_ready", "s5_mm", "s5_used", "gelu_done"))
        g_added, decay_set = sem("g_added"), sem("decay_set")
        glu_mm, gate_sig, glu_used = sem("glu_mm"), sem("gate_sig"), sem("glu_used")
        mlp1_mm, relu_done, sqr_done, mlp_split, mlp2_mm, mlp_added = (
            sem(n) for n in ("mlp1_mm", "relu_done", "sqr_done", "mlp_split", "mlp2_mm", "mlp_added"))
        xbc_mm, conv_done, xs_ready, dt_mm = (sem(n) for n in ("xbc_mm", "conv_done", "xs_ready", "dt_mm"))
        step_dve = sem("step_dve")
        step_act = sem("step_act")
        state_decayed = sem("state_decayed")
        ssd_staged, xs_tok_mm, xdt_ready, xdt_dec_ready, b_tok_evac, cb_mm = (
            sem(n) for n in ("ssd_staged", "xs_tok_mm", "xdt_ready", "xdt_dec_ready", "b_tok_evac", "cb_mm"))
        cs_mm, decay_ready, m_ready, off_mm, off_used = (sem(n) for n in ("cs_mm", "decay_ready", "m_ready", "off_mm", "off_used"))
        y7_mm, y_tok_evac, y_turned, y_added, st_mm, state_new = (
            sem(n) for n in ("y7_mm", "y_tok_evac", "y_turned", "y_added", "st_mm", "state_new"))
        z_mm, z_ready, z_used, yn_ready, x5_ready = (sem(n) for n in ("z_mm", "z_ready", "z_used", "yn_ready", "x5_ready"))
        y_hi_ready = sem("y_hi_ready")

        PAIRS, SPLITS, LOWS = {}, {}, {}
        for name, n in (("in", 2), ("out", 1), ("s5_in", 1), ("glu", 2), ("mlp0", 8), ("xbc", 3), ("z", 2), ("m2_out", 2),
                        ("mlp1", 8)):
            PAIRS[name] = (sum(m for _, m in PAIRS.values()), n)
        for name, n in (("glu", KC), ("mlp0", KC), ("xbc", KC), ("z", KC), ("m2_out", M2_XC), ("mlp1", KC)):
            SPLITS[name] = 4 * (PAIRS[name][0] - PAIRS["glu"][0])
            LOWS[name] = (sum(m for _, m in LOWS.values()), n)

        def rows(w):
            return w.rearrange("(c p) n -> p c n", p=P)

        block = ctx.enter_context(nc.Block())

        @block.sync
        def _(sp):
            sp.dma_start(c_cols, A["c_cols"]).then_inc(in_cond, 16)
            sp.dma_start(x[:], A["xT"]).then_inc(in_x, 16)
            for name, tile in (("cols", cols), ("mats", mats), ("iota", iota), ("tokid", tokid)):
                sp.dma_start(tile[:], A[name]).then_inc(in_small, 16)
            sp.dma_start(lam4, A["lam4"]).then_inc(in_small, 16)
            for n in range(4):
                sp.dma_start(w_early[n], rows(A["w_ada"])[:, :, n * TN:(n + 1) * TN]).then_inc(in_mod[n], 16)
            sp.dma_start(cx, A["ctxT"]).then_inc(in_ctx, 16)
            sp.dma_start(cond1, A["c_rows"][0, :].partition_broadcast(P)).then_inc(in_rows, 16)
            sp.dma_start(cond2[:], A["c_rows"][1, :].partition_broadcast(P)).then_inc(in_rows, 16)

            def load_pair(pair, i, source):
                for s in range(2):
                    for half in range(2):
                        sp.wait_ge(tile_used, pair * 4 + (2 * s + half + 1))
                        sp.dma_start(ring[:, s, 4 * half:4 * half + 4, :], source(i, s)[:, 4 * half:4 * half + 4, :]) \
                            .then_inc(tile_loaded[2 * s + half], 16)

            def load_pairs(name, source):
                first, count = PAIRS[name]
                with sp.Fori(0, count) as i:
                    load_pair(i + first, i, source)

            def columns(w, first=0):
                return lambda i, s: rows(w)[:, :, bass.ds(i * (2 * TN) + (first + s * TN), TN)]

            for name, tile in (("rope_c", rope_c), ("rope_s", rope_s), ("dft_c", dft_c), ("dft_s", dft_s),
                               ("dft_ch", dft_ch), ("wfour", wfour)):
                sp.dma_start(tile, A[name]).then_inc(in_mix, 16)
            load_pairs("in", columns(A["w_in"]))
            load_pairs("out", columns(A["w_out"]))

            sp.wait_ge(consts_set, 2)
            sp.dma_start(h_rows[T:T + 1, :].rearrange("o (q n) -> o q n", n=256),
                         zeros[0:1, :].unsqueeze(1).broadcast_to([1, 4, 256])).then_inc(zero_row, 16)
            sp.wait_ge(ada_used, 2 + ADA_LATE + ADA_TILES)
            y_quarters = y_rows.rearrange("(b p) (q n) -> q p b n", p=P, n=256)
            for q in range(4):
                sp.dma_start(y_quarters[q], zeros[:].unsqueeze(1).broadcast_to([P, BLOCKS + 2, 256])) \
                    .then_inc(y_stored[0] if q == 3 else y_zeroed, 16)
            sp.wait_ge(x1_ready, KC)
            sp.dma_start(w_router, A["w_router"]).then_inc(in_late, 16)
            sp.dma_start(b_router, A["b_router"]).then_inc(in_late, 16)
            sp.wait_ge(idx_loaded, 16)
            sp.wait_ge(route_ready, 2)
            pairs = sp.value_load(route_i[0:1, BLOCKS:BLOCKS + 1], min_val=1, max_val=BLOCKS // 2)
            with sp.Fori(0, pairs) as i:
                for s in range(2):
                    e = sp.value_load(route_i[0:1, bass.ds(i * 2 + s, 1)], min_val=0, max_val=EXPERTS - 1)
                    for w, tile, used, loaded in (("w_gate", expert_w[s][0], gate_mm, gate_loaded[s]),
                                                  ("w_up", expert_w[s][1], up_mm, up_loaded[s]),
                                                  ("w_down", expert_w[s][2], down_mm, down_loaded[s])):
                        sp.wait_ge(used, i * 2 + (s + 1))
                        sp.dma_start(tile, A[w][bass.ds(e, 1), :, :].rearrange("o (c p) n -> p (o c) n", p=P)) \
                            .then_inc(loaded, 16)

            sp.wait_ge(ysum_ready, TC)
            sp.dma_start(s5_b, A["s5_b"]).then_inc(in_late, 16)
            sp.dma_start(s5_c, A["s5_c"]).then_inc(in_late, 16)
            load_pairs("s5_in", columns(A["s5_w_in"]))
            load_pairs("glu", lambda i, s: rows(A["w_glu"])[:, :, bass.ds(i * TN + s * D, TN)])

            def load_mlp(layer):
                first = PAIRS[f"mlp{layer}"][0]
                with sp.Fori(0, 4) as i:
                    load_pair(i * 2 + first, i, columns(A["mlp_w1"][layer, :, :]))
                    load_pair(i * 2 + (first + 1), i, lambda i, s: A["mlp_w2"][
                        layer, bass.ds(i * D, D), s * TN:(s + 1) * TN].rearrange("(c p) n -> p c n", p=P))

            load_mlp(0)
            sp.dma_start(w_dt, A["m2_w_dt"]).then_inc(in_late, 16)
            load_pairs("xbc", columns(A["m2_w_in"], M2_IN))
            load_pairs("z", columns(A["m2_w_in"]))
            load_pairs("m2_out", lambda i, s: A["m2_w_out"][s * D:(s + 1) * D, bass.ds(i * TN, TN)]
                       .rearrange("(c p) n -> p c n", p=P))
            load_mlp(1)
            for c in range(0, KC, 2):
                sp.wait_ge(xn_ready, 8 * KC + c + 2)
                sp.dma_start(out[:, c:c + 2, :], x[:, c:c + 2, :]).then_inc(out_stored, 16)
            sp.wait_ge(out_stored, 16 * (KC // 2))

        @block.gpsimd
        def _(pool):
            pool.memset(ones[:], 1.0).then_inc(consts_set, 1)
            pool.memset(zeros[:], 0.0).then_inc(consts_set, 1)
            pool.iota(idx_all[:], [[0, BLOCKS]], base=T, channel_multiplier=0).then_inc(idx_set, 1)
            pool.wait_ge(idx_set, 1)
            pool.dma_start(slot_tok.rearrange("(p b) o -> p (b o)", b=BLOCKS), idx_all[:]).then_inc(idx_filled, 16)
            pool.sem_inc(ada_used, 2)
            pool.wait_ge(mod_mm, 4)
            for before, count, w in ((0, ADA_LATE, A["w_adaT"]), (ADA_LATE, ADA_TILES, A["ada_w_2T"][0, :, :])):
                with pool.Fori(0, count // 2) as i:
                    for s in range(2):
                        pool.wait_ge(ada_used, i * 2 + (before + s + 1))
                        pool.dma_start(ada_buf[s], w[bass.ds(i * (8 * P) + s * 4 * P, 4 * P), :]
                                       .rearrange("(n p) k -> p n k", p=P)).then_inc(ada_loaded[s], 16)

            pool.wait_ge(idx_filled, 16)
            pool.wait_ge(route_ready, 1)
            for k in range(2):
                for t in range(TC):
                    pool.indirect_dma_start(slot_tok, bass.IndirectOffsetOnAxis(slot_at[:, k, t:t + 1], 0),
                                            tokid[:, t:t + 1], None).then_inc(idx_stored, 16)
            pool.wait_ge(idx_stored, 16 * 2 * TC)
            pool.dma_start(idx_all[:], slot_tok.rearrange("(p b) o -> p (b o)", b=BLOCKS)).then_inc(idx_loaded, 16)
            pool.wait_ge(route_ready, 2)
            pairs = pool.value_load(route_i[0:1, BLOCKS:BLOCKS + 1], min_val=1, max_val=BLOCKS // 2)
            pool.wait_ge(idx_loaded, 16)
            pool.wait_ge(zero_row, 16)
            for s in range(2):
                pool.wait_ge(hrow_stored[s], 32)
            with pool.Fori(0, pairs) as i:
                for s in range(2):
                    pool.wait_ge(xT_mm, i * 2 + (s + 1))
                    pool.tensor_copy(idx[s][:], idx_all[:, bass.ds(i * 2 + s, 1)])
                    pool.drain()
                    pool.indirect_dma_start(xb[:, s, :], None, h_rows, bass.IndirectOffsetOnAxis(idx[s][:, 0:1], 0)) \
                        .then_inc(xb_loaded[s], 16)
            pool.wait_ge(moe_done, 1)
            for t in range(TC):
                for k in range(2):
                    pool.indirect_dma_start(y_of[:, k, t, :], None, y_rows,
                                            bass.IndirectOffsetOnAxis(slot_of[:, k, t:t + 1].bitcast(U32), 0)) \
                        .then_inc(y_loaded, 16)
            pool.wait_ge(ysum_ready, TC)
            pool.memset(wk(29440, 1152), 0.0).then_inc(c_zero, 1)
            pool.memset(decay_now, 0.0).then_inc(c_zero, 1)
            pool.sem_inc(g_added, 2)
            with pool.Fori(0, KC) as q:
                for a in range(3):
                    pool.wait_ge(bu_used, q * 4 + (4 + a + 1))
                    t = [chunked(rot[:, 1 - a % 2, n, :]) for n in range(4)]
                    nc.gpsimd.tensor_tensor(scan_g[:, :, 2 * a, :], t[0], t[1], ALU.add)
                    nc.gpsimd.tensor_tensor(scan_g[:, :, 2 * a + 1, :], t[2], t[3], ALU.subtract).then_inc(g_added, 1)
            pool.wait_ge(glu_used, KC)
            with pool.Fori(0, 4) as i:
                for j in range(4):
                    pool.wait_ge(ada_used, i * 4 + (ADA_LATE + ADA_TILES + j + 1))
                    pool.dma_start(ada_buf1[j % 2], A["ada_w_2T"][1, bass.ds(i * (12 * P) + j * 3 * P, 3 * P), :]
                                   .rearrange("(n p) k -> p n k", p=P)).then_inc(ada_loaded[j % 2], 16)
            with pool.Fori(0, M2_NC) as c:
                def by_head(v):
                    return v[:, bass.ds(c, 1), :].rearrange("p c h -> p (c h)").unsqueeze(2).broadcast_to([P, M2_HEADS, 64])

                def of_heads(v):
                    return v.rearrange("p (h n) -> p h n", n=64)

                pool.wait_ge(xdt_ready, c * 4 + 4)
                nc.gpsimd.tensor_tensor(of_heads(xdt_dec), of_heads(xdt), by_head(dec_tok), ALU.mult).then_inc(xdt_dec_ready, 1)
                pool.wait_ge(off_mm, c * 4 + 4)
                nc.gpsimd.tensor_tensor(of_heads(state), of_heads(state), by_head(dec_chunk), ALU.mult).then_inc(state_decayed, 1)

        @block.tensor
        def _(pe):
            pe.sem_inc(tile_used, 4)

            def tile_wait(name, i, s):
                for half in range(2):
                    pe.wait_ge(tile_loaded[2 * s + half], i * 16 + 16 * (PAIRS[name][0] + 1))

            def tile_done():
                pe.drain().then_inc(tile_used, 2)

            def split_half(n, s, half, bank, hi, lo, first, last, freed=None, done=None):
                pe.wait_ge(w_split, n + (2 * s + half + 1))
                for k in range(4):
                    if freed is not None:
                        pe.wait_ge(*freed(k))
                    for c in range(4):
                        at = slice(k * P, (k + 1) * P)
                        w_of, wlo = ring_hi[:, s, 4 * half + c, at], ring[:, s, 4 * half + c, at]
                        nc.tensor.matmul(PS[:, bank + k, :], f32r(w_of), f32r(hi(c)), start=first and c == 0, stop=False)
                        nc.tensor.matmul(PS[:, bank + k, :], f32r(wlo), f32r(hi(c)), start=False, stop=False)
                        mm = nc.tensor.matmul(PS[:, bank + k, :], f32r(w_of), f32r(lo(c)), start=False, stop=last and c == 3)
                    if done is not None:
                        mm.then_inc(done, 1)
                pe.drain().then_inc(tile_used, 1)

            def split_tile(n, s, bank, hi, lo, freed, done, lows=None):
                for half in range(2):
                    if lows is not None:
                        pe.wait_ge(lo_ready, LOWS[lows][0] + 4 * half + 4)
                    split_half(n, s, half, bank, lambda c: hi[:, 4 * half + c, :], lambda c: lo[:, 4 * half + c, :],
                               half == 0, half == 1, freed if half == 0 else None, done if half == 1 else None)

            def norm_sum(k, sq, n, first=0, last=KC):
                for c in range(first, last):
                    pe.wait_ge(sq_ready, KC * k + c + 1)
                    mm = nc.tensor.matmul(PS[:, NORM_BANKS[k], 0:n], ones[:], sq[:, c, 0:n], start=(c == 0), stop=(c == KC - 1))
                if last == KC:
                    mm.then_inc(ms_done, 1)

            pe.wait_ge(consts_set, 1)
            norm_sum(0, h, T)
            pe.wait_ge(cond_ready, 1)
            for n in range(4):
                pe.wait_ge(in_mod[n], 16)
                for c in range(KC):
                    mm = nc.tensor.matmul(PS[0:2, 4 + n, :], c_cols[:, c, :], w_early[n][:, c, :], start=(c == 0), stop=(c == KC - 1))
                mm.then_inc(mod_mm, 1)
            pe.wait_ge(in_small, 16 * 5)
            for k in range(MOD_EARLY):
                pe.wait_ge(mod_evac, k // 4 + 1)
                mm = nc.tensor.transpose(PS[:, 2, 2 * k:2 * k + 2], mod_rows[:, k // 4, (k % 4) * P:(k % 4 + 1) * P], eye[0:2, 0:2])
            mm.then_inc(mod_turned, 1)
            norm_sum(1, csq, CTX)

            pe.wait_ge(h_ready, KC)
            group = [0]

            def projection(s, cols_of, rhs_of, n):
                e = group[0]
                if e >= 8:
                    pe.wait_ge(qkv_evac, e - 7)
                elif e == 1:
                    pe.wait_ge(var_ready, 2)
                for c in range(KC):
                    mm = nc.tensor.matmul(PS[:, e % 8, 0:n], cols_of(c), rhs_of(c), start=(c == 0), stop=(c == KC - 1))
                mm.then_inc(qkv_mm, 1)
                group[0] += 1

            tile_wait("in", 0, 0)
            for k in range(4):
                projection(0, lambda c: ring[:, 0, c, k * P:(k + 1) * P], lambda c: h[:, c, :], T)
            tile_done()
            tile_wait("in", 0, 1)
            for k in range(4):
                projection(1, lambda c: ring[:, 1, c, k * P:(k + 1) * P], lambda c: h[:, c, :], T)
            pe.wait_ge(h_ready, 2 * KC)
            for k in range(4):
                projection(1, lambda c: ring[:, 1, c, k * P:(k + 1) * P], lambda c: cx[:, c, :], CTX)
            tile_done()
            tile_wait("in", 1, 0)
            for k in range(KCH):
                tok = (lambda c: cx[:, c, k * P:(k + 1) * P]) if k < 2 else (lambda c: h[:, c, (k - 2) * P:(k - 1) * P])
                projection(0, tok, lambda c: ring[:, 0, c, :], TN)
            tile_done()
            tile_wait("in", 1, 1)
            for k in range(4):
                projection(1, lambda c: ring[:, 1, c, k * P:(k + 1) * P], lambda c: h[:, c, :], T)
            tile_done()

            pe.wait_ge(qkv_evac, 22)
            for j in range(8):
                src = qT[:, j, :] if j < 4 else kT[:, j - 4, CTX:KEYS]
                nc.tensor.matmul(PS[:, j, :], rope_rot, src, start=True, stop=True).then_inc(rope_mm, 1)

            pe.wait_ge(rope_done, 8)
            pe.wait_ge(in_mix, 16 * 6)
            for g in range(GROUPS):
                if g:
                    pe.wait_ge(ab_evac, 2 * g)
                for t in range(TC):
                    mm = nc.tensor.matmul(PS[:, t // 2, (t % 2) * 256:(t % 2 + 1) * 256], fT[:, g, t * P:(t + 1) * P],
                                          dft_ch, start=True, stop=True)
                    if t % 2:
                        mm.then_inc(ab_mm, 1)
                pe.wait_ge(ab_evac, 2 * g + 2)
                for t in range(TC):
                    nc.tensor.matmul(PS[:, 2, :], fab[:, g % 2, t, 0:P], dft_c[:, t, :], start=(t == 0), stop=False)
                    mm = nc.tensor.matmul(PS[:, 2, :], fab[:, g % 2, t, P:2 * P], dft_s[:, t, :], start=False,
                                          stop=(t == TC - 1))
                mm.then_inc(fr_mm, 1)
                pe.wait_ge(fr_evac, g + 1)
                if g:
                    pe.wait_ge(fo_evac, g)
                nc.tensor.matmul(PS[:, 3, :], wfour[:, g, :], fre, start=True, stop=True).then_inc(fo_mm, 1)

            def scores(n):
                hd, qc, first = n // TC, n % TC, 3 * (n % 2)
                if n >= 2:
                    pe.wait_ge(exp_done, 2 * (n - 1))
                flat = PS[:, first:first + 3, :].rearrange("p a b -> p (a b)")
                for m, a, b in ((0, 512, KEYS), (0, 0, 512), (1, KEYS - 512, KEYS), (1, 0, KEYS - 512)):
                    half = slice(m * DH, (m + 1) * DH)
                    if m and a == 0:
                        pe.drain()
                    mm = nc.tensor.matmul(flat[:, m * KEYS + a:m * KEYS + b], qT[half, hd, qc * P:(qc + 1) * P],
                                          kT[half, hd, a:b], start=True, stop=True)
                mm.then_inc(score_mm, 1)

            def turn_weights(n):
                for part in range(2):
                    if n or part:
                        pe.wait_ge(at_evac, 2 * n + part)
                    if part == 0:
                        pe.wait_ge(a_ready, n + 1)
                    for k in range(3):
                        mm = nc.tensor.transpose(PS[:, 6, k * P:(k + 1) * P],
                                                 attn_a[:, n % 2, (3 * part + k) * P:(3 * part + k + 1) * P], eye)
                    mm.then_inc(at_mm, 1)
                    if part == 0 and n >= TC and n % TC < 3:
                        head_values(n // TC - 1, n % TC * (KCH // 3), (n % TC + 1) * (KCH // 3))

            def head_values(hd, first=0, last=KCH):
                if first == 0:
                    pe.wait_ge(at_evac, 2 * TC * (hd + 1))
                    if hd:
                        pe.wait_ge(head_done, hd)
                for k in range(first, last):
                    mm = nc.tensor.matmul(PS[:, 7, :], vtok[:, k, hd * P:(hd + 1) * P], aT[hd % 2][:, k, :],
                                          start=(k == 0), stop=(k == KCH - 1))
                if last == KCH:
                    mm.then_inc(pv_mm, 1)

            def head_norm_sum(hd):
                pe.wait_ge(osq_ready, hd + 1)
                nc.tensor.matmul(PS[:, 7, :], ones[:], oSq, start=True, stop=True).then_inc(oms_done, 1)

            pe.wait_ge(fo_evac, GROUPS)
            scores(0)
            scores(1)
            for n in range(HEADS * TC):
                if n + 2 < HEADS * TC:
                    scores(n + 2)
                turn_weights(n)
                if n >= TC and n % TC == 3:
                    head_norm_sum(n // TC - 1)
            head_values(HEADS - 1)
            head_norm_sum(HEADS - 1)

            pe.wait_ge(head_done, HEADS)
            for s in range(2):
                tile_wait("out", 0, s)
                for k in range(4):
                    for c in range(KC):
                        mm = nc.tensor.matmul(PS[:, 4 * s + k, :], ring[:, s, c, k * P:(k + 1) * P], h[:, c, :],
                                              start=(c == 0), stop=(c == KC - 1))
                    mm.then_inc(proj_mm, 1)
                    if s == 1 and k >= 1:
                        norm_sum(2, x1_sq, T, 2 * k - 2, 2 * k)
                tile_done()

            norm_sum(2, x1_sq, T, 6)
            pe.wait_ge(h_ready, 3 * KC)
            pe.wait_ge(in_late, 32)
            for t in range(TC):
                for c in range(KC):
                    mm = nc.tensor.matmul(PS[:, 1, t * 36:(t + 1) * 36], h[:, c, t * P:(t + 1) * P], w_router[:, c, :],
                                          start=(c == 0), stop=(c == KC - 1))
            mm.then_inc(route_mm, 1)
            for t in range(TC):
                if t >= 2:
                    pe.wait_ge(hrow_evac, t - 1)
                for c in range(KC):
                    mm = nc.tensor.transpose(PS[:, 2 + 2 * (t % 2) + c // 4, (c % 4) * P:(c % 4 + 1) * P],
                                             h[:, c, t * P:(t + 1) * P], eye)
                mm.then_inc(hrow_mm, 1)
            pe.wait_ge(chosen_ready, 1)
            for t in range(TC):
                for before in range(t):
                    nc.tensor.matmul(PS[:, 6, t * EXPERTS:(t + 1) * EXPERTS], ones[:], chosen[:, before, :],
                                     start=(before == 0), stop=False)
                nc.tensor.matmul(PS[:, 6, t * EXPERTS:(t + 1) * EXPERTS], tri, chosen[:, t, :], start=(t == 0), stop=True)
            for t in range(TC):
                mm = nc.tensor.matmul(PS[:, 6, TC * EXPERTS:(TC + 1) * EXPERTS], ones[:], chosen[:, t, :],
                                      start=(t == 0), stop=(t == TC - 1))
            mm.then_inc(route_mm, 1)

            pe.wait_ge(route_ready, 2)
            pe.wait_ge(hrow_evac, TC)
            pairs = pe.value_load(route_i[0:1, BLOCKS:BLOCKS + 1], min_val=1, max_val=BLOCKS // 2)
            for freed in (gate_mm, up_mm, down_mm, xT_mm):
                pe.sem_inc(freed, 2)

            def turn_tokens(i, s):
                pe.wait_ge(xb_loaded[s], i * 16 + 16)
                pe.wait_ge(xT_evac, i * 2 + (s + 1))
                for c in range(KC):
                    mm = nc.tensor.transpose(PS[:, c // 4, (c % 4) * P:(c % 4 + 1) * P], xb[:, s, c * P:(c + 1) * P], eye)
                mm.then_inc(xT_mm, 1)

            def gate_up(i, s):
                pe.wait_ge(xT_evac, i * 2 + (s + 2))
                pe.wait_ge(hid_ready, i * 2 + (s + 1))
                for loaded, w, bank, done in ((gate_loaded[s], expert_w[s][0], 2, gate_mm),
                                              (up_loaded[s], expert_w[s][1], 3, up_mm)):
                    pe.wait_ge(loaded, i * 16 + 16)
                    for c in range(KC):
                        mm = nc.tensor.matmul(PS[:, bank, :], xbT[:, s, c, :], w[:, c, :], start=(c == 0),
                                              stop=(c == KC - 1))
                    mm.then_inc(done, 1)

            def turn_hidden(i, s):
                pe.wait_ge(hid_ready, i * 2 + (s + 2))
                pe.wait_ge(hT_evac, i * 2 + (s + 1))
                for c in range(4):
                    mm = nc.tensor.transpose(PS[:, 4, c * P:(c + 1) * P], hid[:, s, c * P:(c + 1) * P], eye)
                mm.then_inc(hT_mm, 1)

            def down(i, s):
                pe.wait_ge(hT_evac, i * 2 + (s + 2))
                pe.wait_ge(y_ready, i * 2 + (s + 1))
                pe.wait_ge(down_loaded[s], i * 16 + 16)
                for n in range(2):
                    for c in range(4):
                        mm = nc.tensor.matmul(PS[:, 5 + n, :], hidT[:, s, c, :], expert_w[s][2][:, c, n * 512:(n + 1) * 512],
                                              start=(c == 0), stop=(c == 3))
                mm.then_inc(down_mm, 1)

            with pe.Fori(0, pairs) as i:
                turn_tokens(i, 0)
                gate_up(i, 0)
                turn_tokens(i, 1)
                turn_hidden(i, 0)
                down(i, 0)
                gate_up(i, 1)
                turn_hidden(i, 1)
                down(i, 1)
            pe.wait_ge(moe_done, 1)
            for t in range(TC):
                pe.wait_ge(ysum_ready, t + 1)
                if t >= 2:
                    pe.wait_ge(yT_used, t - 1)
                for c in range(KC):
                    mm = nc.tensor.transpose(PS[:, 2 * (t % 2) + c // 4, (c % 4) * P:(c % 4 + 1) * P],
                                             ysum[:, t % 2, c * P:(c + 1) * P], eye)
                mm.then_inc(yT_mm, 1)
            norm_sum(3, h, T)

            norm_sum(4, h, T)
            pe.wait_ge(h_ready, 4 * KC)
            for s in range(2):
                tile_wait("s5_in", 0, s)
                for k in range(4):
                    for c in range(KC):
                        mm = nc.tensor.matmul(PS[:, 4 * s + k, :], ring[:, s, c, k * P:(k + 1) * P], h[:, c, :],
                                              start=(c == 0), stop=(c == KC - 1))
                    mm.then_inc(proj_mm, 1)
                tile_done()
            pe.wait_ge(u_evac, KC)
            pe.sem_inc(bu_mm, 4)
            pe.sem_inc(s5_mm, 2)

            def inputs_to_states(q, a):
                pe.wait_ge(bu_used, q * 4 + (5 if a == 3 else 4))
                for part in range(2):
                    mm = nc.tensor.matmul(PS[:, 2 * (a % 3) + part, :], b_now[32 * a:32 * a + 32, part, :],
                                          u_now[32 * a:32 * a + 32, :], start=True, stop=True)
                mm.then_inc(bu_mm, 1)

            def s5_quad(q, last):
                inputs_to_states(q, 3)
                if not last:
                    pe.wait_ge(ub_staged, q + 2)
                    for a in range(3):
                        inputs_to_states(q + 1, a)
                pe.wait_ge(c_staged, q + 1)
                pe.wait_ge(s5_used, q + 1)
                c_pad = c_now.rearrange("p a n -> p (a n)")
                for a in range(4):
                    pe.wait_ge(state_ready, q * 4 + (a + 2))
                    for n in range(4):
                        at = (2 * a + n // 2) * P
                        mm = nc.tensor.matmul(PS[:, 6, :], c_pad[:, at:at + P], turned_back(a)[:, n, :],
                                              start=(a == 0 and n == 0), stop=(a == 3 and n == 3))
                    mm.then_inc(s5_mm, 1)

            pe.wait_ge(ub_staged, 1)
            for a in range(3):
                inputs_to_states(0, a)
            with pe.Fori(0, KC - 1) as q:
                s5_quad(q, False)
            s5_quad(KC - 1, True)
            for i in range(2):
                for s in range(2):
                    split_tile(SPLITS["glu"] + 4 * i, s, 4 * s, h, glu_lo, (lambda k: (glu_used, k + 1)) if i else None, glu_mm,
                               "glu" if i + s == 0 else None)

            def mlp(layer, k_norm):
                name = f"mlp{layer}"

                def quarter(i, last):
                    for s in range(2):
                        split_tile(i * 8 + SPLITS[name], s, 4 * s, h, mlp_h_lo,
                                   lambda k: (mlp_added, i * 8 + (32 * layer + 4 * s + k + 1)), mlp1_mm,
                                   name if s == 0 else None)
                    for s in range(2):
                        for half in range(2):
                            if s == 0:
                                pe.wait_ge(mlp_split, i * 8 + (32 * layer + 4 * half + 4))
                            if last and s + half == 2:
                                norm_sum(k_norm + 1, h, T, 0, 4)
                            split_half(i * 8 + (SPLITS[name] + 4), s, half, 4 * s, lambda c: mlp_hi[:, 4 * half + c, :],
                                       lambda c: mlp_lo[:, 4 * half + c, :], half == 0, half == 1,
                                       (lambda k: (relu_done, i * 8 + (32 * layer + 4 * s + k + 1))) if half == 0 else None,
                                       mlp2_mm if half else None)

                with pe.Fori(0, 3) as i:
                    quarter(i, False)
                quarter(3, True)

            pe.wait_ge(glu_used, 5)
            norm_sum(5, glu_sq, T)
            mlp(0, 5)

            norm_sum(6, h, T, 4)
            with pe.Fori(0, 3) as i:
                for s in range(2):
                    split_tile(i * 4 + SPLITS["xbc"], s, 4 * s, h, xbc_h_lo,
                               lambda k: (conv_done, i * 8 + (4 * s + k + 1)), xbc_mm, "xbc" if s == 0 else None)
            pe.wait_ge(conv_done, 8 + M2_CC)
            pe.wait_ge(step_dve, 1)
            pe.wait_ge(in_late, 80)
            for c in range(KC):
                mm = nc.tensor.matmul(PS[0:M2_HEADS, 0, :], w_dt[:, c, :], h[:, c, :], start=(c == 0), stop=(c == KC - 1))
            mm.then_inc(dt_mm, 1)
            pe.wait_ge(step_dve, 3)
            for c in range(M2_NC):
                for n, rows_of in enumerate((dt_t, a_cs)):
                    nc.tensor.transpose(PS[:, 1, (4 * n + c) * M2_HEADS:(4 * n + c + 1) * M2_HEADS],
                                        rows_of[:, c * M2_Q:(c + 1) * M2_Q], eye[0:M2_HEADS, 0:M2_HEADS])
            nc.tensor.matmul(PS[:, 2, 0:M2_NC * M2_HEADS], ones[0:M2_HEADS, :], last_diag.rearrange("p c h -> p (c h)"),
                             start=True, stop=True).then_inc(dt_mm, 1)
            pe.wait_ge(step_act, 2)
            pe.wait_ge(xs_ready, M2_CC)
            pe.sem_inc(y7_mm, 2)
            pe.sem_inc(y_turned, 2)
            with pe.Fori(0, M2_NC) as c:
                pe.wait_ge(ssd_staged, c + 1)
                pe.wait_ge(y_added, c * 8 + 1)
                for g in range(M2_G):
                    mm = nc.tensor.transpose(PS[:, 4, g * P:(g + 1) * P], xs_now[:, M2_XC + g, :], eye)
                for g in range(M2_G):
                    mm = nc.tensor.matmul(PS[:, 5, g * P:(g + 1) * P], xs_now[:, M2_XC + g, :], xs_now[:, M2_XC + M2_G + g, :],
                                          start=True, stop=True)
                mm.then_inc(cb_mm, 1)

                def spread_sums(q):
                    if 1 <= q <= 4:
                        pe.wait_ge(off_used, c * 4 + q)
                    elif q:
                        pe.wait_ge(decay_ready, c * 8 + (q - 4))
                    bank = SUM_BANKS[q % 5]
                    nc.tensor.matmul(PS[:, bank, :], eye16, mask16.unsqueeze(1).broadcast_to([P, 4, P]), start=True, stop=False)
                    for k in range(4):
                        n = 4 * q + k
                        mm = nc.tensor.matmul(PS[:, bank, k * P:(k + 1) * P], eye[0:M2_HEADS, n:n + 1].broadcast_to([M2_HEADS, P]),
                                              sums_now, start=False, stop=(k == 3))
                    mm.then_inc(cs_mm, 1)

                def turn_y(q):
                    pe.wait_ge(y_tok_evac, c * 8 + (q + 2))
                    pe.wait_ge(b_tok_evac, c + 1)
                    pe.wait_ge(y_added, c * 8 + (q + 1))
                    for j in range(2):
                        mm = nc.tensor.transpose(PS[:, 4, j * P:(j + 1) * P], y_tok[:, q % 2, j * P:(j + 1) * P], eye)
                    mm.then_inc(y_turned, 1)

                spread_sums(0)
                pe.wait_ge(state_new, c + 1)
                for j in range(M2_XC):
                    mm = nc.tensor.transpose(PS[:, j // 4, (j % 4) * P:(j % 4 + 1) * P], xs_now[:, j, :], eye)
                    if j % 4 == 3:
                        mm.then_inc(xs_tok_mm, 1)
                for g in range(M2_G):
                    pe.wait_ge(xdt_ready, c * 4 + (g + 1))
                    nc.tensor.matmul(PS[:, g, :], xs_now[:, M2_XC + M2_G + g, :], state[:, g * 512:(g + 1) * 512], start=True,
                                     stop=True).then_inc(off_mm, 1)
                spread_sums(1)
                spread_sums(2)
                for q in range(8):
                    pe.wait_ge(m_ready, c * 8 + (q + 3))
                    pe.wait_ge(y_tok_evac, c * 8 + (q + 1))
                    for k in range(4):
                        at = (4 * q + k) * 64
                        mm = nc.tensor.matmul(PS[:, 7, k * 64:(k + 1) * 64], m_now[:, q % 2, k, :], xdt[:, at:at + 64], start=True,
                                              stop=True)
                    mm.then_inc(y7_mm, 1)
                    if q < 5:
                        spread_sums(q + 3)
                    if q:
                        turn_y(q - 1)
                turn_y(7)
                pe.wait_ge(xdt_dec_ready, c + 1)
                for g in range(M2_G):
                    mm = nc.tensor.matmul(PS[:, g, :], b_tok[:, g, :], xdt_dec[:, g * 512:(g + 1) * 512], start=True, stop=True)
                mm.then_inc(st_mm, 1)
            pe.wait_ge(state_new, 1 + M2_NC)

            def group_sum(g):
                for j in range(4):
                    pe.wait_ge(osq_ready, HEADS + 4 * g + j + 1)
                    mm = nc.tensor.matmul(PS[:, 4 * (g % 2), :], ones[:], m2_sq[:, 4 * (g % 2) + j, :], start=(j == 0),
                                          stop=(j == 3))
                mm.then_inc(oms_done, 1)

            for t in range(4):
                if t >= 2:
                    pe.wait_ge(ovar_ready, HEADS + t - 1)
                for half in range(2):
                    if t == 0:
                        pe.wait_ge(lo_ready, LOWS["z"][0] + 4 * half + 4)
                    split_half(SPLITS["z"] + 4 * (t // 2), t % 2, half, 4 * (t % 2), lambda c: z_h_hi[:, 4 * half + c, :],
                               lambda c: h[:, 4 * half + c, :], half == 0, half == 1,
                               (lambda k: (z_ready, 4 * t + k + 1)) if half == 0 else None, z_mm if half else None)
                    if t and half == 0:
                        group_sum(t - 1)
            pe.wait_ge(z_ready, 8 + M2_XC)
            pe.wait_ge(ovar_ready, HEADS + M2_G - 1)
            for out_half in range(2):
                for s in range(2):
                    for half in range(2):
                        rows_at = 8 * s + 4 * half
                        if out_half == 0:
                            pe.wait_ge(lo_ready, LOWS["m2_out"][0] + rows_at + 4)
                        elif rows_at == 0:
                            pe.wait_ge(ovar_ready, HEADS + M2_G)
                        elif rows_at == 12:
                            norm_sum(7, h, T, 0, 4)
                        split_half(SPLITS["m2_out"] + 4 * out_half, s, half, 4 * out_half, lambda c: xs[:, rows_at + c, :],
                                   lambda c: y_lo[:, rows_at + c, :], rows_at == 0, rows_at == 12, None,
                                   proj_mm if rows_at == 12 else None)
                        if out_half == 0 and rows_at == 0:
                            group_sum(M2_G - 1)
            norm_sum(7, h, T, 4)
            mlp(1, 7)
            norm_sum(8, h, T, 4)

        @block.scalar
        def _(act):
            def copy(out, in_):
                return nc.scalar.activation(out, in_, ACT.Copy)

            def norm_squares(src, sq, ready=None, count=0):
                for c in range(KC):
                    if ready is not None:
                        act.wait_ge(ready, count + c + 1)
                    nc.scalar.activation(sq[:, c, :], src[:, c, :], ACT.Square).then_inc(sq_ready, 1)

            def norm_root(k, n):
                nc.scalar.activation(sm[:, 32 + k:33 + k], ones[:, 0:1], ACT.Sqrt)
                act.wait_ge(var_ready, k + 1)
                nc.scalar.activation(rstd[:, 0:n], var[:, 0:n], ACT.Sqrt).then_inc(std_ready, 1)

            def norm_affine(k, dst, scale, shift):
                for c in range(KC):
                    act.wait_ge(xn_ready, KC * k + c + 1)
                    nc.scalar.activation(dst[:, c, :], dst[:, c, :], ACT.Identity, scale=scale[:, c:c + 1],
                                         bias=shift[:, c:c + 1]).then_inc(h_ready, 1)

            def norm_shift_rounded(k, scaled, shift):
                for c in range(KC):
                    act.wait_ge(xn_ready, KC * k + c + 1)
                    nc.scalar.activation(f32r(h[:, c, :]), scaled[:, c, :], ACT.Identity, bias=shift[:, c:c + 1]) \
                        .then_inc(h_ready, 1)

            def round_weights(pair, s):
                for half in range(2):
                    act.wait_ge(tile_loaded[2 * s + half], pair * 16 + 16)
                    at = slice(4 * half, 4 * half + 4)
                    copy(f32r(ring_hi[:, s, at, :]), ring[:, s, at, :]).then_inc(w_hi, 1)

            act.wait_ge(consts_set, 1)
            act.wait_ge(in_cond, 16)
            nc.scalar.activation(c_cols, c_cols, ACT.Silu).then_inc(cond_ready, 1)
            act.wait_ge(in_x, 16)
            norm_squares(x, h)
            norm_root(0, T)
            for n in range(4):
                act.wait_ge(mod_mm, n + 1)
                copy(mod_rows[:, n, :], PS[0:2, 4 + n, :]).then_inc(mod_evac, 1)
            act.wait_ge(in_ctx, 16)
            norm_squares(cx, csq)
            act.wait_ge(mods_ready, 1)
            norm_affine(0, h, gain[:, 0, :], mod1[:, 0:KC])
            norm_root(1, CTX)
            norm_affine(1, cx, gain[:, 1, :], modc[:, 0:KC])
            act.wait_ge(exp_in, 1)
            nc.scalar.activation(lam_d[:, 2:4], lam_d[:, 0:2], ACT.Exp).then_inc(exp_out, 1)
            act.wait_ge(in_rows, 32)
            nc.scalar.activation(cond1, cond1, ACT.Silu)
            nc.scalar.activation(cond2[:], cond2[:], ACT.Silu).then_inc(cond_ready, 1)

            for e in range(22):
                act.wait_ge(qkv_mm, e + 1)
                if e < 4:
                    dst, n = qT[:, e, :], T
                elif e < 8:
                    dst, n = kT[:, e - 4, CTX:KEYS], T
                elif e < 12:
                    dst, n = kT[:, e - 8, 0:CTX], CTX
                elif e < 18:
                    dst, n = vtok[:, e - 12, :], TN
                else:
                    dst, n = fT[:, e - 18, :], T
                copy(dst, PS[:, e % 8, 0:n]).then_inc(qkv_evac, 1)

            for g in range(GROUPS):
                for b in range(2):
                    act.wait_ge(ab_mm, 2 * g + b + 1)
                    if g >= 2:
                        act.wait_ge(fr_mm, g - 1)
                    copy(fab[:, g % 2, 2 * b:2 * b + 2, :], PS[:, b, :].rearrange("p (t n) -> p t n", n=256)) \
                        .then_inc(ab_evac, 1)
                act.wait_ge(fr_mm, g + 1)
                if g:
                    act.wait_ge(fo_mm, g)
                copy(fre, PS[:, 2, :]).then_inc(fr_evac, 1)
                act.wait_ge(fo_mm, g + 1)
                copy(h[:, HEADS + g, :], PS[:, 3, :]).then_inc(fo_evac, 1)

            def exps(n):
                act.wait_ge(negmax_ready, n + 1)
                if n >= 2:
                    act.wait_ge(a_ready, n - 1)
                first = 3 * (n % 2)
                flat = PS[:, first:first + 3, :].rearrange("p a b -> p (a b)")
                for m in range(2):
                    nc.scalar.activation(probs[:, n % 2, m, :], flat[:, m * KEYS:(m + 1) * KEYS], ACT.Exp,
                                         bias=negmax[:, n % 2, m:m + 1], scale=DH ** -0.5,
                                         accum_out=rowsum[:, n % 2, m:m + 1]).then_inc(exp_done, 1)

            def head_square(hd):
                act.wait_ge(o_ready, hd + 1)
                nc.scalar.activation(oSq, oT, ACT.Square).then_inc(osq_ready, 1)

            def head_root(hd):
                act.wait_ge(ovar_ready, hd + 1)
                nc.scalar.activation(rstd, var, ACT.Sqrt).then_inc(ostd_ready, 1)

            exps(0)
            for n in range(HEADS * TC):
                hd, qc = n // TC, n % TC
                if n + 1 < HEADS * TC:
                    exps(n + 1)
                if hd >= 2 and qc == 0:
                    act.wait_ge(pv_mm, hd - 1)
                for part in range(2):
                    act.wait_ge(at_mm, 2 * n + part + 1)
                    copy(aT[hd % 2][:, 3 * part:3 * part + 3, qc * P:(qc + 1) * P],
                         PS[:, 6, 0:3 * P].rearrange("p (k q) -> p k q", q=P)).then_inc(at_evac, 1)
                if hd and qc == 2:
                    head_square(hd - 1)
                if hd and qc == 3:
                    head_root(hd - 1)
            head_square(HEADS - 1)
            head_root(HEADS - 1)

            norm_squares(x, x1_sq, x1_ready)
            norm_root(2, T)
            norm_affine(2, h, gain[:, 2, :], mod1[:, 3 * KC:4 * KC])
            for t in range(TC):
                act.wait_ge(hrow_mm, t + 1)
                if t >= 2:
                    act.wait_ge(hrow_stored[t % 2], 16)
                copy(hrow[:, t % 2, :].rearrange("p (a b) -> p a b", a=2),
                     PS[:, 2 + 2 * (t % 2):4 + 2 * (t % 2), :]).then_inc(hrow_evac, 1)
                act.wait_ge(hrow_evac, t + 1)
                act.dma_start(h_rows[t * P:(t + 1) * P, :], hrow[:, t % 2, :]).then_inc(hrow_stored[t % 2], 16)
                if t == 1:
                    act.wait_ge(exp_in, 2)
                    nc.scalar.activation(g_exp, g_exp, ACT.Exp).then_inc(exp_out, 1)
                    act.wait_ge(exp_in, 3)
                    nc.scalar.activation(e2, e2, ACT.Exp).then_inc(exp_out, 1)

            act.wait_ge(route_ready, 2)
            pairs = act.value_load(route_i[0:1, BLOCKS:BLOCKS + 1], min_val=1, max_val=BLOCKS // 2)
            for freed in (xT_evac, hT_evac):
                act.sem_inc(freed, 1)
            act.wait_ge(y_zeroed, 48)
            act.wait_ge(y_stored[0], 16)

            def tokens_turned(i, s):
                act.wait_ge(xT_mm, i * 2 + (s + 3))
                copy(xbT[:, s, :, :].rearrange("p (a c) q -> p a (c q)", a=2), PS[:, 0:2, :]).then_inc(xT_evac, 1)

            def gate_silu(i, s):
                act.wait_ge(gate_mm, i * 2 + (s + 3))
                nc.scalar.activation(silu_b[:, s, :], PS[:, 2, :], ACT.Silu).then_inc(silu_done, 1)

            def hidden_turned(i, s):
                act.wait_ge(hT_mm, i * 2 + (s + 1))
                copy(hidT[:, s, :, :].rearrange("p c q -> p (c q)"), PS[:, 4, :]).then_inc(hT_evac, 1)

            def store_last(i, s):
                act.wait_ge(y_ready, i * 2 + (s + 1))
                act.dma_start(y_rows[bass.ds(i * (2 * P) + s * P, P), :], yb[:, 1 - s, :]).then_inc(y_stored[1 - s], 16)

            with act.Fori(0, pairs) as i:
                tokens_turned(i, 0)
                gate_silu(i, 0)
                store_last(i, 0)
                tokens_turned(i, 1)
                hidden_turned(i, 0)
                gate_silu(i, 1)
                store_last(i, 1)
                hidden_turned(i, 1)
            act.wait_ge(y_ready, pairs * 2 + 1)
            act.dma_start(y_rows[bass.ds(pairs * (2 * P), P), :], yb[:, 1, :]).then_inc(y_stored[1], 16)
            for s in range(2):
                act.wait_ge(y_stored[s], pairs * 16 + 16)
            act.sem_inc(moe_done, 1)

            act.wait_ge(ysum_ready, 1)
            nc.scalar.activation(s5_dt, col("log_dt", 0, S5_TILES), ACT.Exp).then_inc(exp_out, 1)
            norm_squares(x, h, x2_ready)
            norm_root(3, T)
            norm_squares(x, h, xn_ready, 3 * KC)

            norm_root(4, T)
            norm_affine(4, h, gain[:, 3, :], mod2[:, 0, 0:KC])
            act.wait_ge(exp_in, 4)
            nc.scalar.activation(radius, s5_a, ACT.Exp)
            nc.scalar.activation(half_sin, s5_r, ACT.Sin)
            nc.scalar.activation(half_cos, s5_ab, ACT.Sin).then_inc(exp_out, 1)
            for k in range(KC):
                act.wait_ge(proj_mm, KC + k + 1)
                copy(uT[:, k, :], PS[:, k, :]).then_inc(u_evac, 1)
            act.wait_ge(in_late, 64)
            act.wait_ge(u_evac, KC)
            act.wait_ge(c_zero, 2)
            act.wait_ge(c_ready, 1)
            with act.Fori(0, KC) as q:
                act.wait_ge(bu_mm, q * 4 + 4)
                copy(u_now, uT[:, bass.ds(q, 1), :].rearrange("p a n -> p (a n)"))
                copy(b_now, s5_b[:, bass.ds(q, 1), :, :].rearrange("p a r n -> p (a r) n")).then_inc(ub_staged, 1)
                act.wait_ge(state_ready, q * 4 + 1)
                copy(decay_now[:, :, :, 1:S5_Q], radius[:, bass.ds(q * 4, 4)].unsqueeze(2).unsqueeze(3)
                     .broadcast_to([P, 4, 2, S5_Q - 1])).then_inc(decay_set, 1)
                act.wait_ge(s5_mm, q * 4 + 2)
                for g in range(2):
                    part = slice(64 * g, 64 * g + 64)
                    for r in range(2):
                        last = copy(c_now[part, :, r * P + HP * g:r * P + HP * (g + 1)],
                                    s5_cf[part, bass.ds(q * 4, 4), r, :])
                last.then_inc(c_staged, 1)
            act.wait_ge(s5_used, KC + 1)
            first = PAIRS["glu"][0]
            round_weights(first, 0)
            for k in range(KC):
                nc.scalar.activation(glu_lo[:, k, :], h[:, k, :], ACT.Gelu_apprx_tanh)
                nc.scalar.activation(f32r(h[:, k, :]), h[:, k, :], ACT.Gelu_apprx_tanh).then_inc(gelu_done, 1)
            round_weights(first, 1)
            for i in range(2):
                round_weights(first + 1, i)
                for k in range(4):
                    n = 4 * i + k
                    act.wait_ge(glu_mm, 8 * i + 4 + k + 1)
                    if n >= 2:
                        act.wait_ge(glu_used, n - 1)
                    nc.scalar.activation(glu_gate[:, n % 2, :], PS[:, 4 + k, :], ACT.Sigmoid, bias=col("b_glu", KC + n)) \
                        .then_inc(gate_sig, 1)

            def mlp(layer, k_norm):
                first = PAIRS[f"mlp{layer}"][0]
                if layer == 0:
                    norm_squares(x, glu_sq, glu_used)
                else:
                    norm_squares(x, h, x5_ready)
                round_weights(first, 0)
                norm_root(k_norm, T)
                norm_shift_rounded(k_norm, mlp_h_lo, mod2[:, layer, 3 * KC:4 * KC])

                def quarter(i, last):
                    for t in range(4):
                        if t < 3 or not last:
                            round_weights(i * 2 + (first + (t + 1) // 2), (t + 1) % 2)
                        if t < 2:
                            for n in range(4 * t, 4 * t + 4):
                                act.wait_ge(relu_done, i * 8 + (32 * layer + n + 1))
                                for dst in (f32r(mlp_hi[:, n, :]), mlp_lo[:, n, :]):
                                    done = nc.scalar.activation(dst, mlp_lo[:, n, :], ACT.Square)
                                done.then_inc(sqr_done, 1)

                with act.Fori(0, 3) as i:
                    quarter(i, False)
                quarter(3, True)

            mlp(0, 5)

            first = PAIRS["xbc"][0]
            norm_squares(x, h, mlp_added, 8 + 3 * KC)
            round_weights(first, 0)
            norm_root(6, T)
            norm_shift_rounded(6, xbc_h_lo, mod2[:, 1, 0:KC])

            def conv_out(i, last):
                for s in range(2):
                    if s == 0 or not last:
                        round_weights(i + (first + s), 1 - s)
                    for k in range(4 * s, 4 * s + 4):
                        act.wait_ge(conv_done, i * 8 + (8 + k + 1))
                        chunk = xs[:, bass.ds(i * 8 + k, 1), :]
                        nc.scalar.activation(chunk, chunk, ACT.Silu,
                                             bias=cols[:, bass.ds(i * 8 + (COLS["conv_b"][0] + k), 1)]).then_inc(xs_ready, 1)

            with act.Fori(0, 2) as i:
                conv_out(i, False)
            conv_out(2, True)
            act.wait_ge(step_dve, 2)
            nc.scalar.activation(dt_abs, dt_raw, ACT.Abs)
            act.drain()
            nc.scalar.activation(dt_abs, dt_abs, ACT.Exp, scale=-1.0)
            nc.scalar.activation(a_pos, col("a_log")[0:M2_HEADS, :], ACT.Exp)
            act.drain()
            nc.scalar.activation(dt_abs, dt_abs, ACT.Ln, bias=1.0).then_inc(step_act, 1)
            act.wait_ge(step_dve, 4)
            nc.scalar.activation(dec_tok, dec_tok, ACT.Exp)
            nc.scalar.activation(exp_cs_tok, cs_neg, ACT.Exp, scale=-1.0)
            nc.scalar.activation(dec_chunk, PS[:, 2, 0:M2_NC * M2_HEADS].rearrange("p (c h) -> p c h", h=M2_HEADS), ACT.Exp) \
                .then_inc(step_act, 1)
            act.wait_ge(xs_ready, M2_CC)
            act.wait_ge(state_new, 1)

            def stage(c):
                copy(sums_now, a_cs[:, bass.ds(c * M2_Q, M2_Q)])
                copy(xs_now, xs[:, :, bass.ds(c * M2_Q, M2_Q)]).then_inc(ssd_staged, 1)

            def decays(c):
                act.wait_ge(cb_mm, c + 1)
                copy(b_tok.rearrange("p g n -> p (g n)"), PS[:, 4, :]).then_inc(b_tok_evac, 1)
                for q in range(8):
                    act.wait_ge(cs_mm, c * 8 + (q + 1))
                    act.wait_ge(m_ready, c * 8 + (q + 1))
                    for k in range(4):
                        n = 4 * q + k
                        last = nc.scalar.activation(decay[:, q % 2, k, :], PS[:, SUM_BANKS[q % 5], k * P:(k + 1) * P], ACT.Exp,
                                                    bias=cs_neg[:, bass.ds(c, 1), n:n + 1].rearrange("p c h -> p (c h)"))
                    last.then_inc(decay_ready, 1)

            stage(0)
            with act.Fori(0, M2_NC - 1) as c:
                decays(c)
                act.wait_ge(off_mm, c * 4 + 4)
                stage(c + 1)
            decays(M2_NC - 1)
            act.sem_inc(z_ready, 8)
            act.wait_ge(state_new, 1 + M2_NC)
            first = PAIRS["z"][0]
            round_weights(first, 0)
            for c in range(KC):
                copy(f32r(z_h_hi[:, c, :]), h[:, c, :]).then_inc(h_ready, 1)

            def group_root(g):
                act.wait_ge(ovar_ready, HEADS + g + 1)
                nc.scalar.activation(rstd, var, ACT.Sqrt).then_inc(ostd_ready, 1)

            for t in range(4):
                if t < 3:
                    round_weights(first + (t + 1) // 2, (t + 1) % 2)
                else:
                    round_weights(PAIRS["m2_out"][0], 0)
                for n in range(4 * t, 4 * t + 4):
                    act.wait_ge(z_mm, n + 1)
                    act.wait_ge(z_used, n + 1)
                    nc.scalar.activation(z_silu[:, n % 2, :], PS[:, n % 8, :], ACT.Silu).then_inc(z_ready, 1)
                if t >= 2:
                    act.wait_ge(oms_done, HEADS + t - 1)
                for n in range(4 * t, 4 * t + 4):
                    act.wait_ge(z_used, 2 + n + 1)
                    nc.scalar.activation(m2_sq[:, n % 8, :], xs[:, n, :], ACT.Square).then_inc(osq_ready, 1)
                if t:
                    group_root(t - 1)
            first = PAIRS["m2_out"][0]
            for g in range(M2_G):
                if g == 1:
                    round_weights(first, 1)
                if g == 2:
                    group_root(3)
                for n in range(4 * g, 4 * g + 4):
                    act.wait_ge(yn_ready, n + 1)
                    copy(f32r(xs[:, n, :]), y_lo[:, n, :]).then_inc(y_hi_ready, 1)
            for s in range(2):
                round_weights(first + 1, s)
            mlp(1, 7)
            norm_squares(x, h, mlp_added, 8 + 7 * KC)
            norm_root(8, T)

        @block.vector
        def _(dve):
            tt, ts, stt = nc.vector.tensor_tensor, nc.vector.tensor_scalar, nc.vector.scalar_tensor_tensor

            def norm_var(k, n, eps):
                dve.wait_ge(ms_done, k + 1)
                ts(var[:, 0:n], PS[:, NORM_BANKS[k], 0:n], 1.0 / D, eps, ALU.mult, ALU.add).then_inc(var_ready, 1)

            def norm_inverse(k, n):
                dve.wait_ge(std_ready, k + 1)
                nc.vector.reciprocal(rstd[:, 0:n], rstd[:, 0:n])
                dve.drain()

            def norm_scale(k, scale):
                norm_inverse(k, T)
                for c in range(KC):
                    stt(x[:, c, :], x[:, c, :], scale[:, c:c + 1], rstd, ALU.mult, ALU.mult).then_inc(xn_ready, 1)

            def norm_divide(k, src, dst, n):
                norm_inverse(k, n)
                for c in range(KC):
                    tt(dst[:, c, :], src[:, c, :], rstd[:, 0:n], ALU.mult).then_inc(xn_ready, 1)

            def modulation(pairs, base, cond_row, bias, dst, buf=ada_buf):
                with dve.Fori(*pairs) as i:
                    for s in range(2):
                        dve.wait_ge(ada_loaded[s], i * 16 + 16 * (base // 2 + 1))
                        for n in range(4):
                            w = buf[s][:, n, :]
                            last = stt(w, w, 1.0, cond_row, ALU.mult, ALU.mult,
                                       accum_out=dst[:, bass.ds(i * 8 + (4 * s + n), 1)])
                        last.then_inc(ada_used, 1)
                dve.drain()
                done = slice(8 * pairs[0], 8 * pairs[1])
                tt(dst[:, done], dst[:, done], bias[:, done], ALU.add)

            def norm_gain(n, scale, g):
                stt(gain[:, n, :], scale, 1.0, col(g, 0, KC), ALU.add, ALU.mult)

            def split_weight_half(name, n, s, half):
                dve.wait_ge(w_hi, n + (SPLITS[name] + half + 1))
                at = slice(4 * half, 4 * half + 4)
                tt(f32r(ring[:, s, at, :]), ring[:, s, at, :], f32r(ring_hi[:, s, at, :]), ALU.subtract).then_inc(w_split, 1)

            def split_weights(name, n, s):
                for half in range(2):
                    split_weight_half(name, n, s, half)

            def split_first(name, lo, hi, done, count):
                for half in range(2):
                    split_weight_half(name, 0, 0, half)
                    for c in range(4 * half, 4 * half + 4):
                        dve.wait_ge(done, count + c + 1)
                        tt(f32r(lo[:, c, :]), lo[:, c, :], f32r(hi[:, c, :]), ALU.subtract).then_inc(lo_ready, 1)

            def split_normed(name, lo, count, k, scale, shift):
                split_weight_half(name, 0, 0, 0)
                norm_inverse(k, T)
                for half in range(2):
                    chunks = range(4 * half, 4 * half + 4)
                    for c in chunks:
                        stt(lo[:, c, :], x[:, c, :], scale[:, c:c + 1], rstd, ALU.mult, ALU.mult).then_inc(xn_ready, 1)
                    if half:
                        split_weight_half(name, 0, 0, 1)
                    for c in chunks:
                        dve.wait_ge(h_ready, count + c + 1)
                        stt(f32r(lo[:, c, :]), lo[:, c, :], shift[:, c:c + 1], f32r(h[:, c, :]), ALU.add, ALU.subtract) \
                            .then_inc(lo_ready, 1)

            dve.wait_ge(in_small, 16 * 5)
            ts(gsub, col("g_subln"), 1.0 - LAMBDA_INIT, None, ALU.mult)
            tt(lam_t[:, 0, :], lam4[:, 0, :], lam4[:, 1, :], ALU.mult)
            tt(lam_t[:, 1, :], lam4[:, 2, :], lam4[:, 3, :], ALU.mult)
            dve.drain()
            nc.vector.tensor_reduce(lam_d[:, 0:2], lam_t, AX, ALU.add).then_inc(exp_in, 1)
            norm_var(0, T, 1e-6)
            norm_divide(0, x, h, T)
            dve.wait_ge(mod_turned, 1)
            turned_mods = PS[:, 2, 0:2 * MOD_EARLY].rearrange("p (k r) -> p r k", r=2)
            tt(mod1[:, 0:MOD_EARLY], turned_mods[:, 0, :], col("b_ada", 0, MOD_EARLY), ALU.add)
            tt(modc[:], turned_mods[:, 1, :], col("b_ada", 0, MOD_EARLY), ALU.add)
            dve.drain()
            norm_gain(0, mod1[:, KC:2 * KC], "g_mix")
            stt(gain[:, 1, :], modc[:, KC:2 * KC], 1.0, col("g_mix", 0, KC), ALU.add, ALU.mult).then_inc(mods_ready, 1)
            dve.wait_ge(h_ready, KC)
            norm_var(1, CTX, 1e-6)
            norm_divide(1, cx, cx, CTX)
            dve.wait_ge(exp_out, 1)
            tt(neglam, lam_d[:, 3:4], lam_d[:, 2:3], ALU.subtract)
            dve.drain()
            ts(neglam, neglam, -LAMBDA_INIT, None, ALU.add)

            dve.wait_ge(cond_ready, 2)
            modulation((2, ADA_TILES // 2), -MOD_EARLY // 4, cond1, col("b_ada", 0, 48), mod1)
            modulation((0, 4), ADA_LATE, cond2[:], col("ada_b0", 0, 48), mod2[:, 0, :])

            dve.wait_ge(in_mix, 16 * 6)
            for j in range(8):
                dve.wait_ge(rope_mm, j + 1)
                src = qT[:, j, :] if j < 4 else kT[:, j - 4, CTX:KEYS]
                tt(rope_t[:, j % 2, 0, :], src, rope_c, ALU.mult)
                tt(rope_t[:, j % 2, 1, :], PS[:, j, :], rope_s, ALU.mult)
                dve.drain()
                tt(src, rope_t[:, j % 2, 0, :], rope_t[:, j % 2, 1, :], ALU.add).then_inc(rope_done, 1)

            modulation((4, ADA_TILES // 2), ADA_LATE, cond2[:], col("ada_b0", 0, 48), mod2[:, 0, :])
            dve.drain()
            norm_gain(2, mod1[:, 4 * KC:5 * KC], "g_ffn")
            norm_gain(3, mod2[:, 0, KC:2 * KC], "nmix0")
            norm_gain(4, mod2[:, 0, 4 * KC:5 * KC], "nmlp0")

            def maxima(n):
                dve.wait_ge(score_mm, n + 1)
                first = 3 * (n % 2)
                nc.vector.tensor_reduce(rowmax[:, n % 2, :],
                                        PS[:, first:first + 3, :].rearrange("p a b -> p (a b)").rearrange("p (m k) -> p m k", m=2),
                                        AX, ALU.max)
                dve.drain()
                ts(negmax[:, n % 2, :], rowmax[:, n % 2, :], -DH ** -0.5, None, ALU.mult).then_inc(negmax_ready, 1)

            def attention_weights(n):
                b = n % 2
                dve.wait_ge(exp_done, 2 * n + 2)
                nc.vector.reciprocal(rsum[:, b, :], rowsum[:, b, :])
                dve.drain()
                ts(attn_t, probs[:, b, 1, :], rsum[:, b, 1:2], neglam, ALU.mult, ALU.mult)
                dve.drain()
                if n >= 2:
                    dve.wait_ge(at_mm, 2 * (n - 1))
                stt(attn_a[:, b, :], probs[:, b, 0, :], rsum[:, b, 0:1], attn_t, ALU.mult, ALU.add).then_inc(a_ready, 1)

            def head_out(hd):
                dve.wait_ge(pv_mm, hd + 1)
                nc.vector.tensor_copy(oT, PS[:, 7, :]).then_inc(o_ready, 1)

            def head_norm(hd):
                dve.wait_ge(oms_done, hd + 1)
                ts(var, PS[:, 7, :], 1.0 / P, 1e-6, ALU.mult, ALU.add).then_inc(ovar_ready, 1)
                dve.wait_ge(ostd_ready, hd + 1)
                nc.vector.reciprocal(rstd, rstd)
                dve.drain()
                stt(h[:, hd, :], oT, gsub, rstd, ALU.mult, ALU.mult).then_inc(head_done, 1)

            maxima(0)
            maxima(1)
            for n in range(HEADS * TC):
                hd, qc = n // TC, n % TC
                attention_weights(n)
                if n + 2 < HEADS * TC:
                    maxima(n + 2)
                if hd and qc == 2:
                    head_out(hd - 1)
                if hd and qc == 3:
                    head_norm(hd - 1)
            head_out(HEADS - 1)
            head_norm(HEADS - 1)

            for c in range(KC):
                dve.wait_ge(proj_mm, c + 1)
                stt(x[:, c, :], PS[:, c, :], mod1[:, 2 * KC + c:2 * KC + c + 1], x[:, c, :], ALU.mult, ALU.add).then_inc(x1_ready, 1)

            norm_var(2, T, 1e-6)
            norm_divide(2, x, h, T)
            dve.wait_ge(in_late, 32)
            dve.wait_ge(route_mm, 1)

            def per_token(v, n):
                return v.unsqueeze(2).broadcast_to([P, TC, n])

            def first_max(v, n, peak, eq, ids, least, onehot):
                nc.vector.tensor_reduce(peak, v, AX, ALU.max)
                dve.drain()
                tt(eq, v, per_token(peak, n), ALU.is_equal)
                dve.drain()
                stt(ids, eq, -float(P), iota[:, 0:n].unsqueeze(1).broadcast_to([P, TC, n]), ALU.mult, ALU.add)
                dve.drain()
                nc.vector.tensor_reduce(least, ids, AX, ALU.min)
                dve.drain()
                tt(onehot, ids, per_token(least, n), ALU.is_equal)
                dve.drain()

            tt(logits, PS[:, 1, 0:TC * 36].rearrange("p (t n) -> p t n", n=36),
               b_router.unsqueeze(1).broadcast_to([P, TC, 36]), ALU.add)
            dve.drain()
            first_max(logits[:, :, 0:4], 4, g_max, g_eq, g_id, g_idx, g_hot)
            tt(g_exp, logits[:, :, 0:4], per_token(g_max, 4), ALU.subtract).then_inc(exp_in, 1)
            tt(e_all, logits[:, :, 4:36].rearrange("p t (g e) -> p t g e", e=EPG),
               g_hot.unsqueeze(3).broadcast_to([P, TC, 4, EPG]), ALU.mult)
            dve.drain()
            nc.vector.tensor_reduce(e_in, e_all.rearrange("p t g e -> p t e g"), AX, ALU.add)
            dve.drain()
            first_max(e_in, EPG, top1, e_eq, e_id, e_idx, e_hot[:, 0, :, :])
            stt(e_left, e_hot[:, 0, :, :], -1e30, e_in, ALU.mult, ALU.add)
            dve.drain()
            first_max(e_left, EPG, top2, e_eq, e_id, e_idx, e_hot[:, 1, :, :])
            tt(e2, top2, top1, ALU.subtract).then_inc(exp_in, 1)
            for k in range(2):
                tt(hot[:, k, :, :].rearrange("p t (g e) -> p t g e", e=EPG),
                   g_hot.unsqueeze(3).broadcast_to([P, TC, 4, EPG]),
                   e_hot[:, k, :, :].unsqueeze(2).broadcast_to([P, TC, 4, EPG]), ALU.mult)
            dve.drain()
            tt(chosen, hot[:, 0, :, :], hot[:, 1, :, :], ALU.add).then_inc(chosen_ready, 1)
            nc.vector.memset(yb[:, 1, :], 0.0)
            dve.wait_ge(exp_out, 2)
            nc.vector.tensor_reduce(g_sum, g_exp, AX, ALU.add)
            dve.wait_ge(exp_out, 3)
            ts(e_sum, e2, 1.0, None, ALU.add)
            dve.drain()
            tt(g_sum, g_sum, e_sum, ALU.mult)
            dve.drain()
            nc.vector.reciprocal(gates[:, 0, :], g_sum)
            dve.drain()
            tt(gates[:, 1, :], gates[:, 0, :], e2, ALU.mult)
            nc.vector.memset(ones_e, 1.0)
            dve.wait_ge(route_mm, 2)
            count = PS[:, 6, TC * EXPERTS:(TC + 1) * EXPERTS]
            ts(n_blk, count, 0.0, None, ALU.is_gt)
            for n in range(1, TC):
                dve.drain()
                stt(n_blk, count, float(n * P), n_blk, ALU.is_gt, ALU.add)
            dve.drain()
            nc.vector.tensor_tensor_scan(blk_end, ones_e, n_blk, 0.0, ALU.mult, ALU.add)
            dve.drain()
            tt(blk_start, blk_end, n_blk, ALU.subtract)
            dve.drain()
            stt(place, blk_start.unsqueeze(1).broadcast_to([P, TC, EXPERTS]), float(P),
                PS[:, 6, 0:TC * EXPERTS].rearrange("p (t e) -> p t e", e=EXPERTS), ALU.mult, ALU.add)
            dve.drain()
            for k in range(2):
                tt(hot[:, k, :, :], hot[:, k, :, :], place, ALU.mult)
            dve.drain()
            nc.vector.tensor_reduce(dest, hot, AX, ALU.add)
            dve.drain()
            nc.vector.tensor_copy(slot_part[:, 0, :, :], dest)
            ts(slot_of[:], dest, float(P), None, ALU.add)
            dve.drain()
            ts(slot_part[:, 1, :, :], slot_part[:, 0, :, :], 7, None, ALU.arith_shift_right)
            dve.drain()
            ts(slot_part[:, 0, :, :], slot_part[:, 0, :, :], P - 1, None, ALU.bitwise_and)
            dve.drain()
            stt(slot_at[:], slot_part[:, 0, :, :], float(BLOCKS), slot_part[:, 1, :, :], ALU.mult, ALU.add) \
                .then_inc(route_ready, 1)
            tt(blk_cmp, blk_end.unsqueeze(1).broadcast_to([P, BLOCKS, EXPERTS]),
               iota[:, 0:BLOCKS].unsqueeze(2).broadcast_to([P, BLOCKS, EXPERTS]), ALU.is_le)
            ts(pair_cmp, iota[:, 0:BLOCKS // 2], 2.0, blk_end[:, EXPERTS - 1:EXPERTS], ALU.mult, ALU.is_lt)
            dve.drain()
            nc.vector.tensor_reduce(blk_exp, blk_cmp, AX, ALU.add)
            nc.vector.tensor_reduce(n_pairs, pair_cmp, AX, ALU.add)
            dve.drain()
            ts(route_i[:, 0:BLOCKS], blk_exp, float(EXPERTS - 1), None, ALU.min)
            nc.vector.tensor_copy(route_i[:, BLOCKS:BLOCKS + 1], n_pairs)
            dve.drain()
            dve.sem_inc(route_ready, 1)

            pairs = dve.value_load(route_i[0:1, BLOCKS:BLOCKS + 1], min_val=1, max_val=BLOCKS // 2)
            for freed in (hid_ready, y_ready):
                dve.sem_inc(freed, 1)

            def hidden(i, s):
                dve.wait_ge(silu_done, i * 2 + (s + 1))
                dve.wait_ge(up_mm, i * 2 + (s + 3))
                tt(hid[:, s, :], silu_b[:, s, :], PS[:, 3, :], ALU.mult).then_inc(hid_ready, 1)

            def result(i, s):
                dve.wait_ge(down_mm, i * 2 + (s + 3))
                dve.wait_ge(y_stored[s], i * 16 + 16)
                nc.vector.tensor_copy(yb[:, s, :].rearrange("p (a b) -> p a b", a=2), PS[:, 5:7, :]).then_inc(y_ready, 1)

            with dve.Fori(0, pairs) as i:
                hidden(i, 0)
                result(i, 0)
                hidden(i, 1)
                result(i, 1)
            dve.wait_ge(moe_done, 1)
            dve.wait_ge(y_loaded, 32 * TC)

            def gated_sum(t):
                if t >= 2:
                    dve.wait_ge(yT_mm, t - 1)
                ts(y_of[:, 0, t, :], y_of[:, 0, t, :], gates[:, 0, t:t + 1], None, ALU.mult)
                dve.drain()
                stt(ysum[:, t % 2, :], y_of[:, 1, t, :], gates[:, 1, t:t + 1], y_of[:, 0, t, :], ALU.mult, ALU.add) \
                    .then_inc(ysum_ready, 1)

            gated_sum(0)
            for t in range(TC):
                if t + 1 < TC:
                    gated_sum(t + 1)
                dve.wait_ge(yT_mm, t + 1)
                for c in range(KC):
                    xc = x[:, c, t * P:(t + 1) * P]
                    last = stt(xc, PS[:, 2 * (t % 2) + c // 4, (c % 4) * P:(c % 4 + 1) * P],
                               mod1[:, 5 * KC + c:5 * KC + c + 1], xc, ALU.mult, ALU.add)
                    if t == TC - 1:
                        last.then_inc(x2_ready, 1)
                if t < TC - 1:
                    last.then_inc(yT_used, 1)
            dve.drain()
            norm_var(3, T, 1e-6)
            norm_scale(3, col("g_final", 0, KC))

            norm_var(4, T, 1e-5)
            norm_divide(4, x, h, T)
            re, im = col("lam_re", 0, S5_TILES), col("lam_im", 0, S5_TILES)

            def step(op, *args):
                op(*args)
                dve.drain()

            dve.wait_ge(exp_out, 4)
            step(tt, s5_a, re, s5_dt, ALU.mult)
            step(tt, s5_th, im, s5_dt, ALU.mult)
            step(ts, s5_th, s5_th, 0.5, None, ALU.mult)
            step(ts, s5_k, s5_th, 1.0 / (2 * np.pi), ROUND, ALU.mult, ALU.add)
            step(ts, s5_k, s5_k, -ROUND, None, ALU.add)
            step(stt, s5_r, s5_k, -TWO_PI_HI, s5_th, ALU.mult, ALU.add)
            step(stt, s5_r, s5_k, -TWO_PI_LO, s5_r, ALU.mult, ALU.add)
            step(ts, s5_r, s5_r, PI_BELOW, -PI_BELOW, ALU.min, ALU.max)
            step(ts, s5_t, s5_r, -1.0, None, ALU.mult)
            step(tt, s5_ab, s5_r, s5_t, ALU.max)
            ts(s5_ab, s5_ab, -1.0, np.pi / 2, ALU.mult, ALU.add).then_inc(exp_in, 1)
            dve.wait_ge(exp_out, 5)
            step(tt, s5_s2, half_sin, half_sin, ALU.mult)
            step(ts, cos1, s5_s2, -2.0, 1.0, ALU.mult, ALU.add)
            step(stt, sin1, half_sin, 2.0, half_cos, ALU.mult, ALU.mult)
            step(stt, num_re, radius, -1.0, cos1, ALU.add, ALU.mult)
            step(stt, num_re, s5_s2, -2.0, num_re, ALU.mult, ALU.add)
            step(tt, num_im, radius, sin1, ALU.mult)
            step(tt, s5_den, re, re, ALU.mult)
            step(tt, s5_t, im, im, ALU.mult)
            step(tt, s5_den, s5_den, s5_t, ALU.add)
            step(nc.vector.reciprocal, s5_den, s5_den)
            step(tt, f_re, num_re, re, ALU.mult)
            step(tt, s5_t, num_im, im, ALU.mult)
            step(tt, f_re, f_re, s5_t, ALU.add)
            step(tt, f_re, f_re, s5_den, ALU.mult)
            step(tt, f_im, num_im, re, ALU.mult)
            step(tt, s5_t, num_re, im, ALU.mult)
            step(tt, f_im, f_im, s5_t, ALU.subtract)
            step(tt, f_im, f_im, s5_den, ALU.mult)
            dve.wait_ge(in_late, 64)
            ctmp = [v[:, 0:8, :].rearrange("p a n -> p (a n)").rearrange("p (t n) -> p t n", n=HP) for v in turn_t]
            for n, (part, f) in enumerate(((0, f_re), (1, f_im), (0, f_im), (1, f_re))):
                tt(ctmp[n], s5_c[:, :, part, :], f.unsqueeze(2).broadcast_to([P, S5_TILES, HP]), ALU.mult)
            dve.drain()
            tt(s5_cf[:, :, 0, :], ctmp[0], ctmp[1], ALU.subtract)
            step(tt, s5_cf[:, :, 1, :], ctmp[2], ctmp[3], ALU.add)
            ts(s5_cf[:, :, 1, :], s5_cf[:, :, 1, :], -1.0, None, ALU.mult).then_inc(c_ready, 1)
            nc.vector.tensor_copy(turn[:, 0, :, 0:1], cos1.unsqueeze(2))
            nc.vector.tensor_copy(turn[:, 1, :, 0:1], sin1.unsqueeze(2))
            n = 1
            while n < S5_Q:
                dve.drain()
                by = [turn[:, r, :, n - 1:n].broadcast_to([P, S5_TILES, n]) for r in range(2)]
                for k, (part, f) in enumerate(((0, 0), (1, 1), (0, 1), (1, 0))):
                    tt(turn_t[k][:, :, 0:n], turn[:, part, :, 0:n], by[f], ALU.mult)
                dve.drain()
                tt(turn[:, 0, :, n:2 * n], turn_t[0][:, :, 0:n], turn_t[1][:, :, 0:n], ALU.subtract)
                tt(turn[:, 1, :, n:2 * n], turn_t[2][:, :, 0:n], turn_t[3][:, :, 0:n], ALU.add)
                n *= 2
            dve.drain()
            dve.sem_inc(bu_used, 4)
            dve.sem_inc(s5_used, 1)
            dve.sem_inc(state_ready, 1)
            for part in range(2):
                tt(carry_by[:, part, :], turn[:, part, :, S5_Q - 1], radius, ALU.mult)
            dve.wait_ge(u_evac, KC)

            def add_feedthrough(q):
                dve.wait_ge(s5_mm, q * 4 + 6)
                stt(h[:, bass.ds(q, 1), :], uT[:, bass.ds(q, 1), :], cols[:, bass.ds(q + COLS["s5_d"][0], 1)],
                    PS[:, 6:7, :], ALU.mult, ALU.add).then_inc(s5_used, 1)

            def s5_quad(q, first_quad):
                def turns(a, r):
                    return turn[:, r, bass.ds(q * 4 + a, 1), :].broadcast_to([P, S5_NC, S5_Q])

                for a in range(4):
                    bu = [chunked(PS[:, 2 * (a % 3) + r, :]) for r in range(2)]
                    t = [chunked(rot[:, 1 - a % 2, n, :]) for n in range(4)]
                    if a < 2:
                        dve.wait_ge(g_added, q * 3 + (1 + a))
                    else:
                        dve.wait_ge(g_added, q * 3 + (a + 1))
                    if a == 1:
                        dve.wait_ge(s5_mm, q * 4 + 1)
                    dve.wait_ge(bu_mm, q * 4 + (4 + a + 1))
                    tt(t[0], bu[0], turns(a, 0), ALU.mult)
                    tt(t[1], bu[1], turns(a, 1), ALU.mult)
                    tt(t[2], bu[1], turns(a, 0), ALU.mult)
                    tt(t[3], bu[0], turns(a, 1), ALU.mult).then_inc(bu_used, 1)
                dve.drain()
                tt(scan_g[:, :, 6, :], t[0], t[1], ALU.add)
                tt(scan_g[:, :, 7, :], t[2], t[3], ALU.subtract)
                if not first_quad:
                    add_feedthrough(q - 1)
                dve.drain()
                dve.wait_ge(g_added, q * 3 + 5)
                dve.wait_ge(decay_set, q + 1)
                for c in range(S5_NC):
                    g = scan_g[:, c, :, :].rearrange("p n t -> p (n t)")
                    nc.vector.tensor_tensor_scan(g, decay_now.rearrange("p a r t -> p (a r t)"), g, 0.0, ALU.mult, ALU.add)
                    dve.drain()
                    if c < S5_NC - 1:
                        ends = [scan_g[:, c, r:8:2, S5_Q - 1] for r in range(2)]
                        by = [carry_by[:, r, bass.ds(q * 4, 4)] for r in range(2)]
                        for k, (part, f) in enumerate(((0, 0), (1, 1), (0, 1), (1, 0))):
                            tt(carry_t[:, k, :], ends[part], by[f], ALU.mult)
                        dve.drain()
                        tt(carry[:, :, 0], carry_t[:, 0, :], carry_t[:, 1, :], ALU.subtract)
                        tt(carry[:, :, 1], carry_t[:, 2, :], carry_t[:, 3, :], ALU.add)
                        dve.drain()
                        first = scan_g[:, c + 1, :, 0]
                        tt(first, first, carry.rearrange("p a r -> p (a r)"), ALU.add)
                        dve.drain()
                for a in range(4):
                    g = [scan_g[:, :, 2 * a + r, :] for r in range(2)]
                    t = [chunked(turned_back(a)[:, n, :]) for n in range(4)]
                    if a in (0, 3):
                        dve.wait_ge(s5_mm, q * 4 + (2 + a // 3))
                    tt(t[0], g[0], turns(a, 0), ALU.mult)
                    stt(t[1], g[1], -1.0, turns(a, 1), ALU.mult, ALU.mult)
                    tt(t[2], g[0], turns(a, 1), ALU.mult)
                    tt(t[3], g[1], turns(a, 0), ALU.mult).then_inc(state_ready, 1)

            s5_quad(0, True)
            with dve.Fori(1, KC) as q:
                s5_quad(q, False)
            add_feedthrough(KC - 1)
            split_first("glu", glu_lo, h, gelu_done, 0)
            split_weights("glu", 2, 1)
            for i in range(2):
                split_weights("glu", 4 + 2 * i, i)
                for n in range(4 * i, 4 * i + 4):
                    dve.wait_ge(gate_sig, n + 1)
                    stt(glu_t[:, n % 2, :], PS[:, n % 4, :], col("b_glu", n), glu_gate[:, n % 2, :], ALU.add, ALU.mult)
                    dve.drain()
                    stt(x[:, n, :], glu_t[:, n % 2, :], mod2[:, 0, 2 * KC + n:2 * KC + n + 1], x[:, n, :], ALU.mult, ALU.add) \
                        .then_inc(glu_used, 1)

            def mlp(layer, k_norm):
                name = f"mlp{layer}"
                norm_var(k_norm, T, 1e-5)
                if layer == 0:
                    dve.sem_inc(mlp_added, 8)
                split_normed(name, mlp_h_lo, KC * (k_norm - 1 + layer), k_norm, gain[:, 4 + 2 * layer, :],
                             mod2[:, layer, 3 * KC:4 * KC])

                def quarter(i, last):
                    for t in range(4):
                        if t < 3 or not last:
                            split_weights(name, i * 8 + 2 * (t + 1), (t + 1) % 2)
                        if layer == 0:
                            dve.wait_ge(ada_loaded[t % 2], i * 32 + 16 * ((ADA_LATE + ADA_TILES) // 2 + t // 2 + 1))
                            for n in range(3):
                                w = ada_buf1[t % 2][:, n, :]
                                last_mod = stt(w, w, 1.0, cond2[:], ALU.mult, ALU.mult,
                                               accum_out=mod2[:, 1, bass.ds(i * 12 + (3 * t + n), 1)])
                            last_mod.then_inc(ada_used, 1)
                        if t < 2:
                            for n in range(4 * t, 4 * t + 4):
                                dve.wait_ge(mlp1_mm, i * 8 + (32 * layer + n + 1))
                                ts(mlp_lo[:, n, :], PS[:, n, :], 0.0, None, ALU.max).then_inc(relu_done, 1)
                            for n in range(4 * t, 4 * t + 4):
                                dve.wait_ge(sqr_done, i * 8 + (32 * layer + n + 1))
                                tt(f32r(mlp_lo[:, n, :]), mlp_lo[:, n, :], f32r(mlp_hi[:, n, :]), ALU.subtract).then_inc(mlp_split, 1)
                        else:
                            for n in range(4 * t - 8, 4 * t - 4):
                                dve.wait_ge(mlp2_mm, i * 8 + (32 * layer + n + 1))
                                stt(x[:, n, :], PS[:, n, :], mod2[:, layer, 5 * KC + n:5 * KC + n + 1], x[:, n, :], ALU.mult,
                                    ALU.add).then_inc(mlp_added, 1)

                with dve.Fori(0, 3) as i:
                    quarter(i, False)
                quarter(3, True)
                if layer == 0:
                    dve.drain()
                    tt(mod2[:, 1, :], mod2[:, 1, :], col("ada_b1", 0, 48), ALU.add)
                    dve.drain()
                    norm_gain(5, mod2[:, 1, KC:2 * KC], "nmix1")
                    norm_gain(6, mod2[:, 1, 4 * KC:5 * KC], "nmlp1")
                    dve.drain()

            mlp(0, 5)

            norm_var(6, T, 1e-5)
            dve.sem_inc(conv_done, 8)
            split_normed("xbc", xbc_h_lo, 5 * KC, 6, gain[:, 5, :], mod2[:, 1, 0:KC])

            def convolution(i, last_pair):
                def tap(n, k):
                    return cols[:, bass.ds(i * 8 + (COLS["conv_w"][0] + M2_CC * n + k), 1)]

                for s in range(2):
                    if s == 0 or not last_pair:
                        split_weights("xbc", i * 4 + 2 * (s + 1), 1 - s)
                    for k in range(4 * s, 4 * s + 4):
                        dve.wait_ge(xbc_mm, i * 8 + (k + 1))
                        ts(xs[:, bass.ds(i * 8 + k, 1), :], PS[:, k:k + 1, :], tap(3, k), None, ALU.mult)
                        for back in range(1, 4):
                            dve.drain()
                            late = xs[:, bass.ds(i * 8 + k, 1), back:T]
                            last = stt(late, PS[:, k:k + 1, 0:T - back], tap(3 - back, k), late, ALU.mult, ALU.add)
                        last.then_inc(conv_done, 1)

            with dve.Fori(0, 2) as i:
                convolution(i, False)
            convolution(2, True)
            for c in range(KC):
                last = tt(h[:, c, :], f32r(h[:, c, :]), f32r(xbc_h_lo[:, c, :]), ALU.add)
            last.then_inc(step_dve, 1)
            dve.wait_ge(dt_mm, 1)
            ts(dt_raw, PS[0:M2_HEADS, 0, :], col("dt_bias")[0:M2_HEADS, :], None, ALU.add).then_inc(step_dve, 1)
            nc.vector.memset(state, 0.0)
            nc.vector.memset(z_silu[0:M2_HEADS, 0, :], 1.0)
            dve.wait_ge(step_act, 1)
            step(stt, dt_t, dt_raw, 0.0, dt_abs, ALU.max, ALU.add)
            step(ts, a_dt, dt_t, a_pos, -1.0, ALU.mult, ALU.mult)
            for c in range(M2_NC):
                at = slice(c * M2_Q, (c + 1) * M2_Q)
                nc.vector.tensor_tensor_scan(a_cs[:, at], z_silu[0:M2_HEADS, 0, at], a_dt[:, at], 0.0, ALU.mult, ALU.add)
            dve.drain()
            for c in range(M2_NC):
                last = ts(last_diag[:, c, :], eye[0:M2_HEADS, 0:M2_HEADS], a_cs[:, (c + 1) * M2_Q - 1:(c + 1) * M2_Q], None,
                          ALU.mult)
            last.then_inc(step_dve, 1)
            dve.wait_ge(dt_mm, 2)
            by_token = PS[:, 1, 0:2 * M2_NC * M2_HEADS].rearrange("p (n c h) -> p n c h", c=M2_NC, h=M2_HEADS)
            nc.vector.tensor_copy(dt_tok, by_token[:, 0, :, :])
            step(ts, cs_neg, by_token[:, 1, :, :], -1.0, None, ALU.mult)
            nc.vector.tensor_copy(eye16, eye)
            ts(mask16, causal, -1.0, 1e30, ALU.add, ALU.mult)
            tt(dec_tok, PS[:, 2, 0:M2_NC * M2_HEADS].rearrange("p (c h) -> p c h", h=M2_HEADS), cs_neg, ALU.add) \
                .then_inc(step_dve, 1)
            dve.wait_ge(step_act, 2)
            dve.sem_inc(m_ready, 2)
            dve.sem_inc(y_tok_evac, 1)
            dve.sem_inc(y_added, 1)
            dve.sem_inc(state_new, 1)
            with dve.Fori(0, M2_NC) as c:
                def heads(v, first, count):
                    return v[:, bass.ds(c, 1), first:first + count].rearrange("p c h -> p (c h)")

                for b in range(4):
                    dve.wait_ge(xs_tok_mm, c * 4 + (b + 1))
                    tt(xdt[:, b * 512:(b + 1) * 512].rearrange("p (h n) -> p h n", n=64),
                       PS[:, b, :].rearrange("p (h n) -> p h n", n=64),
                       heads(dt_tok, 8 * b, 8).unsqueeze(2).broadcast_to([P, 8, 64]), ALU.mult).then_inc(xdt_ready, 1)
                for g in range(M2_G):
                    dve.wait_ge(off_mm, c * 4 + (g + 1))
                    tt(y_off[:, g * 512:(g + 1) * 512].rearrange("p (h n) -> p h n", n=64),
                       PS[:, g, :].rearrange("p (h n) -> p h n", n=64),
                       heads(exp_cs_tok, 8 * g, 8).unsqueeze(2).broadcast_to([P, 8, 64]), ALU.mult).then_inc(off_used, 1)
                dve.wait_ge(cb_mm, c + 1)

                def weights(q):
                    dve.wait_ge(decay_ready, c * 8 + (q + 1))
                    dve.wait_ge(y7_mm, c * 8 + (q + 1))
                    g = q // 2
                    tt(m_now[:, q % 2, :, :], decay[:, q % 2, :, :],
                       PS[:, 5, g * P:(g + 1) * P].unsqueeze(1).broadcast_to([P, 4, P]), ALU.mult).then_inc(m_ready, 1)

                def sum_y(q):
                    dve.wait_ge(y7_mm, c * 8 + (q + 3))
                    dve.wait_ge(y_turned, c * 8 + (q + 1))
                    tt(y_tok[:, q % 2, :], PS[:, 7, 0:2 * P], y_off[:, q * 256:(q + 1) * 256], ALU.add).then_inc(y_tok_evac, 1)

                def add_y(q):
                    dve.wait_ge(y_turned, c * 8 + (q + 3))
                    for j in range(2):
                        n = 2 * q + j
                        xc = xs[:, n, bass.ds(c * M2_Q, M2_Q)]
                        last = stt(xc, xc, col("m2_d", n), PS[:, 4, j * P:(j + 1) * P], ALU.mult, ALU.add)
                    last.then_inc(y_added, 1)

                weights(0)
                for q in range(8):
                    if q < 7:
                        weights(q + 1)
                    sum_y(q)
                    if q:
                        add_y(q - 1)
                add_y(7)
                dve.wait_ge(st_mm, c + 1)
                dve.wait_ge(state_decayed, c + 1)
                for g in range(M2_G):
                    part = state[:, g * 512:(g + 1) * 512]
                    last = tt(part, part, PS[:, g, :], ALU.add)
                last.then_inc(state_new, 1)
            dve.drain()
            dve.sem_inc(z_used, 2)
            split_first("z", h, z_h_hi, h_ready, 6 * KC)

            def group_var(g):
                dve.wait_ge(oms_done, HEADS + g + 1)
                ts(var, PS[:, 4 * (g % 2), :], 1.0 / 512, 1e-5, ALU.mult, ALU.add).then_inc(ovar_ready, 1)

            def group_inverse(g):
                dve.wait_ge(ostd_ready, HEADS + g + 1)
                nc.vector.reciprocal(m2_rstd[:, g, :], rstd)
                dve.drain()

            def group_out(g):
                for n in range(4 * g, 4 * g + 4):
                    stt(y_lo[:, n, :], xs[:, n, :], col("m2_norm", n), m2_rstd[:, g, :], ALU.mult, ALU.mult).then_inc(yn_ready, 1)
                for n in range(4 * g, 4 * g + 4):
                    dve.wait_ge(y_hi_ready, n + 1)
                    tt(f32r(y_lo[:, n, :]), y_lo[:, n, :], f32r(xs[:, n, :]), ALU.subtract).then_inc(lo_ready, 1)

            for t in range(4):
                if t < 3:
                    split_weights("z", 2 * (t + 1), (t + 1) % 2)
                else:
                    split_weights("m2_out", 0, 0)
                for n in range(4 * t, 4 * t + 4):
                    dve.wait_ge(z_ready, 8 + n + 1)
                    tt(xs[:, n, :], xs[:, n, :], z_silu[:, n % 2, :], ALU.mult).then_inc(z_used, 1)
                if t:
                    group_var(t - 1)
                if t in (1, 2):
                    group_inverse(t - 1)
            group_out(0)
            group_inverse(2)
            group_out(1)
            split_weights("m2_out", 2, 1)
            group_var(3)
            group_inverse(3)
            group_out(2)
            group_out(3)
            for s in range(2):
                split_weights("m2_out", 4 + 2 * s, s)
            for n in range(KC):
                dve.wait_ge(proj_mm, 2 * KC + n + 1)
                stt(x[:, n, :], PS[:, n, :], mod2[:, 1, 2 * KC + n:2 * KC + n + 1], x[:, n, :], ALU.mult, ALU.add) \
                    .then_inc(x5_ready, 1)
            mlp(1, 7)
            norm_var(8, T, 1e-5)
            norm_scale(8, col("fin", 0, KC))


def _constants():
    f = np.float32
    p = np.arange(P)
    rot = np.zeros((P, P), f)
    for m in range(P):
        rot[m + 16 if m % 32 < 16 else m - 16, m] = -1.0 if m % 32 < 16 else 1.0
    mats = np.stack([np.eye(P, dtype=f), (p[:, None] < p[None, :]).astype(f), (p[:, None] <= p[None, :]).astype(f), rot], 1)
    t = np.arange(T)
    pos = np.stack([t // 64, t % 64], -1).astype(f)
    axis = DH // 2
    freq = (f(10000.0) ** (-np.arange(0, axis, 2, dtype=f) / f(axis))).astype(f)
    ang = (pos[:, :, None] * freq).astype(f)
    ang = np.concatenate([ang, ang], -1).reshape(T, DH)
    ang = np.concatenate([ang, ang], -1).T
    tt = 2 * np.pi * ((t[:, None] * t[None, :]) % T) / T
    cc = 2 * np.pi * ((p[:, None] * p[None, :]) % P) / P
    ortho = 1.0 / np.sqrt(T * P)

    def token_rows(a):
        return np.ascontiguousarray(a.astype(f).reshape(TC, P, T).transpose(1, 0, 2))

    return {
        "mats": mats, "rope_c": np.cos(ang).astype(f), "rope_s": np.sin(ang).astype(f),
        "dft_c": token_rows(np.cos(tt) * ortho), "dft_s": token_rows(-np.sin(tt) * ortho),
        "dft_ch": np.concatenate([np.cos(cc), np.sin(cc)], 1).astype(f),
        "iota": np.tile(np.arange(64, dtype=f), (P, 1)),
        "tokid": (p[:, None] + P * np.arange(TC)[None, :]).astype(np.uint32),
    }


def _layout(a):
    def chunks(v):
        return np.asarray(v).reshape(-1, P).T

    def features(m):
        m = np.asarray(m)
        return m.T.reshape(-1, P, m.shape[0]).transpose(1, 0, 2)

    def rows(w):
        return np.asarray(w).reshape(-1, P, w.shape[-1]).transpose(1, 0, 2)

    def padded(v):
        return np.concatenate([np.asarray(v), np.zeros(P - len(v), np.float32)])[:, None]

    def states(v):
        return np.asarray(v).reshape(S5_TILES, P).T

    packed = {
        "b_ada": chunks(a["b_ada"][0]), "ada_b0": chunks(a["ada_b_2"][0]), "ada_b1": chunks(a["ada_b_2"][1]),
        "g_mix": chunks(a["g_mix_norm"][0]), "g_ffn": chunks(a["g_ffn_norm"][0]), "g_final": chunks(a["g_final"]),
        "g_subln": chunks(a["g_subln"][0]), "nmix0": chunks(a["norm_mix_g_2"][0]), "nmix1": chunks(a["norm_mix_g_2"][1]),
        "nmlp0": chunks(a["norm_mlp_g_2"][0]), "nmlp1": chunks(a["norm_mlp_g_2"][1]), "s5_d": chunks(a["s5_d_2"][0]),
        "b_glu": chunks(a["s5_b_glu_2"][0]),
        "conv_w": np.concatenate([chunks(a["m2_conv_w_2"][0][k]) for k in range(4)], 1),
        "conv_b": chunks(a["m2_conv_b_2"][0]), "m2_d": chunks(np.repeat(np.asarray(a["m2_d_2"][0]), 64)),
        "m2_norm": chunks(a["m2_norm_g_2"][0]), "fin": chunks(a["final_norm_g_2"]),
        "dt_bias": padded(a["m2_dt_bias_2"][0]), "a_log": padded(a["m2_a_log_2"][0]),
        "lam_re": states(a["s5_lambda_re_2"][0]), "lam_im": states(a["s5_lambda_im_2"][0]),
        "log_dt": states(np.repeat(np.asarray(a["s5_log_dt_2"][0])[:, None], 64, 1)),
    }
    s5_b = np.zeros((4, 2, HP, 8, 2, 2, 64), np.float32)
    s5_c = np.empty((2, 64, S5_TILES, 2, HP), np.float32)
    for r, (bname, cname) in enumerate((("s5_b_re_2", "s5_c_re_2"), ("s5_b_im_2", "s5_c_im_2"))):
        b = np.asarray(a[bname][0]).reshape(8, 4, 2, 64, HP)
        for g in range(2):
            s5_b[:, g, :, :, r, g, :] = b[:, :, g].transpose(1, 3, 0, 2)
        s5_c[:, :, :, r, :] = np.asarray(a[cname][0]).reshape(S5_TILES, 2, HP, 64).transpose(1, 3, 0, 2)
    m2_in = np.asarray(a["m2_w_in_2"][0])
    lams = np.stack([a[n][0] for n in ("lambda_q1", "lambda_k1", "lambda_q2", "lambda_k2")])
    return {
        "xT": features(a["x"][0]), "ctxT": features(a["ctx"][0]),
        "c_rows": np.stack([a["c"][0], a["c_2"][0]]),
        "c_cols": np.stack([chunks(a["c"][0]), chunks(a["c_ctx"])], 2),
        "cols": np.concatenate([packed[n] for n in COLS], 1),
        "lam4": np.tile(lams[None], (P, 1, 1)),
        "w_ada": np.asarray(a["w_ada"][0])[:, :MOD_EARLY * P], "w_adaT": np.asarray(a["w_ada"][0])[:, MOD_EARLY * P:].T,
        "ada_w_2T": np.asarray(a["ada_w_2"]).transpose(0, 2, 1),
        "w_in": a["w_in"][0], "w_out": a["w_out"][0],
        "wfour": np.asarray(a["w_fourier"][0]).transpose(1, 0, 2),
        "w_router": rows(np.concatenate([a["w_router_group"][0], a["w_router_expert"][0]], 1)),
        "b_router": np.tile(np.concatenate([a["b_router_group"][0], a["b_router_expert"][0]])[None], (P, 1)),
        "w_gate": a["w_gate"][0], "w_up": a["w_up"][0], "w_down": a["w_down"][0],
        "s5_w_in": a["s5_w_in_2"][0], "s5_b": s5_b.reshape(P, 8, 2, P), "s5_c": s5_c.reshape(P, S5_TILES, 2, HP),
        "w_glu": a["s5_w_glu_2"][0], "mlp_w1": a["mlp_w1_2"], "mlp_w2": a["mlp_w2_2"],
        "m2_w_in": m2_in, "m2_w_dt": rows(m2_in[:, M2_IN + M2_XBC:]), "m2_w_out": a["m2_w_out_2"][0],
    }


def kernel(**inputs):
    import concourse.bacc as bacc
    from concourse.bass_utils import run_bass_kernel_spmd

    nc = bacc.Bacc("TRN2", target_bir_lowering=False, num_devices=1)
    arrays = {name: np.ascontiguousarray(v) for name, v in {**_layout(inputs), **_constants()}.items()}
    handles = {name: nc.dram_tensor(f"in_{name}", v.shape, mybir.dt.from_np(v.dtype), kind="ExternalInput").ap()
               for name, v in arrays.items()}
    out = nc.dram_tensor("outT", [P, KC, T], F32, kind="ExternalOutput").ap()
    build(nc, handles, out)
    r = run_bass_kernel_spmd(nc, [{f"in_{name}": v for name, v in arrays.items()}], core_ids=[0])
    got = np.asarray(r.results[0]["outT"])
    return got.transpose(2, 1, 0).reshape(1, T, D)
```
